# Optimizing a Trainium2 kernel written in Bass

```python
import math
import jax, jax.numpy as jnp
from jax import lax
import numpy as np

D_MODEL = 1024
BATCH = 1
SEQ = 256
DEPTH = 1

D_MIX = 2 * D_MODEL
ATTN_WIDTH = D_MIX // 2
SB_HEAD_DIM = 64
SB_HEADS = ATTN_WIDTH // SB_HEAD_DIM
SB_BLOCK = 128
SSD_WIDTH = D_MIX - ATTN_WIDTH
SSD_HEAD_DIM = 64
SSD_HEADS = SSD_WIDTH // SSD_HEAD_DIM
SSD_GROUPS = 2
SSD_STATE = 128
SSD_CONV_K = 4
SSD_CHUNK = 128
SSD_CONV_CH = SSD_WIDTH + 2 * SSD_GROUPS * SSD_STATE
IN_SPLITS = (ATTN_WIDTH, ATTN_WIDTH, ATTN_WIDTH, SSD_WIDTH, SSD_WIDTH,
             SSD_GROUPS * SSD_STATE, SSD_GROUPS * SSD_STATE, SSD_HEADS)
D_IN = sum(IN_SPLITS)
MEM_LEN = 256
XA_HEADS = 4
XA_HEAD_DIM = D_MODEL // XA_HEADS
D_FF = 2816
EPS = 1e-6


def rmsnorm(x, g):
    x32 = x.astype(jnp.float32)
    y = x32 * lax.rsqrt(jnp.mean(x32 * x32, axis=-1, keepdims=True) + EPS)
    return (y * g.astype(jnp.float32)).astype(x.dtype)

def swiglu(h, w_gu, w_down):
    gu = h @ w_gu
    g, u = jnp.split(gu, 2, axis=-1)
    return (jax.nn.silu(g) * u) @ w_down

def stick_breaking_attention(q, k, v):
    b_, h_, s_, d_ = q.shape
    scale = 1.0 / math.sqrt(d_)
    outs = []
    for i in range(s_ // SB_BLOCK):
        t0, t1 = i * SB_BLOCK, (i + 1) * SB_BLOCK
        qb = q[:, :, t0:t1].astype(jnp.float32)
        kb = k[:, :, :t1].astype(jnp.float32)
        vb = v[:, :, :t1]
        z = jnp.einsum('bhtd,bhsd->bhts', qb, kb) * scale
        t_idx = t0 + jnp.arange(SB_BLOCK)
        s_idx = jnp.arange(t1)
        causal = s_idx[None, :] < t_idx[:, None]
        log_1mb = jnp.where(causal, jax.nn.log_sigmoid(-z), 0.0)
        suffix = lax.cumsum(log_1mb, axis=3, reverse=True) - log_1mb
        log_a = jnp.where(causal, jax.nn.log_sigmoid(z) + suffix, -jnp.inf)
        a = jnp.exp(log_a)
        outs.append(jnp.einsum('bhts,bhsd->bhtd', a, vb.astype(jnp.float32)))
    return jnp.concatenate(outs, axis=2).astype(v.dtype)

def ssd_chunked(xs, dt, a, bmat, cmat):
    b_, s_, h_, p_ = xs.shape
    L, G, N = SSD_CHUNK, SSD_GROUPS, SSD_STATE
    R = h_ // G
    nc = s_ // L
    x = (xs.astype(jnp.float32) * dt[..., None]).reshape(b_, nc, L, G, R, p_)
    adt = (dt * a).reshape(b_, nc, L, G, R).transpose(0, 3, 4, 1, 2)
    a_cs = jnp.cumsum(adt, axis=-1)
    bc = bmat.astype(jnp.float32).reshape(b_, nc, L, G, N)
    cc = cmat.astype(jnp.float32).reshape(b_, nc, L, G, N)
    tri = jnp.tril(jnp.ones((L, L), dtype=bool))
    diff = a_cs[..., :, None] - a_cs[..., None, :]
    lmat = jnp.exp(jnp.where(tri, diff, -jnp.inf))
    cb = jnp.einsum('bclgn,bcsgn->bcgls', cc, bc)
    y_diag = jnp.einsum('bcgls,bgrcls,bcsgrp->bclgrp', cb, lmat, x)
    decay_states = jnp.exp(a_cs[..., -1:] - a_cs)
    states = jnp.einsum('bclgn,bgrcl,bclgrp->bcgrpn', bc, decay_states, x)
    chunk_decay = jnp.exp(a_cs[..., -1])

    def step(h, inp):
        st, dec = inp
        return h * dec[..., None, None] + st, h

    h0 = jnp.zeros_like(states[:, 0])
    _, states_in = lax.scan(step, h0, (jnp.moveaxis(states, 1, 0),
                                       jnp.moveaxis(chunk_decay, -1, 0)))
    states_in = jnp.moveaxis(states_in, 0, 1)
    y_off = jnp.einsum('bclgn,bcgrpn,bgrcl->bclgrp', cc, states_in, jnp.exp(a_cs))
    return (y_diag + y_off).reshape(b_, s_, h_, p_)

def hybrid_mixer(u, w_in, conv_w, conv_b, dt_bias, a_log, d_skip,
                 ssd_norm_g, attn_norm_g, w_out):
    b_, s_, _ = u.shape
    proj = u @ w_in
    q, k, v, z, xs, bm, cm, dt_raw = jnp.split(proj, np.cumsum(IN_SPLITS)[:-1], axis=-1)
    def heads(t):
        return t.reshape(b_, s_, SB_HEADS, SB_HEAD_DIM).transpose(0, 2, 1, 3)
    o_att = stick_breaking_attention(heads(q), heads(k), heads(v))
    o_att = o_att.transpose(0, 2, 1, 3).reshape(b_, s_, ATTN_WIDTH)
    o_att = rmsnorm(o_att, attn_norm_g)
    xbc = jnp.concatenate([xs, bm, cm], axis=-1)
    xbc = lax.conv_general_dilated(
        xbc, conv_w.astype(xbc.dtype)[:, None, :], window_strides=(1,),
        padding=[(SSD_CONV_K - 1, 0)], dimension_numbers=('NWC', 'WIO', 'NWC'),
        feature_group_count=SSD_CONV_CH)
    xbc = jax.nn.silu(xbc + conv_b)
    xs, bm, cm = jnp.split(xbc, [SSD_WIDTH, SSD_WIDTH + SSD_GROUPS * SSD_STATE], axis=-1)
    xs = xs.reshape(b_, s_, SSD_HEADS, SSD_HEAD_DIM)
    bm = bm.reshape(b_, s_, SSD_GROUPS, SSD_STATE)
    cm = cm.reshape(b_, s_, SSD_GROUPS, SSD_STATE)
    dt = jax.nn.softplus(dt_raw.astype(jnp.float32) + dt_bias.astype(jnp.float32))
    a = -jnp.exp(a_log.astype(jnp.float32))
    y = ssd_chunked(xs, dt, a, bm, cm)
    y = y + d_skip.astype(jnp.float32)[:, None] * xs.astype(jnp.float32)
    y = y.reshape(b_, s_, SSD_WIDTH) * jax.nn.silu(z.astype(jnp.float32))
    y = rmsnorm(y.reshape(b_, s_, SSD_GROUPS, SSD_WIDTH // SSD_GROUPS),
                ssd_norm_g.reshape(SSD_GROUPS, SSD_WIDTH // SSD_GROUPS))
    o_ssd = y.reshape(b_, s_, SSD_WIDTH).astype(u.dtype)
    return jnp.concatenate([o_att, o_ssd], axis=-1) @ w_out

def memory_cross_attention(h, mem_n, wq, wkv, wo):
    b_, s_, _ = h.shape
    q = (h @ wq).reshape(b_, s_, XA_HEADS, XA_HEAD_DIM)
    kv = mem_n @ wkv
    k, v = jnp.split(kv, 2, axis=-1)
    k = k.reshape(b_, MEM_LEN, XA_HEADS, XA_HEAD_DIM)
    v = v.reshape(b_, MEM_LEN, XA_HEADS, XA_HEAD_DIM)
    sc = jnp.einsum('bshd,bmhd->bhsm', q.astype(jnp.float32), k.astype(jnp.float32))
    p = jax.nn.softmax(sc / math.sqrt(XA_HEAD_DIM), axis=-1)
    o = jnp.einsum('bhsm,bmhd->bshd', p, v.astype(jnp.float32)).astype(h.dtype)
    return o.reshape(b_, s_, D_MODEL) @ wo

def first_inputs(seed: int = 0) -> dict:
    key = jax.random.key(seed)
    ks = iter(jax.random.split(key, 40))

    def w(shape, fan_in):
        return jax.random.normal(next(ks), (DEPTH,) + shape, jnp.float32) * fan_in ** -0.5

    def gain(n):
        return 1.0 + 0.02 * jax.random.normal(next(ks), (DEPTH, n), jnp.float32)

    x = jax.random.normal(next(ks), (BATCH, SEQ, D_MODEL), jnp.float32)
    mem = jax.random.normal(next(ks), (BATCH, MEM_LEN, D_MODEL), jnp.float32)
    dt0 = jnp.exp(jax.random.uniform(next(ks), (DEPTH, SSD_HEADS), jnp.float32,
                                     math.log(1e-3), math.log(1e-1)))
    dt_bias = dt0 + jnp.log(-jnp.expm1(-dt0))
    a_log = jnp.log(jax.random.uniform(next(ks), (DEPTH, SSD_HEADS), jnp.float32, 1.0, 16.0))
    return {
        "x": x, "mem": mem,
        "ffn1_pre_g": gain(D_MODEL),
        "ffn1_w_gu": w((D_MODEL, 2 * D_FF), D_MODEL),
        "ffn1_w_down": w((D_FF, D_MODEL), D_FF),
        "ffn1_post_g": gain(D_MODEL),
        "mix_pre_g": gain(D_MODEL),
        "w_in": w((D_MODEL, D_IN), D_MODEL),
        "conv_w": w((SSD_CONV_K, SSD_CONV_CH), SSD_CONV_K),
        "conv_b": 0.02 * jax.random.normal(next(ks), (DEPTH, SSD_CONV_CH), jnp.float32),
        "dt_bias": dt_bias,
        "a_log": a_log,
        "d_skip": 1.0 + 0.1 * jax.random.normal(next(ks), (DEPTH, SSD_HEADS), jnp.float32),
        "ssd_norm_g": gain(SSD_WIDTH),
        "attn_norm_g": gain(ATTN_WIDTH),
        "w_out": w((D_MIX, D_MODEL), D_MIX),
        "mix_post_g": gain(D_MODEL),
        "xa_pre_g": gain(D_MODEL),
        "mem_g": gain(D_MODEL),
        "xa_wq": w((D_MODEL, D_MODEL), D_MODEL),
        "xa_wkv": w((D_MODEL, 2 * D_MODEL), D_MODEL),
        "xa_wo": w((D_MODEL, D_MODEL), D_MODEL),
        "xa_post_g": gain(D_MODEL),
        "ffn2_pre_g": gain(D_MODEL),
        "ffn2_w_gu": w((D_MODEL, 2 * D_FF), D_MODEL),
        "ffn2_w_down": w((D_FF, D_MODEL), D_FF),
        "ffn2_post_g": gain(D_MODEL),
    }

def first_block(x, mem, ffn1_pre_g, ffn1_w_gu, ffn1_w_down, ffn1_post_g,
              mix_pre_g, w_in, conv_w, conv_b, dt_bias, a_log, d_skip,
              ssd_norm_g, attn_norm_g, w_out, mix_post_g,
              xa_pre_g, mem_g, xa_wq, xa_wkv, xa_wo, xa_post_g,
              ffn2_pre_g, ffn2_w_gu, ffn2_w_down, ffn2_post_g):
    h = x
    for l in range(DEPTH):
        f = swiglu(rmsnorm(h, ffn1_pre_g[l]), ffn1_w_gu[l], ffn1_w_down[l])
        h = h + 0.5 * rmsnorm(f, ffn1_post_g[l])
        m = hybrid_mixer(rmsnorm(h, mix_pre_g[l]), w_in[l], conv_w[l], conv_b[l],
                         dt_bias[l], a_log[l], d_skip[l], ssd_norm_g[l],
                         attn_norm_g[l], w_out[l])
        h = h + rmsnorm(m, mix_post_g[l])
        c = memory_cross_attention(rmsnorm(h, xa_pre_g[l]), rmsnorm(mem, mem_g[l]),
                                   xa_wq[l], xa_wkv[l], xa_wo[l])
        h = h + rmsnorm(c, xa_post_g[l])
        f = swiglu(rmsnorm(h, ffn2_pre_g[l]), ffn2_w_gu[l], ffn2_w_down[l])
        h = h + 0.5 * rmsnorm(f, ffn2_post_g[l])
    return h


ATTN_HEADS = 8
ATTN_KV_HEADS = 2
ATTN_GROUP = ATTN_HEADS // ATTN_KV_HEADS
ATTN_HEAD_DIM = 64
ATTN_WIDTH_2 = ATTN_HEADS * ATTN_HEAD_DIM
KV_WIDTH = ATTN_KV_HEADS * ATTN_HEAD_DIM
WINDOW = 128
ATTN_BLOCK = 128

HGRN_HEADS = 4
HGRN_DK = 128
HGRN_DV = 128
HGRN_WIDTH = HGRN_HEADS * HGRN_DK
HGRN_V_WIDTH = HGRN_HEADS * HGRN_DV
HGRN_CHUNK = 32

N_BRANCHES = 2
IN_WIDTH = ATTN_WIDTH_2 + 2 * KV_WIDTH + 2 * HGRN_WIDTH + 2 * HGRN_V_WIDTH + N_BRANCHES * D_MODEL

PEER_HEADS = 8
PEER_N_KEYS = 128
PEER_N_EXPERTS = PEER_N_KEYS * PEER_N_KEYS
PEER_KEY_DIM = 128
PEER_TOPK = 16
PEER_TOKEN_BLOCK = 128

MASK_VALUE = -1e30


def rms_norm(x, g):
    xf = x.astype(jnp.float32)
    y = xf * lax.rsqrt(jnp.mean(xf * xf, axis=-1, keepdims=True) + EPS)
    return (y * g.astype(jnp.float32)).astype(x.dtype)

def alibi_slopes():
    return jnp.asarray(2.0 ** (-8.0 * np.arange(1, ATTN_HEADS + 1) / ATTN_HEADS), dtype=jnp.float32)

def split_combined(proj):
    sizes = (ATTN_WIDTH_2, KV_WIDTH, KV_WIDTH, HGRN_WIDTH, HGRN_WIDTH,
             HGRN_V_WIDTH, HGRN_V_WIDTH, D_MODEL, D_MODEL)
    offsets = np.cumsum(sizes)[:-1].tolist()
    return jnp.split(proj, offsets, axis=-1)

def sliding_window_attention(q, k, v, sinks):
    B, S = q.shape[0], q.shape[1]
    W = ATTN_BLOCK
    nb = S // W
    qb = q.reshape(B, nb, W, ATTN_KV_HEADS, ATTN_GROUP, ATTN_HEAD_DIM)

    def with_prev(t):
        tb = t.reshape(B, nb, W, ATTN_KV_HEADS, ATTN_HEAD_DIM)
        prev = jnp.concatenate([jnp.zeros_like(tb[:, :1]), tb[:, :-1]], axis=1)
        return jnp.concatenate([prev, tb], axis=2)

    kc, vc = with_prev(k), with_prev(v)
    scale = ATTN_HEAD_DIM ** -0.5
    s = jnp.einsum('bnqkgd,bnskd->bnkgqs', qb, kc,
                   preferred_element_type=jnp.float32) * scale
    qpos = jnp.arange(W)[:, None] + W
    kpos = jnp.arange(2 * W)[None, :]
    dist = qpos - kpos
    blk = jnp.arange(nb)[:, None, None]
    valid = (dist >= 0) & (dist < WINDOW) & (blk * W + kpos - W >= 0)
    slopes = alibi_slopes().reshape(ATTN_KV_HEADS, ATTN_GROUP)
    s = s - slopes[:, :, None, None] * dist.astype(jnp.float32)
    s = jnp.where(valid[None, :, None, None], s, MASK_VALUE)
    sink = jnp.broadcast_to(sinks.astype(jnp.float32).reshape(ATTN_KV_HEADS, ATTN_GROUP)[:, :, None, None],
                            s.shape[:-1] + (1,))
    p = jax.nn.softmax(jnp.concatenate([s, sink], axis=-1), axis=-1)[..., :-1]
    o = jnp.einsum('bnkgqs,bnskd->bnqkgd', p.astype(v.dtype), vc)
    return o.reshape(B, S, ATTN_WIDTH_2)

def hgrn2_recurrence(q, f_logit, i, lower_bound):
    B, S = q.shape[0], q.shape[1]
    C = HGRN_CHUNK
    nc = S // C
    f32 = jnp.float32
    f = lower_bound + (1.0 - lower_bound) * jax.nn.sigmoid(f_logit.astype(f32))
    k = 1.0 - f
    logf = jnp.log(f)

    def chunk(t):
        return t.reshape(B, nc, C, HGRN_HEADS, t.shape[-1])

    qc, kc, lc, vc = chunk(q.astype(f32)), chunk(k), chunk(logf), chunk(i.astype(f32))
    b = jnp.cumsum(lc, axis=2)
    q_dec = qc * jnp.exp(b)
    k_inv = kc * jnp.exp(-b)
    causal = jnp.tril(jnp.ones((C, C), dtype=bool))
    a = jnp.where(causal, jnp.einsum('bnthd,bnshd->bnhts', q_dec, k_inv), 0.0)
    o_intra = jnp.einsum('bnhts,bnshv->bnthv', a, vc)
    b_last = b[:, :, -1:]
    ds = jnp.einsum('bnshd,bnshv->bnhdv', kc * jnp.exp(b_last - b), vc)
    decay = jnp.exp(b_last[:, :, 0])

    def step(state, inp):
        dec, d = inp
        return dec[..., None] * state + d, state

    s0 = jnp.zeros((B, HGRN_HEADS, HGRN_DK, HGRN_DV), f32)
    _, s_prev = lax.scan(step, s0, (jnp.moveaxis(decay, 1, 0), jnp.moveaxis(ds, 1, 0)))
    s_prev = jnp.moveaxis(s_prev, 0, 1)
    o_inter = jnp.einsum('bnthd,bnhdv->bnthv', q_dec, s_prev)
    return (o_intra + o_inter).reshape(B, S, HGRN_HEADS, HGRN_DV)

def peer_layer(h, w_q, keys, u, v):
    B, S = h.shape[0], h.shape[1]
    q = (h @ w_q).reshape(B, S, PEER_HEADS, 2, PEER_KEY_DIM)
    sc = jnp.einsum('bshpd,phnd->bshpn', q, keys).astype(jnp.float32)
    v1, i1 = lax.top_k(sc[..., 0, :], PEER_TOPK)
    v2, i2 = lax.top_k(sc[..., 1, :], PEER_TOPK)
    cand = (v1[..., :, None] + v2[..., None, :]).reshape(B, S, PEER_HEADS, PEER_TOPK * PEER_TOPK)
    cidx = (i1[..., :, None] * PEER_N_KEYS + i2[..., None, :]).reshape(B, S, PEER_HEADS, PEER_TOPK * PEER_TOPK)
    best, pos = lax.top_k(cand, PEER_TOPK)
    idx = jnp.take_along_axis(cidx, pos, axis=-1)
    gates = jax.nn.softmax(best, axis=-1)
    T = B * S
    nblk = T // PEER_TOKEN_BLOCK
    hk = PEER_HEADS * PEER_TOPK
    hb = h.reshape(nblk, PEER_TOKEN_BLOCK, D_MODEL)
    ib = idx.reshape(nblk, PEER_TOKEN_BLOCK, hk)
    gb = gates.reshape(nblk, PEER_TOKEN_BLOCK, hk).astype(h.dtype)

    def expert_block(args):
        ht, it, gt = args
        ue = jnp.take(u, it, axis=0)
        act = jax.nn.gelu(jnp.einsum('tkd,td->tk', ue, ht), approximate=False)
        ve = jnp.take(v, it, axis=0)
        return jnp.einsum('tk,tkd->td', gt * act, ve)

    out = lax.map(expert_block, (hb, ib, gb))
    return out.reshape(B, S, D_MODEL)

def hybrid_layer(x, norm_mix_g, w_in, sinks, lower_bound, hgrn_norm_g, w_attn_proj,
                 w_hgrn_proj, w_out, norm_ffn_g, w_peer_q, peer_keys, peer_u, peer_v):
    B, S = x.shape[0], x.shape[1]
    h = rms_norm(x, norm_mix_g)
    aq, ak, av, hq, hf, hi, hg, ga, gh = split_combined(h @ w_in)
    y_attn = sliding_window_attention(aq.reshape(B, S, ATTN_HEADS, ATTN_HEAD_DIM),
                                      ak.reshape(B, S, ATTN_KV_HEADS, ATTN_HEAD_DIM),
                                      av.reshape(B, S, ATTN_KV_HEADS, ATTN_HEAD_DIM), sinks)
    o = hgrn2_recurrence(jax.nn.silu(hq).reshape(B, S, HGRN_HEADS, HGRN_DK),
                         hf.reshape(B, S, HGRN_HEADS, HGRN_DK),
                         hi.reshape(B, S, HGRN_HEADS, HGRN_DV), lower_bound)
    o = rms_norm(o, hgrn_norm_g).astype(x.dtype) * jax.nn.silu(hg.reshape(B, S, HGRN_HEADS, HGRN_DV))
    y_hgrn = o.reshape(B, S, HGRN_V_WIDTH)
    merged = jax.nn.sigmoid(ga) * (y_attn @ w_attn_proj) + jax.nn.sigmoid(gh) * (y_hgrn @ w_hgrn_proj)
    x = x + merged @ w_out
    x = x + peer_layer(rms_norm(x, norm_ffn_g), w_peer_q, peer_keys, peer_u, peer_v)
    return x

def second_inputs(seed: int = 0) -> dict:
    key = jax.random.key(seed)
    ks = jax.random.split(key, 16)
    f32 = jnp.float32
    n = jax.random.normal
    return {
        "x": n(ks[0], (BATCH, SEQ, D_MODEL), f32),
        "norm_mix_g": 1.0 + 0.02 * n(ks[1], (DEPTH, D_MODEL), f32),
        "w_in": n(ks[2], (DEPTH, D_MODEL, IN_WIDTH), f32) * D_MODEL ** -0.5,
        "attn_sinks": n(ks[3], (DEPTH, ATTN_HEADS), f32),
        "hgrn_lb_logits": 0.1 * n(ks[4], (DEPTH + 1, HGRN_WIDTH), f32),
        "hgrn_norm_g": 1.0 + 0.02 * n(ks[5], (DEPTH, HGRN_DV), f32),
        "w_attn_proj": n(ks[6], (DEPTH, ATTN_WIDTH_2, D_MODEL), f32) * ATTN_WIDTH_2 ** -0.5,
        "w_hgrn_proj": n(ks[7], (DEPTH, HGRN_V_WIDTH, D_MODEL), f32) * HGRN_V_WIDTH ** -0.5,
        "w_out": n(ks[8], (DEPTH, D_MODEL, D_MODEL), f32) * D_MODEL ** -0.5,
        "norm_ffn_g": 1.0 + 0.02 * n(ks[9], (DEPTH, D_MODEL), f32),
        "w_peer_q": n(ks[10], (DEPTH, D_MODEL, PEER_HEADS * 2 * PEER_KEY_DIM), f32) * D_MODEL ** -0.5,
        "peer_keys": n(ks[11], (DEPTH, 2, PEER_HEADS, PEER_N_KEYS, PEER_KEY_DIM), f32) * PEER_KEY_DIM ** -0.5,
        "peer_u": n(ks[12], (DEPTH, PEER_N_EXPERTS, D_MODEL), f32) * D_MODEL ** -0.5,
        "peer_v": n(ks[13], (DEPTH, PEER_N_EXPERTS, D_MODEL), f32) * PEER_HEADS ** -0.5,
        "norm_final_g": 1.0 + 0.02 * n(ks[14], (D_MODEL,), f32),
    }

def second_block(x, norm_mix_g, w_in, attn_sinks, hgrn_lb_logits, hgrn_norm_g, w_attn_proj,
              w_hgrn_proj, w_out, norm_ffn_g, w_peer_q, peer_keys, peer_u, peer_v, norm_final_g):
    lower_bounds = jnp.cumsum(jax.nn.softmax(hgrn_lb_logits.astype(jnp.float32), axis=0), axis=0)
    for layer in range(DEPTH):
        x = hybrid_layer(x, norm_mix_g[layer], w_in[layer], attn_sinks[layer],
                         lower_bounds[layer].reshape(HGRN_HEADS, HGRN_DK), hgrn_norm_g[layer],
                         w_attn_proj[layer], w_hgrn_proj[layer], w_out[layer], norm_ffn_g[layer],
                         w_peer_q[layer], peer_keys[layer], peer_u[layer], peer_v[layer])
    return rms_norm(x, norm_final_g)


def setup_inputs(seed=0):
    out = dict(first_inputs(seed))
    for name, value in second_inputs(seed + 1).items():
        if name != "x":
            out[name + "_2"] = value
    return out


def reference(
    x, mem, ffn1_pre_g, ffn1_w_gu, ffn1_w_down, ffn1_post_g, mix_pre_g, w_in, conv_w, conv_b,
    dt_bias, a_log, d_skip, ssd_norm_g, attn_norm_g, w_out, mix_post_g, xa_pre_g, mem_g, xa_wq,
    xa_wkv, xa_wo, xa_post_g, ffn2_pre_g, ffn2_w_gu, ffn2_w_down, ffn2_post_g, norm_mix_g_2,
    w_in_2, attn_sinks_2, hgrn_lb_logits_2, hgrn_norm_g_2, w_attn_proj_2, w_hgrn_proj_2,
    w_out_2, norm_ffn_g_2, w_peer_q_2, peer_keys_2, peer_u_2, peer_v_2, norm_final_g_2,
):
    x = first_block(
        x, mem, ffn1_pre_g, ffn1_w_gu, ffn1_w_down, ffn1_post_g, mix_pre_g, w_in, conv_w,
        conv_b, dt_bias, a_log, d_skip, ssd_norm_g, attn_norm_g, w_out, mix_post_g, xa_pre_g,
        mem_g, xa_wq, xa_wkv, xa_wo, xa_post_g, ffn2_pre_g, ffn2_w_gu, ffn2_w_down, ffn2_post_g,
    )
    return second_block(
        x, norm_mix_g_2, w_in_2, attn_sinks_2, hgrn_lb_logits_2, hgrn_norm_g_2, w_attn_proj_2,
        w_hgrn_proj_2, w_out_2, norm_ffn_g_2, w_peer_q_2, peer_keys_2, peer_u_2, peer_v_2,
        norm_final_g_2,
    )


_drawn_inputs = setup_inputs


def setup_inputs(seed=0):
    import zlib

    import numpy as np

    out = dict(_drawn_inputs(seed))
    spreads = {}
    factors = {'ffn1_pre_g': 2.783,
     'ffn1_post_g': 3.715,
     'conv_b': 3.043,
     'ssd_norm_g': 3.923,
     'attn_norm_g': 4.078,
     'mix_post_g': 3.105,
     'xa_pre_g': 3.593,
     'xa_post_g': 3.559,
     'ffn2_pre_g': 4.792,
     'ffn2_post_g': 16.88,
     'norm_mix_g_2': 5.718,
     'attn_sinks_2': 109.515,
     'hgrn_lb_logits_2': 8.0,
     'hgrn_norm_g_2': 8.0,
     'norm_ffn_g_2': 31.904,
     'norm_final_g_2': 23.091}
    for name, (base, spread) in spreads.items():
        noise = np.random.default_rng([zlib.crc32(name.encode()), seed]).standard_normal(out[name].shape)
        drawn = base * np.exp(spread * noise) if base else spread * noise
        out[name] = __import__('jax').numpy.asarray(drawn.astype(out[name].dtype))
    for name, factor in factors.items():
        out[name] = (out[name] * factor).astype(out[name].dtype)
    return out
```

```python
from contextlib import ExitStack

import concourse.bass as bass
from concourse import mybir

F32 = mybir.dt.float32
U32 = mybir.dt.uint32
ALU = mybir.AluOpType
ACT = mybir.ActivationFunctionType
AX = mybir.AxisListType

P = 128
D = 1024
T = 256
EPS = 1e-6
NSLOT = 8
NGATH = 20
FFN_TILES = 22


class Chip:

    def __init__(self, nc, ctx):
        self.nc = nc
        self.ctx = ctx
        self.count = {}
        self.seen = {}
        self.engine = {"pe": nc.tensor, "dve": nc.vector, "act": nc.scalar, "pool": nc.gpsimd, "sp": nc.sync}
        self.sem = {k: self.semaphore("done_" + k) for k in ("pe", "dve", "act", "pool")}

    def semaphore(self, name):
        s = self.ctx.enter_context(self.nc.semaphore(name))
        self.count[name] = 0
        return (name, s)

    def wait(self, eng, toks):
        for t in toks:
            if t is None:
                continue
            if type(t) is list:
                self.wait(eng, t)
                continue
            (name, s), v = t
            if self.seen.get((eng, name), 0) < v:
                self.seen[(eng, name)] = v
                self.engine[eng].wait_ge(s, v)

    def mark(self, sem, ins, n):
        ins.then_inc(sem[1], n)
        self.count[sem[0]] += n
        return (sem, self.count[sem[0]])

    def dve(self, waits, f):
        self.wait("dve", waits)
        return self.mark(self.sem["dve"], f(self.nc.vector), 1)

    def act(self, waits, f):
        self.wait("act", waits)
        return self.mark(self.sem["act"], f(self.nc.scalar), 1)

    def pool(self, waits, f):
        self.wait("pool", waits)
        return self.mark(self.sem["pool"], f(self.nc.gpsimd), 1)

    def pe(self, waits, f):
        self.wait("pe", waits)
        return self.mark(self.sem["pe"], f(self.nc.tensor), 1)

    def mm(self, out, lhsT, rhs, start, stop=True):
        return self.nc.tensor.matmul(out, lhsT, rhs, start=start, stop=stop, skip_group_check=True)

    def dma(self, eng, sem, waits, out, in_):
        self.wait(eng, waits)
        return self.mark(sem, self.engine[eng].dma_start(out, in_), 16)


class Bank:

    def __init__(self, ap):
        self.ap = ap
        self.free = []


class Banks:
    def __init__(self, banks):
        self.banks = banks
        self.n = 0

    def take(self):
        b = self.banks[self.n % len(self.banks)]
        self.n += 1
        return b


class Slot:
    def __init__(self, ap, sem):
        self.ap = ap
        self.sem = sem
        self.free = []


def build(nc, A, out):
    with ExitStack() as ctx:
        body(nc, ctx, A, out)


def body(nc, ctx, A, out):
    k = Chip(nc, ctx)
    dve, act, pool, pe, mm = k.dve, k.act, k.pool, k.pe, k.mm

    def sb(name, shape, dt=F32):
        return ctx.enter_context(nc.sbuf_tensor(name, shape, dt))

    H = sb("H", [P, 2, D])
    NT = sb("NT", [P, 8, T])
    XN = sb("XN", [P, 2, D])
    JA = sb("JA", [P, D])
    ring = sb("ring", [P, NSLOT, 2048])
    GB = sb("GB", [P, 6, D])
    PG = sb("PG", [P, 160])
    cst = sb("cst", [P, 8, P])
    small = sb("small", [P, 512])
    LB = sb("LB", [P, 2, 512])
    AR = sb("AR", [P, 19300])
    AU = AR[:, :].bitcast(U32)
    ps = ctx.enter_context(nc.psum_tensor("ps", [P, 8, 512], F32))
    bank = [Bank(ps[:, i, :]) for i in range(8)]
    slots = [Slot(ring[:, i, :], k.semaphore(f"slot{i}")) for i in range(NSLOT)]
    nslot = [0]

    ident, ones, negtri, negones, tri_le, tri_gt, bt_le, bt_gt = [cst[:, i, :] for i in range(8)]

    smallat = [0]

    def sm(n):
        a = smallat[0]
        smallat[0] += n
        return small[:, a:a + n]

    def ar(off, *shape):
        n = 1
        for s in shape:
            n *= s
        v = AR[:, off:off + n]
        if len(shape) == 2:
            v = v.rearrange("p (a b) -> p a b", a=shape[0])
        if len(shape) == 3:
            v = v.rearrange("p (a b c) -> p a b c", a=shape[0], b=shape[1])
        return v

    def load(src, kt, n):
        s = slots[nslot[0] % NSLOT]
        nslot[0] += 1
        v = s.ap[:, 0:kt * n].rearrange("p (k n) -> p k n", k=kt)
        tok = k.dma("sp", s.sem, s.free, v, src)
        return s, v, tok

    s_x = k.semaphore("s_x")
    t_x = k.dma("sp", s_x, [], H[:, :, :], A["x"][0].rearrange("(h p) d -> p h d", p=P))
    rows1 = AR[:, 0:128]
    rows2 = AR[0:61, 128:256]
    s_g = k.semaphore("s_g")
    col = {}
    at = 0
    t_g = None
    for name, n in (("ffn1_pre_g", 8), ("mix_pre_g", 8), ("xa_pre_g", 8), ("mem_g", 8), ("ffn2_pre_g", 8),
                    ("norm_mix_g_2", 8), ("norm_ffn_g_2", 8), ("attn_norm_g", 8), ("ssd_norm_g", 8),
                    ("conv_b", 12), ("hgrn_norm_g_2", 1)):
        col[name] = at
        t_g = k.dma("act", s_g, [], AR[at:at + n, 0:128], A[name][0].rearrange("(c p) -> c p", p=P))
        at += n
    n_rows1 = at
    for i in range(4):
        col["conv_w%d" % i] = 112 + 12 * i
    t_g = k.dma("act", s_g, [], AR[0:48, 128:256], A["conv_w"][0].rearrange("k (c p) -> (k c) p", p=P))

    s_b = k.semaphore("s_b")
    gi = {}
    for i, name in enumerate(("ffn1_post_g", "mix_post_g", "xa_post_g", "ffn2_post_g", "norm_ffn_g_2",
                              "norm_final_g_2")):
        gi[name] = i
        src = A[name] if name == "norm_final_g_2" else A[name][0]
        t_b = k.dma("act", s_b, [], GB[:, i, :], src.unsqueeze(0).broadcast_to([P, D]))
    dtb, alog, dsk, sink = sm(16), sm(16), sm(16), sm(8)
    for v, name, n in ((dtb, "dt_bias", 16), (alog, "a_log", 16), (dsk, "d_skip", 16), (sink, "attn_sinks_2", 8)):
        t_b = k.dma("act", s_b, [], v, A[name][0].unsqueeze(0).broadcast_to([P, n]))
    t_b = k.dma("act", s_b, [], LB[:, :, :], A["hgrn_lb_logits_2"].unsqueeze(0).broadcast_to([P, 2, 512]))

    t = pool([], lambda e: e.memset(ident, 0.0))
    t = pool([], lambda e: e.memset(cst[:, 1:3, :], 1.0))
    t = pool([], lambda e: e.memset(cst[:, 3, :], -1.0))
    t = pool([], lambda e: e.memset(cst[:, 4:8, :], 1.0))
    t = pool([t], lambda e: e.memset(negtri, -1.0))

    def sel(v, base, pattern, cm, op, fill=0.0):
        return lambda e: e.affine_select(out=v, in_=v, compare_op=op, fill=fill, base=base, pattern=pattern,
                                         channel_multiplier=cm)

    t_id = pool([t], sel(ident, 0, [[-1, P]], 1, ALU.not_equal, 1.0))
    pool([], sel(negtri, 0, [[-1, P]], 1, ALU.is_ge))
    pool([], sel(tri_le, 0, [[1, P]], -1, ALU.is_ge))
    pool([], sel(tri_gt, 0, [[-1, P]], 1, ALU.is_gt))
    t1 = pool([], sel(bt_le, 0, [[1, P]], -1, ALU.is_ge))
    t2 = pool([], sel(bt_gt, 0, [[-1, P]], 1, ALU.is_gt))
    t1 = pool([t1, t2], sel(bt_le, 0, [[-32, 4], [0, 32]], 1, ALU.is_ge))
    t_cst = pool([t1], sel(bt_gt, 31, [[32, 4], [0, 32]], -1, ALU.is_ge))

    b = bank[0]
    k.wait("pe", [t_id, t_g])
    nc.tensor.transpose(b.ap[:, 0:n_rows1], AR[0:n_rows1, 0:128], ident[0:n_rows1, 0:n_rows1])
    t = pe([], lambda e: e.transpose(b.ap[:, 112:160], AR[0:48, 128:256], ident[0:48, 0:48]))
    dve([t], lambda e: e.tensor_copy(PG[:, 0:n_rows1], b.ap[:, 0:n_rows1]))
    t_pg = dve([], lambda e: e.tensor_copy(PG[:, 112:160], b.ap[:, 112:160]))
    b.free = [t_pg]

    def pg(name, c):
        a = col[name] + c
        return PG[:, a:a + 1]

    lt = ar(17000, 3, 512)
    t = dve([t_b], lambda e: e.tensor_tensor(lt[:, 2, :], LB[:, 0, :], LB[:, 1, :], ALU.max))
    t = dve([t], lambda e: e.tensor_tensor(lt[:, 0:2, :], LB[:, :, :], lt[:, 2, :].unsqueeze(1).broadcast_to([P, 2, 512]),
                                           ALU.subtract))
    t = act([t], lambda e: e.activation(lt[:, 0:2, :], lt[:, 0:2, :], ACT.Exp))
    t = dve([t], lambda e: e.tensor_tensor(lt[:, 1, :], lt[:, 0, :], lt[:, 1, :], ALU.add))
    t = dve([t], lambda e: e.reciprocal(lt[:, 1, :], lt[:, 1, :]))
    t = dve([t], lambda e: e.tensor_tensor(LB[:, 0, :], lt[:, 0, :], lt[:, 1, :], ALU.mult))
    t_lb = dve([t], lambda e: e.tensor_scalar(LB[:, 1, :], LB[:, 0, :], -1.0, 1.0, ALU.mult, ALU.add))

    ssq = sm(2)
    rs = sm(2)
    msq = sm(2)
    half_c = sm(16)
    t_hc = pool([], lambda e: e.memset(half_c, -0.5))
    norm_state = {"ja": None, "xn": [], "nt": [], "rs": None}

    def rstd(half, src, n, waits, ss=None, j=None):
        i = half if j is None else j
        t = act([waits, norm_state["ja"]], lambda e: e.activation(JA[:, 0:src_len(src)], src, ACT.Square,
                                                                  accum_out=ssq[:, i:i + 1]))
        norm_state["ja"] = t
        t1 = dve([t], lambda e: e.tensor_scalar(msq[:, i:i + 1], ssq[:, i:i + 1], 1.0 / n, EPS, ALU.mult, ALU.add))
        t2 = pool([t1, t_hc], lambda e: e.tensor_tensor(rs[:, i:i + 1], msq[:, i:i + 1], half_c[:, 0:1], ALU.pow))
        return t, t2

    def src_len(src):
        return src.shape[-1]

    def turn(src, gain, waits, banks, dst=NT):
        last = []
        for pair in range(4):
            b = banks.take()
            k.wait("pe", [b.free, waits, t_id])
            for cc in range(2):
                for half in range(2):
                    c = 2 * pair + cc
                    ins = nc.tensor.transpose(b.ap[:, cc * 256 + half * 128:cc * 256 + half * 128 + 128],
                                              src[:, half, c * 128:(c + 1) * 128], ident)
            t = k.mark(k.sem["pe"], ins, 1)
            for cc in range(2):
                c = 2 * pair + cc
                o, i_ = dst[:, c, :], b.ap[:, cc * 256:cc * 256 + 256]
                if gain is None:
                    t2 = dve([t, norm_state["nt"]], lambda e: e.tensor_copy(o, i_))
                elif pair % 2:
                    t2 = act([t, norm_state["nt"], t_pg],
                             lambda e: e.activation(o, i_, ACT.Copy, scale=pg(gain, c)))
                else:
                    t2 = dve([t, norm_state["nt"], t_pg],
                             lambda e: e.tensor_scalar(o, i_, pg(gain, c), None, ALU.mult))
            b.free = [t2]
            last.append(t2)
        return last

    def prenorm(src, gain, waits, banks):
        ts = []
        for half in range(2):
            _, t = rstd(half, src[:, half, :], D, [waits, norm_state["rs"]])
            ts.append(dve([t, norm_state["xn"]], lambda e: e.tensor_scalar(XN[:, half, :], src[:, half, :],
                                                                           rs[:, half:half + 1], None, ALU.mult)))
        norm_state["rs"] = ts[-1]
        r = turn(XN, gain, ts, banks)
        norm_state["xn"] = []
        return r

    def postnorm(gain, coef, waits):
        out_t = []
        for half in range(2):
            acc = ps[:, 2 * half:2 * half + 2, :].rearrange("p a b -> p (a b)")
            ta, t = rstd(half, acc, D, [waits[half], norm_state["rs"]])
            if coef != 1.0:
                t = dve([t], lambda e: e.tensor_scalar(rs[:, half:half + 1], rs[:, half:half + 1], coef, None,
                                                       ALU.mult))
            t = dve([ta, t, t_b], lambda e: e.scalar_tensor_tensor(out=acc, in0=acc, scalar=rs[:, half:half + 1],
                                                                   in1=GB[:, gi[gain], :], op0=ALU.mult,
                                                                   op1=ALU.mult))
            t = dve([t], lambda e: e.tensor_tensor(H[:, half, :], acc, H[:, half, :], ALU.add))
            bank[2 * half].free = [t]
            bank[2 * half + 1].free = [t]
            out_t.append(t)
        norm_state["rs"] = out_t[-1]
        return out_t

    b47 = Banks(bank[4:8])
    ball = Banks(bank)

    def cols(w, a, n):
        return w.rearrange("(c p) n -> p c n", p=P)[:, :, a:a + n]

    def product_T(w, col0, ntiles, rhs, waits, banks, evac, kt=8):
        per = min(2048 // (kt * 128), ntiles)
        for n0 in range(0, ntiles, per):
            s, v, tok = load(cols(w, col0 + n0 * 128, per * 128), kt, per * 128)
            k.wait("pe", [tok, waits])
            for q in range(0, per, 2):
                b = banks.take()
                k.wait("pe", [b.free])
                for r in range(2):
                    for c in range(kt):
                        ins = mm(b.ap[:, r * 256:r * 256 + 256], v[:, c, (q + r) * 128:(q + r + 1) * 128],
                                 rhs[:, c, :], c == 0, c == kt - 1)
                t = k.mark(k.sem["pe"], ins, 1)
                b.free = [evac(n0 + q, b.ap, t)]
            s.free = [t]

    def product_N(w, col0, ncols, lhs, waits, banks, evac):
        for n0 in range(0, ncols, 256):
            n = min(256, ncols - n0)
            s, v, tok = load(cols(w, col0 + n0, n), 8, n)
            b = banks.take()
            k.wait("pe", [tok, waits, b.free])
            for half in range(2):
                for c in range(8):
                    ins = mm(b.ap[:, half * n:half * n + n], lhs[:, c, half * 128:half * 128 + 128], v[:, c, :],
                             c == 0, c == 7)
            t = k.mark(k.sem["pe"], ins, 1)
            s.free = [t]
            b.free = [evac(n0, b.ap, t)]

    def product_acc(w, j0, n, total, lhs, waits):
        s, v, tok = load(w.rearrange("(j p) n -> p j n", p=P)[:, j0:j0 + n, :], n, D)
        k.wait("pe", [tok, waits] + ([bank[i].free for i in range(4)] if j0 == 0 else []))
        toks = []
        for half in range(2):
            for jj in range(n):
                for nb in range(2):
                    ins = mm(bank[2 * half + nb].ap, lhs[:, j0 + jj, half * 128:half * 128 + 128],
                             v[:, jj, nb * 512:nb * 512 + 512], j0 + jj == 0, j0 + jj == total - 1)
            toks.append(k.mark(k.sem["pe"], ins, 1))
        s.free = [toks[-1]]
        return toks

    def ffn(pre, wgu, wdown, post, waits):
        nt = prenorm(H, pre, waits, ball)
        aT = ar(0, FFN_TILES, 256)
        sg = [ar(5632 + 256 * i, 256) for i in range(4)]
        sgfree = [None] * 4
        last = None
        pend = None
        for i in range(FFN_TILES // 2):
            sg_, vg, tg = load(cols(wgu, i * 256, 256), 8, 256)
            su, vu, tu = load(cols(wgu, 2816 + i * 256, 256), 8, 256)
            for r in range(2):
                j = 2 * i + r
                b = b47.take()
                k.wait("pe", [tg, tu, nt, b.free])
                for q, v in enumerate((vg, vu)):
                    for c in range(8):
                        ins = mm(b.ap[:, q * 256:q * 256 + 256], v[:, c, r * 128:(r + 1) * 128], NT[:, c, :],
                                 c == 0, c == 7)
                t = k.mark(k.sem["pe"], ins, 1)
                x = sg[j % 4]
                t1 = act([t, sgfree[j % 4]], lambda e: e.activation(x, b.ap[:, 0:256], ACT.Silu))
                t2 = dve([t1], lambda e: e.tensor_tensor(aT[:, j, :], b.ap[:, 256:512], x, ALU.mult))
                sgfree[j % 4] = t2
                b.free = [t2]
            sg_.free = [t]
            su.free = [t]
            if pend is not None:
                product_acc(wdown, pend[0], 2, FFN_TILES, aT, [pend[1]])
            pend = (2 * i, t2)
        toks = product_acc(wdown, pend[0], 2, FFN_TILES, aT, [pend[1]])
        norm_state["nt"] = [toks[-1]]
        norm_state["xn"] = [toks[-1]]
        return postnorm(post, 0.5, toks)

    t_h = ffn("ffn1_pre_g", A["ffn1_w_gu"][0], A["ffn1_w_down"][0], "ffn1_post_g", [t_x])


    def softplus(dst, e, z, waits, efree):
        t = act([waits, efree], lambda g: g.activation(e, z, ACT.Abs))
        t = act([t], lambda g: g.activation(e, e, ACT.Exp, scale=-1.0))
        t = act([t], lambda g: g.activation(e, e, ACT.Ln, bias=1.0))
        return t, dve([t, waits], lambda g: g.scalar_tensor_tensor(out=dst, in0=z, scalar=0.0, in1=e, op0=ALU.max,
                                                                  op1=ALU.add))

    nt = prenorm(H, "mix_pre_g", t_h, ball)
    w_in = A["w_in"][0]
    qT, kT, catT = ar(0, 8, 256), ar(2048, 8, 256), ar(4096, 16, 256)
    Z = ar(8192, 2, D)
    xc = ar(10240, 12, 256)
    xn = ar(13312, 2, D)
    bn = ar(15360, 256)
    raw = [ar(15616 + 259 * i, 259) for i in range(4)]
    V = XN
    two = Banks([bank[4], bank[5]])
    tt = {}

    def ev_q(n, b, t):
        tt["q"] = act([t], lambda e: e.activation(qT[:, n:n + 2, :], b.rearrange("p (a b) -> p a b", a=2), ACT.Copy,
                                                  scale=0.125))
        return tt["q"]

    def ev_k(n, b, t):
        tt["k"] = dve([t], lambda e: e.tensor_copy(kT[:, n:n + 2, :], b.rearrange("p (a b) -> p a b", a=2)))
        return tt["k"]

    def ev_v(n, b, t):
        tt["v"] = dve([t], lambda e: e.tensor_copy(V[:, :, n:n + 256], b.rearrange("p (a b) -> p a b", a=2)))
        return tt["v"]

    product_T(w_in, 0, 8, NT, nt, ball, ev_q)
    product_T(w_in, 1024, 8, NT, nt, ball, ev_k)
    product_N(w_in, 2048, 1024, NT, nt, ball, ev_v)

    zb = Banks(bank[0:4])
    ee = [ar(16652 + 384 * i, 384) for i in range(2)]
    sp = [ar(17420 + 384 * i, 384) for i in range(2)]
    at_ = [ar(18188 + 384 * i, 384) for i in range(2)]
    sqb = [small[:, 256:512]]
    zbank, t_sp, t_a, pv_t = {}, {}, {}, {}
    sp_free, e_free, a_free = [None, None], [None, None], [None, None]
    sq_state = {"free": None, "pend": None}

    def diag(v, fill):
        return lambda g: g.affine_select(out=v, in_=v, compare_op=ALU.is_gt, fill=fill, base=0,
                                         pattern=[[0, 2], [1, P]], channel_multiplier=-1)

    def dview(x):
        return x.rearrange("p (a b) -> p a b", a=3)[:, 0:3:2, :]

    def at_scores(h):
        b = zb.take()
        zbank[h] = b
        o = 64 * (h % 2)
        k.wait("pe", [b.free, tt["q"], tt["k"]])
        mm(b.ap[:, 0:256], kT[o:o + 64, h // 2, 0:128], qT[o:o + 64, h // 2, :], True)
        t = pe([], lambda e: mm(b.ap[:, 256:384], kT[o:o + 64, h // 2, 128:256], qT[o:o + 64, h // 2, 128:256],
                                False))
        i = h % 2
        te, ts = softplus(sp[i], ee[i], b.ap[:, 0:384], [t, sp_free[i]], e_free[i])
        e_free[i] = ts
        t_sp[h] = pool([ts], diag(dview(sp[i]), 0.0))

    def at_logs(h):
        b, i = zbank[h], h % 2
        k.wait("pe", [t_sp[h], t_cst])
        mm(b.ap[:, 0:256], negtri, sp[i][:, 0:256], False)
        mm(b.ap[:, 128:256], negones, sp[i][:, 256:384], False)
        t = pe([], lambda e: mm(b.ap[:, 256:384], negtri, sp[i][:, 256:384], False))
        sp_free[i] = t
        t = act([t, a_free[i]], lambda e: e.activation(at_[i], b.ap[:, 0:384], ACT.Exp))
        b.free = [t]
        t_a[h] = pool([t], diag(dview(at_[i]), 0.0))


    def at_values(h):
        i, o = h % 2, 64 * (h % 2)
        b = bank[6]
        k.wait("pe", [t_a[h], tt["v"]] + ([b.free] if i == 0 else []))
        mm(b.ap[o:o + 64, 0:256], V[:, 0, 64 * h:64 * h + 64], at_[i][:, 0:256], True)
        t = pe([], lambda e: mm(b.ap[o:o + 64, 128:256], V[:, 1, 64 * h:64 * h + 64], at_[i][:, 256:384], False))
        a_free[i] = t
        if i:
            j = h // 2
            t1 = act([t], lambda e: e.activation(catT[:, j, :], b.ap[:, 0:256], ACT.Copy))
            t2 = act([sq_state["free"]], lambda e: e.activation(sqb[0], b.ap[:, 0:256], ACT.Square))
            b.free = [t2]
            sq_state["pend"] = (j, t2)

    def at_sum():
        if sq_state["pend"] is None:
            return
        j, t = sq_state["pend"]
        sq_state["pend"] = None
        k.wait("pe", [t, t_cst] + ([bank[7].free] if j == 0 else []))
        sq_state["free"] = pe([], lambda e: mm(bank[7].ap[:, 0:256], ones, sqb[0], j == 0, j == 7))

    step = [0]

    def attend():
        i = step[0]
        step[0] += 1
        at_sum()
        for h in (2 * i - 4, 2 * i - 3):
            if 0 <= h < 16:
                at_values(h)
        for h in (2 * i - 2, 2 * i - 1):
            if 0 <= h < 16:
                at_logs(h)
        for h in (2 * i, 2 * i + 1):
            if h < 16:
                at_scores(h)

    def ev_z(n, b, t):
        r = act([t], lambda e: e.activation(Z[:, :, n:n + 256], b.rearrange("p (a b) -> p a b", a=2), ACT.Silu))
        attend()
        tt["z"] = r
        return r

    t_pad = pool([t_pg], lambda e: e.memset(ar(15616, 4, 259)[:, :, 0:3], 0.0))
    raw_free = [None] * 4
    t_xc = {}

    def ev_x(n, b, t):
        for r in range(2):
            c = n + r
            x = raw[c % 4]
            t1 = act([t, raw_free[c % 4], t_pad], lambda e: e.activation(x[:, 3:259], b[:, r * 256:r * 256 + 256],
                                                                         ACT.Copy))
            u = dve([t1], lambda e: e.tensor_scalar(xc[:, c, :], x[:, 0:256], pg("conv_w0", c), None, ALU.mult))
            for q in (1, 2, 3):
                u = dve([u], lambda e: e.scalar_tensor_tensor(out=xc[:, c, :], in0=x[:, q:q + 256],
                                                              scalar=pg("conv_w%d" % q, c), in1=xc[:, c, :],
                                                              op0=ALU.mult, op1=ALU.add))
            raw_free[c % 4] = u
            t_xc[c] = act([u], lambda e: e.activation(xc[:, c, :], xc[:, c, :], ACT.Silu, bias=pg("conv_b", c)))
        attend()
        return t1

    product_N(w_in, 3072, 1024, NT, nt, two, ev_z)
    product_T(w_in, 4096, 12, NT, nt, two, ev_x)

    dt, adt, na = sm(32).rearrange("p (c h) -> p c h", c=2), sm(32).rearrange("p (c h) -> p c h", c=2), sm(16)
    dtmp = sm(32).rearrange("p (c h) -> p c h", c=2)
    wdec, eacs = sm(16), sm(16)

    def ev_dt(n, b, t):
        v = b[:, 0:32].rearrange("p (c h) -> p c h", c=2)
        t1 = dve([t, t_b], lambda e: e.tensor_tensor(dt, v, dtb.unsqueeze(1).broadcast_to([P, 2, 16]), ALU.add))
        ta = act([t_b], lambda e: e.activation(na, alog, ACT.Exp))
        _, t2 = softplus(adt, dtmp, dt, [t1], None)
        t3 = dve([t2], lambda e: e.tensor_copy(dt, adt))
        t3 = dve([t3, ta], lambda e: e.scalar_tensor_tensor(out=adt, in0=dt, scalar=-1.0,
                                                            in1=na.unsqueeze(1).broadcast_to([P, 2, 16]),
                                                            op0=ALU.mult, op1=ALU.mult))
        tt["dt"] = t3
        return t1

    product_N(w_in, 5632, 16, NT, nt, two, ev_dt)
    while step[0] < 11:
        attend()

    rbc = sqb[0]
    t = dve([sq_state["free"]], lambda e: e.tensor_scalar(rbc, bank[7].ap[:, 0:256], 1.0 / D, EPS, ALU.mult, ALU.add))
    bank[7].free = [t]
    t = act([t], lambda e: e.activation(rbc, rbc, ACT.Sqrt))
    t = dve([t], lambda e: e.reciprocal(rbc, rbc))
    for j in range(8):
        t_cat = dve([t], lambda e: e.scalar_tensor_tensor(out=catT[:, j, :], in0=catT[:, j, :],
                                                          scalar=pg("attn_norm_g", j), in1=rbc, op0=ALU.mult,
                                                          op1=ALU.mult))
    t_catA = t_cat

    for c in range(0, 8, 2):
        b = b47.take()
        k.wait("pe", [b.free, t_xc[c + 1]])
        for half in range(2):
            for r in range(2):
                ins = nc.tensor.transpose(b.ap[:, half * 256 + r * 128:half * 256 + r * 128 + 128],
                                          xc[:, c + r, half * 128:half * 128 + 128], ident)
        t = k.mark(k.sem["pe"], ins, 1)
        t_xn = act([t], lambda e: e.activation(xn[:, :, c * 128:c * 128 + 256],
                                               b.ap.rearrange("p (a b) -> p a b", a=2), ACT.Copy))
        b.free = [t_xn]
    b = b47.take()
    k.wait("pe", [b.free, t_xc[11]])
    for g in range(2):
        ins = nc.tensor.transpose(b.ap[:, g * 128:g * 128 + 128], xc[:, 8 + g, 0:128], ident)
    t = k.mark(k.sem["pe"], ins, 1)
    t_bn = act([t], lambda e: e.activation(bn, b.ap[:, 0:256], ACT.Copy))
    b.free = [t_bn]

    b = b47.take()
    k.wait("pe", [b.free, tt["dt"]])
    mm(b.ap[:, 0:16], tri_le, adt[:, 1, :], True)
    t = pe([], lambda e: mm(b.ap[:, 16:32], tri_gt, adt[:, 0, :], False))
    act([t], lambda e: e.activation(eacs, b.ap[:, 0:16], ACT.Exp))
    t = act([], lambda e: e.activation(wdec, b.ap[:, 16:32], ACT.Exp))
    b.free = [t]
    t_w = dve([t], lambda e: e.tensor_tensor(wdec, wdec, dt[:, 0, :], ALU.mult))

    cb = ar(17676, 4, P)
    b = b47.take()
    k.wait("pe", [b.free, t_sp[15]])
    for c in range(2):
        for g in range(2):
            ins = mm(b.ap[:, (2 * c + g) * 128:(2 * c + g) * 128 + 128], xc[:, 8 + g, c * 128:c * 128 + 128],
                     xc[:, 10 + g, c * 128:c * 128 + 128], True)
    t = k.mark(k.sem["pe"], ins, 1)
    t_cb = dve([t], lambda e: e.tensor_tensor(cb, b.ap.rearrange("p (a b) -> p a b", a=4),
                                              tri_le.unsqueeze(1).broadcast_to([P, 4, P]), ALU.mult))
    b.free = [t_cb]

    xw = ar(0, D)
    st = ar(1024, D)
    t_xw = pool([t_w, t_xn], lambda e: e.tensor_tensor(xw.rearrange("p (h d) -> p h d", h=16),
                                                       xn[:, 0, :].rearrange("p (h d) -> p h d", h=16),
                                                       wdec.unsqueeze(2).broadcast_to([P, 16, 64]), ALU.mult))
    Y = XN
    t_y = {}
    for c in range(2):
        t_y[c] = pool([], lambda e: e.tensor_tensor(Y[:, c, :].rearrange("p (h d) -> p h d", h=16),
                                                    xn[:, c, :].rearrange("p (h d) -> p h d", h=16),
                                                    dsk.unsqueeze(2).broadcast_to([P, 16, 64]), ALU.mult))
    for g in range(2):
        b = b47.take()
        k.wait("pe", [b.free, t_xw, t_bn])
        t = pe([], lambda e: mm(b.ap, bn[:, g * 128:g * 128 + 128], xw[:, g * 512:g * 512 + 512], True))
        t_st = act([t], lambda e: e.activation(st[:, g * 512:g * 512 + 512], b.ap, ACT.Copy))
        b.free = [t_st]

    w_out = A["w_out"][0]
    Mb = [ar(2048 + 512 * i, 4, P) for i in range(2)]
    Lb = [ar(3072 + 512 * i, 4, P) for i in range(2)]
    Gb = [ar(16652 + 512 * i, 4, P) for i in range(2)]
    tmp = ar(18188, 512)
    m_free, l_free, g_free = [None] * 2, [None] * 2, [None] * 2
    n = 0
    tmp_free = None
    yb = Banks([bank[6], bank[7]])
    ss2, ms2, rs2 = sm(4), sm(4), sm(4)
    t_catB = []
    for c in range(2):
        for g in range(2):
            y = yb.take()
            for hq in range(2):
                i = n % 2
                n += 1
                h0 = 8 * g + 4 * hq
                for r in range(4):
                    t = dve([tt["dt"], m_free[i]], lambda e: e.tensor_scalar(Mb[i][:, r, :], tri_gt,
                                                                             adt[:, c, h0 + r:h0 + r + 1], None,
                                                                             ALU.mult))
                b = two.take()
                k.wait("pe", [t, b.free])
                for r in range(4):
                    ins = mm(b.ap[:, r * 128:r * 128 + 128], Mb[i][:, r, :], tri_le, True)
                t = m_free[i] = k.mark(k.sem["pe"], ins, 1)
                t = act([t, l_free[i]], lambda e: e.activation(Lb[i], b.ap.rearrange("p (a b) -> p a b", a=4),
                                                               ACT.Exp))
                b.free = [t]
                for r in range(4):
                    t1 = dve([t, t_cb, g_free[i]], lambda e: e.scalar_tensor_tensor(
                        out=Gb[i][:, r, :], in0=Lb[i][:, r, :], scalar=dt[:, c, h0 + r:h0 + r + 1],
                        in1=cb[:, 2 * c + g, :], op0=ALU.mult, op1=ALU.mult))
                l_free[i] = t1
                k.wait("pe", [t1, t_xn] + ([y.free] if hq == 0 else []))
                for r in range(4):
                    h = h0 + r
                    ins = mm(y.ap[:, (h % 8) * 64:(h % 8) * 64 + 64], Gb[i][:, r, :], xn[:, c, h * 64:h * 64 + 64],
                             True)
                g_free[i] = t = k.mark(k.sem["pe"], ins, 1)
            Yv = Y[:, c, g * 512:g * 512 + 512]
            u = dve([t, t_y[c]], lambda e: e.tensor_tensor(Yv, y.ap, Yv, ALU.add))
            y.free = [u]
            if c == 1:
                b = two.take()
                k.wait("pe", [b.free, t_st])
                t = pe([], lambda e: mm(b.ap, xc[:, 10 + g, 128:256], st[:, g * 512:g * 512 + 512], True))
                t = dve([t, tmp_free], lambda e: e.tensor_tensor(
                    tmp.rearrange("p (h d) -> p h d", h=8), b.ap.rearrange("p (h d) -> p h d", h=8),
                    eacs[:, g * 8:g * 8 + 8].unsqueeze(2).broadcast_to([P, 8, 64]), ALU.mult))
                b.free = [t]
                tmp_free = u = dve([t, u], lambda e: e.tensor_tensor(Yv, Yv, tmp, ALU.add))
            u = dve([u, tt["z"]], lambda e: e.tensor_tensor(Yv, Yv, Z[:, c, g * 512:g * 512 + 512], ALU.mult))
            i = 2 * c + g
            u = act([u, norm_state["ja"]], lambda e: e.activation(JA[:, 0:512], Yv, ACT.Square,
                                                                  accum_out=ss2[:, i:i + 1]))
            norm_state["ja"] = u
            u = dve([u], lambda e: e.tensor_scalar(ms2[:, i:i + 1], ss2[:, i:i + 1], 1.0 / 512, EPS, ALU.mult,
                                                   ALU.add))
            u = pool([u], lambda e: e.tensor_tensor(rs2[:, i:i + 1], ms2[:, i:i + 1], half_c[:, 0:1], ALU.pow))
            u = dve([u], lambda e: e.tensor_scalar(Yv, Yv, rs2[:, i:i + 1], None, ALU.mult))
            b = two.take()
            k.wait("pe", [b.free, u])
            for r in range(4):
                ins = nc.tensor.transpose(b.ap[:, r * 128:r * 128 + 128], Yv[:, r * 128:r * 128 + 128], ident)
            t = k.mark(k.sem["pe"], ins, 1)
            for r in range(4):
                j = 4 * g + r
                u = act([t], lambda e: e.activation(catT[:, 8 + j, c * 128:c * 128 + 128],
                                                    b.ap[:, r * 128:r * 128 + 128], ACT.Copy,
                                                    scale=pg("ssd_norm_g", j)))
            b.free = [u]
            t_catB.append(u)
            product_acc(w_out, 2 * i, 2, 16, catT, [t_catA])
    def softmax_rows(S, n_heads, width, scratch, waits, sinks=None):
        mx, sm_, rc, es, _ = scratch
        t = dve([waits], lambda e: e.tensor_reduce(mx, S, AX.X, ALU.max))
        if sinks is not None:
            t = dve([t], lambda e: e.tensor_tensor(mx, mx, sinks, ALU.max))
            t = dve([t], lambda e: e.tensor_tensor(es, sinks, mx, ALU.subtract))
            t_es = act([t], lambda e: e.activation(es, es, ACT.Exp))
        t = dve([t], lambda e: e.tensor_scalar(mx, mx, -1.0, None, ALU.mult))
        for h in range(n_heads):
            te = act([t], lambda e: e.activation(S[:, h, :], S[:, h, :], ACT.Exp, bias=mx[:, h:h + 1],
                                                 accum_out=sm_[:, h:h + 1]))
        if sinks is not None:
            te = dve([te, t_es], lambda e: e.tensor_tensor(sm_, sm_, es, ALU.add))
        t = dve([te], lambda e: e.reciprocal(rc, sm_))
        for h in range(n_heads):
            u = dve([t, te], lambda e: e.tensor_scalar(S[:, h, :], S[:, h, :], rc[:, h:h + 1], None, ALU.mult))
        return u

    M0 = ar(10240, 2, D)
    MT = ar(12288, 8, 256)
    kTm = ar(0, 8, 256)
    Vm = ar(8192, 2, D)
    qTm = ar(2048, 8, 256)
    Sx = [ar(4096 + 1024 * i, 4, 256) for i in range(2)]
    pT = ar(6144, 8, 256)
    oT = ar(14336, 8, 256)

    def ev_copy(dst, eng, scale=None):
        def f(n, b, t):
            v = b.rearrange("p (a b) -> p a b", a=2)
            if eng == "act":
                tt["cp"] = act([t], lambda e: e.activation(dst[:, n:n + 2, :], v, ACT.Copy, scale=scale or 1.0))
            else:
                tt["cp"] = dve([t], lambda e: e.tensor_copy(dst[:, n:n + 2, :], v))
            return tt["cp"]
        return f

    def ev_nat(dst, key, eng):
        def f(n, b, t):
            v = b.rearrange("p (a b) -> p a b", a=2)
            if eng == "act":
                tt[key] = act([t], lambda e: e.activation(dst[:, :, n:n + 256], v, ACT.Copy))
            else:
                tt[key] = dve([t], lambda e: e.tensor_copy(dst[:, :, n:n + 256], v))
            return tt[key]
        return f

    s_m = k.semaphore("s_m")
    t_m = k.dma("sp", s_m, [t_catB[-1]], M0, A["mem"][0].rearrange("(h p) d -> p h d", p=P))
    ssm, msm, rsm = sm(2), sm(2), sm(2)
    for half in range(2):
        u = act([t_m, norm_state["ja"]], lambda e: e.activation(JA[:, :], M0[:, half, :], ACT.Square,
                                                                accum_out=ssm[:, half:half + 1]))
        norm_state["ja"] = u
        u = dve([u], lambda e: e.tensor_scalar(msm[:, half:half + 1], ssm[:, half:half + 1], 1.0 / D, EPS, ALU.mult,
                                               ALU.add))
        u = pool([u], lambda e: e.tensor_tensor(rsm[:, half:half + 1], msm[:, half:half + 1], half_c[:, 0:1],
                                                ALU.pow))
        t_mn = dve([u], lambda e: e.tensor_scalar(M0[:, half, :], M0[:, half, :], rsm[:, half:half + 1], None,
                                                  ALU.mult))
    t_mt = turn(M0, "mem_g", [t_mn], b47, MT)
    for j in range(8, 16, 2):
        toks = product_acc(w_out, j, 2, 16, catT, [t_catB[-1]])
    t_h = postnorm("mix_post_g", 1.0, toks)
    product_T(A["xa_wkv"][0], 0, 8, MT, t_mt, b47, ev_copy(kTm, "act"))
    t_kTm = tt["cp"]
    product_N(A["xa_wkv"][0], 1024, 1024, MT, t_mt, b47, ev_nat(Vm, "vm", "act"))
    nt = prenorm(H, "xa_pre_g", t_h, b47)
    product_T(A["xa_wq"][0], 0, 8, NT, nt, ball, ev_copy(qTm, "act", 0.0625))
    t_q = tt["cp"]
    scr = [[sm(8) for _ in range(5)] for _ in range(2)]
    tp = []
    for half in range(2):
        for hp in range(2):
            b = ball.take()
            k.wait("pe", [b.free, t_q, t_kTm])
            for r in range(2):
                h = 2 * hp + r
                for dt_ in range(2):
                    ins = mm(b.ap[:, r * 256:r * 256 + 256], qTm[:, 2 * h + dt_, half * 128:half * 128 + 128],
                             kTm[:, 2 * h + dt_, :], dt_ == 0, dt_ == 1)
            t = k.mark(k.sem["pe"], ins, 1)
            t = dve([t], lambda e: e.tensor_copy(Sx[half][:, 2 * hp:2 * hp + 2, :],
                                                 b.ap.rearrange("p (a b) -> p a b", a=2)))
            b.free = [t]
        tp.append(softmax_rows(Sx[half], 4, 256, [x[:, 0:4] for x in scr[half]], [t]))
    for h in range(4):
        b = ball.take()
        k.wait("pe", [b.free, tp])
        for mt in range(2):
            for half in range(2):
                ins = nc.tensor.transpose(b.ap[:, mt * 256 + half * 128:mt * 256 + half * 128 + 128],
                                          Sx[half][:, h, mt * 128:mt * 128 + 128], ident)
        t = k.mark(k.sem["pe"], ins, 1)
        if h % 2:
            t = act([t], lambda e: e.activation(pT[:, 2 * h:2 * h + 2, :], b.ap.rearrange("p (a b) -> p a b", a=2),
                                                ACT.Copy))
        else:
            t = dve([t], lambda e: e.tensor_copy(pT[:, 2 * h:2 * h + 2, :],
                                                 b.ap.rearrange("p (a b) -> p a b", a=2)))
        b.free = [t]
        b = ball.take()
        k.wait("pe", [b.free, t, tt["vm"]])
        for dt_ in range(2):
            for mt in range(2):
                ins = mm(b.ap[:, dt_ * 256:dt_ * 256 + 256],
                         Vm[:, mt, h * 256 + dt_ * 128:h * 256 + dt_ * 128 + 128], pT[:, 2 * h + mt, :],
                         mt == 0, mt == 1)
        t = k.mark(k.sem["pe"], ins, 1)
        t_o = act([t], lambda e: e.activation(oT[:, 2 * h:2 * h + 2, :], b.ap.rearrange("p (a b) -> p a b", a=2),
                                              ACT.Copy))
        b.free = [t_o]
    for j in range(0, 8, 2):
        toks = product_acc(A["xa_wo"][0], j, 2, 8, oT, [t_o])
    t_h = postnorm("xa_post_g", 1.0, toks)
    bias = ar(10752, 8, 256)
    di = AR[:, 18944:19200].bitcast(mybir.dt.int32)
    df, ng = ar(15872, 256), ar(16128, 256)
    t = pool([t_h], lambda e: e.iota(di, pattern=[[-1, 256]], base=128, channel_multiplier=1))
    t = pool([t], lambda e: e.tensor_copy(df, di))
    t = pool([t], lambda e: e.memset(ng, 0.0))
    t = pool([t], sel(ng, 128, [[-1, 256]], 1, ALU.is_ge, -1e30))
    t = pool([t], sel(ng, 0, [[1, 256]], -1, ALU.is_gt, -1e30))
    for h in range(8):
        t_bias = dve([t], lambda e: e.scalar_tensor_tensor(out=bias[:, h, :], in0=df, scalar=-(2.0 ** -(h + 1)),
                                                           in1=ng, op0=ALU.mult, op1=ALU.add))
    t_h = ffn("ffn2_pre_g", A["ffn2_w_gu"][0], A["ffn2_w_down"][0], "ffn2_post_g", t_h)

    nt = prenorm(H, "norm_mix_g_2", t_h, ball)
    w2 = A["w_in_2"][0]
    aq, ak, av = ar(0, 4, 256), ar(1024, 256), ar(1280, 2, 128)
    hq, kn, lf, hv, hg = ar(1536, 4, 256), ar(2560, 2, 512), ar(3584, 2, 512), ar(4608, 2, 512), ar(5632, 4, 256)
    eb, kinv, kd, aT = ar(6656, 4, 256), ar(7680, 4, 256), ar(8704, 2, 512), ar(9728, 2, 4, P)
    ga, gh = ar(10752, 8, 256), ar(12800, 8, 256)
    ST = ar(14848, 7, 4, P)
    S0, S1 = ar(12800, 8, 128), ar(13824, 8, 256)
    pT2 = ar(15872, 8, 3, P)
    ya, yh = XN[:, 0, :].rearrange("p (a b) -> p a b", a=4), XN[:, 1, :].rearrange("p (a b) -> p a b", a=4)

    s, v, tok = load(w2.rearrange("(c p) n -> p c n", p=P)[:, :, 0:256], 8, 256)
    s2, v2, tok2 = load(w2.rearrange("(c p) n -> p c n", p=P)[:, :, 256:512], 8, 256)
    for jp in range(2):
        b = ball.take()
        k.wait("pe", [b.free, nt, tok, tok2])
        for r in range(2):
            j = 2 * jp + r
            for q, vv in enumerate((v, v2)):
                for c in range(8):
                    ins = mm(b.ap[64 * q:64 * q + 64, r * 256:r * 256 + 256], vv[:, c, 64 * j:64 * j + 64],
                             NT[:, c, :], c == 0, c == 7)
        t = k.mark(k.sem["pe"], ins, 1)
        t_aq = act([t], lambda e: e.activation(aq[:, 2 * jp:2 * jp + 2, :],
                                               b.ap.rearrange("p (a b) -> p a b", a=2), ACT.Copy, scale=0.125))
        b.free = [t_aq]
    s.free = [t]
    s2.free = [t]
    s, v, tok = load(cols(w2, 512, 256), 8, 256)
    b = ball.take()
    k.wait("pe", [b.free, tok])
    for c in range(8):
        mm(b.ap[:, 0:256], v[:, c, 0:128], NT[:, c, :], c == 0, c == 7)
    for half in range(2):
        for c in range(8):
            ins = mm(b.ap[:, 256 + half * 128:384 + half * 128], NT[:, c, half * 128:half * 128 + 128],
                     v[:, c, 128:256], c == 0, c == 7)
    t = k.mark(k.sem["pe"], ins, 1)
    s.free = [t]
    act([t], lambda e: e.activation(ak, b.ap[:, 0:256], ACT.Copy))
    t_av = act([], lambda e: e.activation(av, b.ap[:, 256:512].rearrange("p (a b) -> p a b", a=2), ACT.Copy))
    b.free = [t_av]

    t_s = [None, None]
    for h in range(8):
        o, j = 64 * (h // 4), h % 4
        b = ball.take()
        k.wait("pe", [b.free, t_aq, t_av])
        mm(b.ap[:, 0:128], aq[o:o + 64, j, 0:128], ak[o:o + 64, 0:128], True)
        t = pe([], lambda e: mm(b.ap[:, 128:384], aq[o:o + 64, j, 128:256], ak[o:o + 64, 0:256], False))
        t_s[0] = dve([t, t_bias], lambda e: e.tensor_tensor(S0[:, h, :], b.ap[:, 0:128], bias[:, h, 128:256], ALU.add))
        t_s[1] = dve([], lambda e: e.tensor_tensor(S1[:, h, :], b.ap[:, 128:384], bias[:, h, :], ALU.add))
        b.free = [t_s[1]]

    def ev_f(n, b, t):
        v = b.rearrange("p (a b) -> p a b", a=2)
        lb = LB[:, 0, n:n + 256].unsqueeze(1).broadcast_to([P, 2, 256])
        om = LB[:, 1, n:n + 256].unsqueeze(1).broadcast_to([P, 2, 256])
        kk, ll = kn[:, :, n:n + 256], lf[:, :, n:n + 256]
        r = act([t], lambda e: e.activation(kk, v, ACT.Sigmoid))
        t = dve([r, t_lb], lambda e: e.tensor_tensor(kk, kk, om, ALU.mult))
        t = dve([t], lambda e: e.tensor_tensor(ll, kk, lb, ALU.add))
        tt["kn"] = dve([t], lambda e: e.tensor_scalar(kk, ll, -1.0, 1.0, ALU.mult, ALU.add))
        tt["lf"] = act([tt["kn"]], lambda e: e.activation(ll, ll, ACT.Ln))
        return r

    product_N(w2, 1280, 512, NT, nt, ball, ev_f)
    product_N(w2, 1792, 512, NT, nt, ball, ev_nat(hv, "hv", "act"))

    def ev_silu(dst, key, func):
        def f(n, b, t):
            tt[key] = act([t, tt.get("over")], lambda e: e.activation(dst[:, n:n + 2, :],
                                                                      b.rearrange("p (a b) -> p a b", a=2), func))
            return tt[key]
        return f

    t_p = [softmax_rows(S0, 8, 128, scr[0], [t_s[0]], sink), softmax_rows(S1, 8, 256, scr[1], [t_s[1]], sink)]
    product_T(w2, 768, 4, NT, nt, ball, ev_silu(hq, "hq", ACT.Silu))
    product_T(w2, 2304, 4, NT, nt, ball, ev_silu(hg, "hg", ACT.Silu))

    for h in range(8):
        b = ball.take()
        k.wait("pe", [b.free, t_p])
        nc.tensor.transpose(b.ap[:, 0:128], S1[:, h, 0:128], ident)
        nc.tensor.transpose(b.ap[:, 128:256], S1[:, h, 128:256], ident)
        t = pe([], lambda e: e.transpose(b.ap[:, 256:384], S0[:, h, :], ident))
        v = b.ap[:, 0:384].rearrange("p (a b) -> p a b", a=3)
        if h % 2:
            t_pt = act([t], lambda e: e.activation(pT2[:, h, :, :], v, ACT.Copy))
            t_pa = t_pt
        else:
            t_pt = dve([t], lambda e: e.tensor_copy(pT2[:, h, :, :], v))
            t_pd = t_pt
        b.free = [t_pt]
    for jp in range(2):
        b = ball.take()
        k.wait("pe", [b.free, t_pa, t_pd])
        for r in range(2):
            for q in range(2):
                h = 2 * (2 * jp + r) + q
                o, g = 64 * q, h // 4
                c0 = r * 256
                mm(b.ap[o:o + 64, c0:c0 + 128], av[:, 0, g * 64:g * 64 + 64], pT2[:, h, 2, :], r == 0)
                mm(b.ap[o:o + 64, c0 + 128:c0 + 256], av[:, 0, g * 64:g * 64 + 64], pT2[:, h, 0, :], False)
                ins = mm(b.ap[o:o + 64, c0 + 128:c0 + 256], av[:, 1, g * 64:g * 64 + 64], pT2[:, h, 1, :], False)
        t = k.mark(k.sem["pe"], ins, 1)
        t_ya = act([t], lambda e: e.activation(ya[:, 2 * jp:2 * jp + 2, :],
                                               b.ap.rearrange("p (a b) -> p a b", a=2), ACT.Copy))
        b.free = [t_ya]
    tt["over"] = t_ya

    t_z = pool([], lambda e: e.memset(aT, 0.0))
    for jp in range(2):
        b = ball.take()
        k.wait("pe", [b.free, tt["lf"], t_cst])
        for r in range(2):
            h = 2 * jp + r
            for half in range(2):
                ins = mm(b.ap[:, r * 256 + half * 128:r * 256 + half * 128 + 128],
                         lf[:, half, h * 128:h * 128 + 128], bt_le, True)
        t = k.mark(k.sem["pe"], ins, 1)
        v = b.ap.rearrange("p (a b) -> p a b", a=2)
        act([t], lambda e: e.activation(eb[:, 2 * jp:2 * jp + 2, :], v, ACT.Exp))
        t_eb = act([], lambda e: e.activation(kinv[:, 2 * jp:2 * jp + 2, :], v, ACT.Exp, scale=-1.0))
        b.free = [t_eb]
        b = ball.take()
        k.wait("pe", [b.free, tt["kn"]])
        for r in range(2):
            h = 2 * jp + r
            for half in range(2):
                ins = nc.tensor.transpose(b.ap[:, r * 256 + half * 128:r * 256 + half * 128 + 128],
                                          kn[:, half, h * 128:h * 128 + 128], ident)
        t = k.mark(k.sem["pe"], ins, 1)
        v2 = b.ap.rearrange("p (a b) -> p a b", a=2)
        t_ki = dve([t, t_eb], lambda e: e.tensor_tensor(kinv[:, 2 * jp:2 * jp + 2, :], v2,
                                                        kinv[:, 2 * jp:2 * jp + 2, :], ALU.mult))
        b.free = [t_ki]
        t_qd = pool([t_eb, tt["hq"]], lambda e: e.tensor_tensor(hq[:, 2 * jp:2 * jp + 2, :],
                                                                hq[:, 2 * jp:2 * jp + 2, :],
                                                                eb[:, 2 * jp:2 * jp + 2, :], ALU.mult))
    for half in range(2):
        b = ball.take()
        k.wait("pe", [b.free])
        t = pe([], lambda e: mm(b.ap, bt_gt, lf[:, half, :], True))
        t = act([t], lambda e: e.activation(kd[:, half, :], b.ap, ACT.Exp))
        b.free = [t]
        t_kd = pool([t, tt["kn"]], lambda e: e.tensor_tensor(kd[:, half, :], kd[:, half, :], kn[:, half, :],
                                                             ALU.mult))
    product_T(w2, 2816, 8, NT, nt, b47, ev_silu(ga, "ga", ACT.Sigmoid))
    for half in range(2):
        b = b47.take()
        k.wait("pe", [b.free, t_ki, t_qd])
        for h in range(4):
            ins = mm(b.ap[:, h * 128:h * 128 + 128], kinv[:, h, half * 128:half * 128 + 128],
                     hq[:, h, half * 128:half * 128 + 128], True)
        t = k.mark(k.sem["pe"], ins, 1)
        m = bt_le.bitcast(U32).unsqueeze(1).broadcast_to([P, 4, P])
        t_aT = dve([t, t_z, t_cst], lambda e: e.copy_predicated(aT[:, half, :, :], m,
                                                                b.ap.rearrange("p (a b) -> p a b", a=4)))
        b.free = [t_aT]
    t_st2 = {}
    for c in range(7):
        b = bank[c % 4]
        half, r = c // 4, 32 * (c % 4)
        k.wait("pe", [b.free, t_kd, tt["hv"]])
        for h in range(4):
            ins = mm(b.ap[:, h * 128:h * 128 + 128], kd[r:r + 32, half, h * 128:h * 128 + 128],
                     hv[r:r + 32, half, h * 128:h * 128 + 128], True)
        t = k.mark(k.sem["pe"], ins, 1)
        if c == 0:
            u = dve([t, t_ya], lambda e: e.tensor_copy(ST[:, 0, :, :], b.ap.rearrange("p (a b) -> p a b", a=4)))
        else:
            w = [t, t_st2[c - 1]]
            for h in range(4):
                u = dve(w, lambda e: e.scalar_tensor_tensor(
                    out=ST[:, c, h, :], in0=ST[:, c - 1, h, :], scalar=eb[:, h, 32 * c + 31:32 * c + 32],
                    in1=b.ap[:, h * 128:h * 128 + 128], op0=ALU.mult, op1=ALU.add))
        t_st2[c] = u
        b.free = [u]
    product_T(w2, 3840, 8, NT, nt, b47, ev_silu(gh, "gh", ACT.Sigmoid))
    for jp in range(2):
        b = bank[2 * jp]
        k.wait("pe", [b.free, t_aT, t_st2[6]])
        for r in range(2):
            h = 2 * jp + r
            for half in range(2):
                mm(b.ap[:, r * 256 + half * 128:r * 256 + half * 128 + 128], hv[:, half, h * 128:h * 128 + 128],
                   aT[:, half, h, :], r == 0 and half == 0)
            for c in range(1, 8):
                ins = mm(b.ap[:, r * 256 + 32 * c:r * 256 + 32 * c + 32], ST[:, c - 1, h, :],
                         hq[:, h, 32 * c:32 * c + 32], False)
        t = k.mark(k.sem["pe"], ins, 1)
        u = act([t, norm_state["ja"]], lambda e: e.activation(JA[:, 0:512], b.ap, ACT.Square))
        norm_state["ja"] = u
        b2 = bank[2 * jp + 1]
        k.wait("pe", [b2.free, u])
        t = pe([], lambda e: mm(b2.ap, ones, JA[:, 0:512], True))
        rb = kinv[:, 2 * jp:2 * jp + 2, :]
        t = dve([t, t_aT], lambda e: e.tensor_scalar(rb, b2.ap.rearrange("p (a b) -> p a b", a=2), 1.0 / 128, EPS,
                                                     ALU.mult, ALU.add))
        b2.free = [t]
        t = act([t], lambda e: e.activation(rb, rb, ACT.Sqrt))
        t = dve([t], lambda e: e.reciprocal(rb, rb))
        t = dve([t, u], lambda e: e.scalar_tensor_tensor(out=rb, in0=b.ap.rearrange("p (a b) -> p a b", a=2),
                                                         scalar=pg("hgrn_norm_g_2", 0), in1=rb, op0=ALU.mult,
                                                         op1=ALU.mult))
        b.free = [t]
        norm_state["ja"] = [u, t]
        t_yh = dve([t, tt["hg"]], lambda e: e.tensor_tensor(yh[:, 2 * jp:2 * jp + 2, :], rb,
                                                            hg[:, 2 * jp:2 * jp + 2, :], ALU.mult))
    for n0 in range(0, 8, 4):
        sa_, va, ta = load(A["w_attn_proj_2"][0].rearrange("(c p) n -> p c n", p=P)[:, :, n0 * 128:n0 * 128 + 512],
                           4, 512)
        sh_, vh, th = load(A["w_hgrn_proj_2"][0].rearrange("(c p) n -> p c n", p=P)[:, :, n0 * 128:n0 * 128 + 512],
                           4, 512)
        for r in range(4):
            n = n0 + r
            b = b47.take()
            k.wait("pe", [b.free, ta, t_ya])
            for c in range(4):
                mm(b.ap[:, 0:256], va[:, c, r * 128:r * 128 + 128], ya[:, c, :], c == 0, c == 3)
            k.wait("pe", [th, t_yh])
            for c in range(4):
                ins = mm(b.ap[:, 256:512], vh[:, c, r * 128:r * 128 + 128], yh[:, c, :], c == 0, c == 3)
            t = k.mark(k.sem["pe"], ins, 1)
            dve([t, tt["ga"], tt["gh"]], lambda e: e.tensor_tensor(b.ap[:, 0:256], b.ap[:, 0:256], ga[:, n, :],
                                                                   ALU.mult))
            u = dve([], lambda e: e.tensor_tensor(NT[:, n, :], b.ap[:, 256:512], gh[:, n, :], ALU.mult))
            t_m = dve([u], lambda e: e.tensor_tensor(NT[:, n, :], b.ap[:, 0:256], NT[:, n, :], ALU.add))
            b.free = [t_m]
        sa_.free = [t]
        sh_.free = [t]
    for j in range(0, 8, 2):
        toks = product_acc(A["w_out_2"][0], j, 2, 8, NT, [t_m])
    t_h = []
    for half in range(2):
        acc = ps[:, 2 * half:2 * half + 2, :].rearrange("p a b -> p (a b)")
        t = dve([toks[half]], lambda e: e.tensor_tensor(H[:, half, :], acc, H[:, half, :], ALU.add))
        bank[2 * half].free = [t]
        bank[2 * half + 1].free = [t]
        t_h.append(t)

    keysT, qp = ar(0, 16, P), ar(2048, 16, 256)
    SC = [ar(6144 + 2048 * i, 16, P) for i in range(2)]
    s, v, tok = load(A["peer_keys_2"][0].rearrange("a h n d -> n (a h) d"), 16, 128)
    for q in range(4):
        b = b47.take()
        k.wait("pe", [b.free, tok, t_h])
        for r in range(4):
            ins = nc.tensor.transpose(b.ap[:, r * 128:r * 128 + 128], v[:, 4 * q + r, :], ident)
        t = k.mark(k.sem["pe"], ins, 1)
        t_keys = act([t], lambda e: e.activation(keysT[:, 4 * q:4 * q + 4, :],
                                                 b.ap.rearrange("p (a b) -> p a b", a=4), ACT.Copy))
        b.free = [t_keys]
    s.free = [t]
    ts = []
    for half in range(2):
        _, t = rstd(half, H[:, half, :], D, [t_h, norm_state["rs"]])
        ts.append(dve([t, t_b], lambda e: e.scalar_tensor_tensor(out=XN[:, half, :], in0=H[:, half, :],
                                                                 scalar=rs[:, half:half + 1],
                                                                 in1=GB[:, gi["norm_ffn_g_2"], :], op0=ALU.mult,
                                                                 op1=ALU.mult)))
    nt = turn(XN, None, ts, ball)
    product_T(A["w_peer_q_2"][0], 0, 16, NT, nt, ball, ev_copy(qp, "act"))
    t_q = tt["cp"]
    t_sc = {}
    for half in range(2):
        for q in range(4):
            b = ball.take()
            k.wait("pe", [b.free, t_q, t_keys])
            for r in range(4):
                i = 4 * q + r
                ins = mm(b.ap[:, r * 128:r * 128 + 128], qp[:, i, half * 128:half * 128 + 128],
                         keysT[:, (i % 2) * 8 + i // 2, :], True)
            t_pq = t = k.mark(k.sem["pe"], ins, 1)
            t_sc[half, q] = act([t], lambda e: e.activation(SC[half][:, 4 * q:4 * q + 4, :],
                                                            b.ap.rearrange("p (a b) -> p a b", a=4), ACT.Copy))
            b.free = [t_sc[half, q]]

    at = [10240]

    def a2(*shape):
        n = 1
        for x in shape:
            n *= x
        o = at[0]
        at[0] += n
        return ar(o, *shape)

    def a2u(n):
        o = at[0]
        at[0] += n
        return AU[:, o:o + n]

    iot = a2(16)
    ioti = AR[:, at[0]:at[0] + 16].bitcast(mybir.dt.int32)
    at[0] += 16
    t = pool([t_pq], lambda e: e.iota(ioti, pattern=[[1, 16]], base=0, channel_multiplier=0))
    t_iota = pool([t], lambda e: e.tensor_copy(iot, ioti))
    UB = 3
    un = []
    for i in range(UB):
        un.append(dict(V=a2(2, 16), I=a2u(32), IF=a2(2, 16), best=a2(16), pos=a2u(16), pp=a2u(32), pf=a2(2, 16),
                       sel=a2(2, 16), idx=a2u(16), e=a2(16), s=a2(1), r=a2(1), nb=a2(1), a=a2(16), g=a2(16),
                       w=a2(16)))
    cand = [ar(0, 256), ar(256, 256)]
    oh = ar(512, 2, 16, 16)
    diag = [ar(1024 + 128 * i, P) for i in range(8)]
    gs = [Slot(ring[:, i // 2, (i % 2) * 1024:(i % 2) * 1024 + 1024], k.semaphore(f"gather{i}"))
          for i in range(2 * NSLOT)]
    ngs = [0]

    def gather(table, idx, waits):
        s = gs[ngs[0] % len(gs)]
        ngs[0] += 1
        k.wait("pool", [s.free, waits])
        ins = nc.gpsimd.indirect_dma_start(s.ap, None, table, bass.IndirectOffsetOnAxis(idx, 0))
        return s, k.mark(s.sem, ins, 16)

    def choose(n):
        half, head = n // 8, n % 8
        x = un[n % UB]
        free = [unit_done.get(n - UB)]

        def step(waits, f):
            return dve(waits, f)

        def top16(src, v, i, waits):
            t = step([waits, free], lambda e: e.max(v[:, 0:8], src))
            t1 = step([t], lambda e: e.max_index(i[:, 0:8], v[:, 0:8], src))
            t = step([t, t1], lambda e: e.match_replace(src, v[:, 0:8], src, -3.0e38))
            t = step([t], lambda e: e.max(v[:, 8:16], src))
            return step([t], lambda e: e.max_index(i[:, 8:16], v[:, 8:16], src))

        for a in range(2):
            t = top16(SC[half][:, 2 * head + a, :], x["V"][:, a, :], x["I"][:, 16 * a:16 * a + 16],
                      [t_sc[half, (2 * head + a) // 4], t_pq])
            yield
        ti = step([t], lambda e: e.tensor_copy(x["IF"], x["I"].rearrange("p (a b) -> p a b", a=2)))
        c = cand[n % 2]
        t = step([t], lambda e: e.tensor_tensor(c.rearrange("p (a b) -> p a b", a=16),
                                                x["V"][:, 0, :].unsqueeze(2).broadcast_to([P, 16, 16]),
                                                x["V"][:, 1, :].unsqueeze(1).broadcast_to([P, 16, 16]), ALU.add))
        yield
        t = top16(c, x["best"], x["pos"], [t])
        yield
        u = act([t], lambda e: e.activation(x["nb"], x["best"][:, 0:1], ACT.Copy, scale=-1.0))
        u = act([u], lambda e: e.activation(x["e"], x["best"], ACT.Exp, bias=x["nb"], accum_out=x["s"]))
        step([t], lambda e: e.tensor_scalar(x["pp"][:, 0:16], x["pos"], 4, None, ALU.logical_shift_right))
        t = step([t], lambda e: e.tensor_scalar(x["pp"][:, 16:32], x["pos"], 15, None, ALU.bitwise_and))
        t = step([t], lambda e: e.tensor_copy(x["pf"], x["pp"].rearrange("p (a b) -> p a b", a=2)))
        yield
        t = step([t, t_iota], lambda e: e.tensor_tensor(
            oh, x["pf"].unsqueeze(3).broadcast_to([P, 2, 16, 16]),
            iot.unsqueeze(1).unsqueeze(1).broadcast_to([P, 2, 16, 16]), ALU.is_equal))
        yield
        t = step([t, ti], lambda e: e.tensor_tensor(oh, oh, x["IF"].unsqueeze(2).broadcast_to([P, 2, 16, 16]),
                                                    ALU.mult))
        yield
        t = step([t], lambda e: e.tensor_reduce(x["sel"], oh, AX.X, ALU.add))
        t = step([t], lambda e: e.scalar_tensor_tensor(out=x["idx"], in0=x["sel"][:, 0, :], scalar=128.0,
                                                       in1=x["sel"][:, 1, :], op0=ALU.mult, op1=ALU.add))
        x["t_idx"] = t
        x["t_r"] = step([u], lambda e: e.reciprocal(x["r"], x["s"]))

    U_, V_ = A["peer_u_2"][0], A["peer_v_2"][0]
    unit_done = {}
    acc = {}
    dfree = [None] * 8
    nd = 0
    ring_free = [s.free for s in slots]
    for g in gs:
        g.free = [ring_free]
    for _ in choose(0):
        pass
    fin = []
    for n in range(17):
        nxt = choose(n + 1) if n + 1 < 16 else iter(())
        half = n // 8
        x = un[n % UB]
        y = un[(n - 1) % UB]
        for kk in range(16):
            if n < 16:
                s, t = gather(U_, x["idx"][:, kk:kk + 1], [x["t_idx"]])
                t = dve([t, ts], lambda e: e.tensor_tensor_reduce(s.ap, s.ap, XN[:, half, :], 1.0, 0.0, ALU.mult,
                                                                  ALU.add, x["a"][:, kk:kk + 1]))
                s.free = [t]
            if n > 0:
                s2, t2 = gather(V_, y["idx"][:, kk:kk + 1], [])
                hv_ = (n - 1) // 8
                d = diag[nd % 8]
                td = act([y["t_w"], dfree[nd % 8]], lambda e: e.activation(d, ident, ACT.Copy,
                                                                            scale=y["w"][:, kk:kk + 1]))
                first, last = (n - 1) % 8 == 0 and kk == 0, (n - 1) % 8 == 7 and kk == 15
                k.wait("pe", [td, t2] + ([bank[4 + 2 * hv_].free, bank[5 + 2 * hv_].free] if first else []))
                for nb in range(2):
                    ins = mm(bank[4 + 2 * hv_ + nb].ap, d, s2.ap[:, nb * 512:nb * 512 + 512], first, last)
                tm = k.mark(k.sem["pe"], ins, 1)
                s2.free = [tm]
                dfree[nd % 8] = tm
                nd += 1
            next(nxt, None)
        for _ in nxt:
            pass
        if n > 0:
            unit_done[n - 1] = tm
        if n < 16:
            t = act([t], lambda e: e.activation(x["g"], x["a"], ACT.Gelu))
            x["t_w"] = dve([t, x["t_r"]], lambda e: e.scalar_tensor_tensor(out=x["w"], in0=x["e"], scalar=x["r"],
                                                                          in1=x["g"], op0=ALU.mult, op1=ALU.mult))
        if n in (8, 16):
            h_ = n // 8 - 1
            av_ = ps[:, 4 + 2 * h_:6 + 2 * h_, :].rearrange("p a b -> p (a b)")
            t = dve([tm], lambda e: e.tensor_tensor(H[:, h_, :], av_, H[:, h_, :], ALU.add))
            _, t = rstd(h_, H[:, h_, :], D, [t, norm_state["rs"]])
            fin.append(dve([t, t_b], lambda e: e.scalar_tensor_tensor(out=H[:, h_, :], in0=H[:, h_, :],
                                                                      scalar=rs[:, h_:h_ + 1],
                                                                      in1=GB[:, gi["norm_final_g_2"], :],
                                                                      op0=ALU.mult, op1=ALU.mult)))
    s_o = k.semaphore("s_o")
    for h_ in range(2):
        t = k.dma("sp", s_o, [fin[h_]], out[0, h_ * P:(h_ + 1) * P, :], H[:, h_, :])
    k.wait("sp", [t])


_INS = ['x', 'mem', 'ffn1_pre_g', 'ffn1_w_gu', 'ffn1_w_down', 'ffn1_post_g', 'mix_pre_g', 'w_in', 'conv_w',
        'conv_b', 'dt_bias', 'a_log', 'd_skip', 'ssd_norm_g', 'attn_norm_g', 'w_out', 'mix_post_g', 'xa_pre_g',
        'mem_g', 'xa_wq', 'xa_wkv', 'xa_wo', 'xa_post_g', 'ffn2_pre_g', 'ffn2_w_gu', 'ffn2_w_down', 'ffn2_post_g',
        'norm_mix_g_2', 'w_in_2', 'attn_sinks_2', 'hgrn_lb_logits_2', 'hgrn_norm_g_2', 'w_attn_proj_2',
        'w_hgrn_proj_2', 'w_out_2', 'norm_ffn_g_2', 'w_peer_q_2', 'peer_keys_2', 'peer_u_2', 'peer_v_2',
        'norm_final_g_2']


def kernel(**inputs):
    import numpy as _np
    import concourse.bacc as _bacc
    from concourse import mybir as _mybir
    from concourse.bass_utils import run_bass_kernel_spmd as _run

    nc = _bacc.Bacc("TRN2", target_bir_lowering=False, num_devices=1)
    arrays, args = {}, {}
    for name in _INS:
        a = _np.ascontiguousarray(inputs[name])
        arrays[f"in_{name}_dram"] = a
        args[name] = nc.dram_tensor(f"in_{name}_dram", a.shape, _mybir.dt.from_np(a.dtype),
                                    kind="ExternalInput").ap()
    o = nc.dram_tensor("out_0_dram", (1, T, D), _mybir.dt.float32, kind="ExternalOutput").ap()
    build(nc, args, o)
    r = _run(nc, [arrays], core_ids=[0])
    return r.results[0]["out_0_dram"]
```

```python
from contextlib import ExitStack

import concourse.bass as bass
from concourse import mybir

F32 = mybir.dt.float32
U32 = mybir.dt.uint32
F32R = mybir.dt.float32r
ALU = mybir.AluOpType
ACT = mybir.ActivationFunctionType
AX = mybir.AxisListType

P = 128
D = 1024
T = 256
EPS = 1e-6
NRAW = 4
NCONV = 2
FFN_TILES = 22


class Chip:

    def __init__(self, nc, ctx):
        self.nc = nc
        self.ctx = ctx
        self.count = {}
        self.seen = {}
        self.engine = {"pe": nc.tensor, "dve": nc.vector, "act": nc.scalar, "pool": nc.gpsimd, "sp": nc.sync}
        self.sem = {k: self.semaphore("done_" + k) for k in ("pe", "dve", "act", "pool")}

    def semaphore(self, name):
        s = self.ctx.enter_context(self.nc.semaphore(name))
        self.count[name] = 0
        return (name, s)

    def wait(self, eng, toks):
        for t in toks:
            if t is None:
                continue
            if type(t) is list:
                self.wait(eng, t)
                continue
            (name, s), v = t
            if self.seen.get((eng, name), 0) < v:
                self.seen[(eng, name)] = v
                self.engine[eng].wait_ge(s, v)

    def mark(self, sem, ins, n):
        ins.then_inc(sem[1], n)
        self.count[sem[0]] += n
        return (sem, self.count[sem[0]])

    def dve(self, waits, f):
        self.wait("dve", waits)
        return self.mark(self.sem["dve"], f(self.nc.vector), 1)

    def act(self, waits, f):
        self.wait("act", waits)
        return self.mark(self.sem["act"], f(self.nc.scalar), 1)

    def pool(self, waits, f):
        self.wait("pool", waits)
        return self.mark(self.sem["pool"], f(self.nc.gpsimd), 1)

    def pe(self, waits, f):
        self.wait("pe", waits)
        return self.mark(self.sem["pe"], f(self.nc.tensor), 1)

    def mm(self, out, lhsT, rhs, start, stop=True):
        return self.nc.tensor.matmul(out, lhsT, rhs, start=start, stop=stop, skip_group_check=True)

    def dma(self, eng, sem, waits, out, in_):
        self.wait(eng, waits)
        return self.mark(sem, self.engine[eng].dma_start(out, in_), 16)


class Bank:

    def __init__(self, ap):
        self.ap = ap
        self.free = []


class Banks:
    def __init__(self, banks):
        self.banks = banks
        self.n = 0

    def take(self):
        b = self.banks[self.n % len(self.banks)]
        self.n += 1
        return b


class Slot:
    def __init__(self, ap, sem):
        self.ap = ap
        self.sem = sem
        self.free = []


def build(nc, A, out):
    with ExitStack() as ctx:
        body(nc, ctx, A, out)


def body(nc, ctx, A, out):
    k = Chip(nc, ctx)
    dve, act, pool, pe, mm = k.dve, k.act, k.pool, k.pe, k.mm

    def sb(name, shape, dt=F32):
        return ctx.enter_context(nc.sbuf_tensor(name, shape, dt))

    H = sb("H", [P, 2, D])
    XN = sb("XN", [P, 2, D])
    JA = sb("JA", [P, D])
    GB = sb("GB", [P, 2, D])
    PG = sb("PG", [P, 160])
    cst = sb("cst", [P, 8, P])
    small = sb("small", [P, 512])
    LB = sb("LB", [P, 2, 512])
    AR = sb("AR", [P, 14604])
    AU = AR[:, :].bitcast(U32)
    wctx = ExitStack()
    RAW = wctx.enter_context(nc.sbuf_tensor("RAW", [P, NRAW, 2048], F32))
    WH = wctx.enter_context(nc.sbuf_tensor("WH", [P, NCONV, 2048], F32R))
    WL = wctx.enter_context(nc.sbuf_tensor("WL", [P, NCONV, 2048], F32R))
    XH = wctx.enter_context(nc.sbuf_tensor("XH", [P, 8, T], F32R))
    XL = wctx.enter_context(nc.sbuf_tensor("XL", [P, 8, T], F32R))
    YY = wctx.enter_context(nc.sbuf_tensor("YY", [P, 32, T], F32R))
    NT = (XH[:, :, :], XL[:, :, :])
    ps = ctx.enter_context(nc.psum_tensor("ps", [P, 8, 512], F32))
    bank = [Bank(ps[:, i, :]) for i in range(8)]
    slots = [Slot(RAW[:, i, :], k.semaphore(f"raw{i}")) for i in range(NRAW)]
    conv_free = [None] * NCONV

    ident, ones, negtri, negones, tri_le, tri_gt, bt_le, bt_gt = [cst[:, i, :] for i in range(8)]

    smallat = [0]

    def sm(n):
        a = smallat[0]
        smallat[0] += n
        return small[:, a:a + n]

    def ar(off, *shape):
        n = 1
        for s in shape:
            n *= s
        v = AR[:, off:off + n]
        if len(shape) == 2:
            v = v.rearrange("p (a b) -> p a b", a=shape[0])
        if len(shape) == 3:
            v = v.rearrange("p (a b c) -> p a b c", a=shape[0], b=shape[1])
        return v

    def cols(w, a, n):
        return w.rearrange("(c p) n -> p c n", p=P)[:, :, a:a + n]

    def rows(w, j, n):
        return w.rearrange("(j p) n -> p j n", p=P)[:, j:j + n, :]

    plan = []

    def plan_cols(w, a, n, kt=8):
        per = 2048 // kt
        for c in range(a, a + n, per):
            plan.append(cols(w, c, per))

    def plan_rows(w, j0, n):
        for j in range(j0, j0 + n, 2):
            plan.append(rows(w, j, 2))

    def plan_ffn(wgu, wd):
        for i in range(FFN_TILES // 2):
            plan_cols(wgu, i * 256, 256)
            plan_cols(wgu, 2816 + i * 256, 256)
            if i:
                plan_rows(wd, 2 * i - 2, 2)
        plan_rows(wd, FFN_TILES - 2, 2)

    plan_ffn(A["ffn1_w_gu"][0], A["ffn1_w_down"][0])
    plan_cols(A["w_in"][0], 0, 5632)
    plan_rows(A["w_out"][0], 0, 16)
    plan_cols(A["xa_wkv"][0], 0, 2048)
    plan_cols(A["xa_wq"][0], 0, 1024)
    plan_rows(A["xa_wo"][0], 0, 8)
    plan_ffn(A["ffn2_w_gu"][0], A["ffn2_w_down"][0])
    w2p = A["w_in_2"][0].rearrange("(c p) n -> p c n", p=P)
    for jp in range(2):
        plan.append((w2p[:, :, jp * 128:jp * 128 + 128], w2p[:, :, 256 + jp * 128:384 + jp * 128]))
    plan_cols(A["w_in_2"][0], 512, 256)
    plan_cols(A["w_in_2"][0], 1280, 1024)
    plan_cols(A["w_in_2"][0], 768, 512)
    plan_cols(A["w_in_2"][0], 2304, 512)
    plan_cols(A["w_in_2"][0], 2816, 2048)
    for n0 in (0, 512):
        plan_cols(A["w_attn_proj_2"][0], n0, 512, 4)
        plan_cols(A["w_hgrn_proj_2"][0], n0, 512, 4)
    plan_rows(A["w_out_2"][0], 0, 8)
    plan_cols(A["w_peer_q_2"][0], 0, 2048)

    state = {"hi": "act", "load": 0, "conv": 0, "ready": 0, "take": 0}
    loaded, pieces = {}, {}

    def load_next():
        n = state["load"]
        if n >= len(plan):
            return
        state["load"] += 1
        src = plan[n]
        s = slots[n % NRAW]
        if type(src) is tuple:
            v = s.ap.rearrange("p (k r q n) -> p k r q n", k=8, r=2, q=2)
            for i in range(4):
                tok = k.dma("sp", s.sem, s.free, v[:, :, i // 2, i % 2, :],
                            src[i % 2][:, :, 64 * (i // 2):64 * (i // 2) + 64])
            loaded[n] = (s, s.ap.rearrange("p (k n) -> p k n", k=8), tok)
            return
        kt, w = src.shape[1], src.shape[2]
        v = s.ap[:, 0:kt * w].rearrange("p (k n) -> p k n", k=kt)
        loaded[n] = (s, v, k.dma("sp", s.sem, s.free, v, src))

    def split_next():
        n = state["ready"]
        if n >= len(plan):
            return
        state["ready"] += 1
        load_next()
        s, v, tok = loaded.pop(n)
        i = state["conv"] % NCONV
        state["conv"] += 1
        kt, w = v.shape[1], v.shape[2]
        hi = WH[:, i, 0:kt * w].rearrange("p (k n) -> p k n", k=kt)
        lo = WL[:, i, 0:kt * w].rearrange("p (k n) -> p k n", k=kt)
        if state["hi"] == "act":
            th = act([tok, conv_free[i]], lambda e: e.activation(hi, v, ACT.Copy))
        else:
            th = dve([tok, conv_free[i]], lambda e: e.tensor_copy(hi, v))
        tl = dve([tok, th, conv_free[i]], lambda e: e.tensor_tensor(lo, v, hi.bitcast(F32), ALU.subtract))
        s.free = [th, tl]
        pieces[n] = (i, hi, lo, [th, tl])

    def take(kt, w):
        n = state["take"]
        state["take"] += 1
        if n not in pieces:
            split_next()
        p = pieces.pop(n)
        assert p[1].shape[1] == kt and p[1].shape[2] == w, (n, p[1].shape, kt, w)
        if n + 1 not in pieces:
            split_next()
        return p

    def release(p, t):
        conv_free[p[0]] = t

    def mm3(out, wh, wl, x, cx, first, last, w_moves=False):
        xh, xl = cx(x[0]), cx(x[1])
        for q, (a, b_) in enumerate(((wh, xh), (wh, xl), (wl, xh))):
            if w_moves:
                a, b_ = b_, a
            ins = mm(out, a, b_, first and q == 0, last and q == 2)
        return ins

    s_x = k.semaphore("s_x")
    t_x = k.dma("sp", s_x, [], H[:, :, :], A["x"][0].rearrange("(h p) d -> p h d", p=P))
    rows1 = AR[:, 0:128]
    rows2 = AR[0:61, 128:256]
    s_g = k.semaphore("s_g")
    col = {}
    at = 0
    t_g = None
    for name, n in (("ffn1_pre_g", 8), ("mix_pre_g", 8), ("xa_pre_g", 8), ("mem_g", 8), ("ffn2_pre_g", 8),
                    ("norm_mix_g_2", 8), ("norm_ffn_g_2", 8), ("attn_norm_g", 8), ("ssd_norm_g", 8),
                    ("conv_b", 12), ("hgrn_norm_g_2", 1)):
        col[name] = at
        t_g = k.dma("sp", s_g, [], AR[at:at + n, 0:128], A[name][0].rearrange("(c p) -> c p", p=P))
        at += n
    n_rows1 = at
    for i in range(4):
        col["conv_w%d" % i] = 112 + 12 * i
    t_g = k.dma("sp", s_g, [], AR[0:48, 128:256], A["conv_w"][0].rearrange("k (c p) -> (k c) p", p=P))

    s_b = k.semaphore("s_b")
    dtb, alog, dsk, sink = sm(16), sm(16), sm(16), sm(8)
    for _ in range(NRAW - 1):
        load_next()

    row_names = ["ffn1_post_g", "mix_post_g", "xa_post_g", "ffn2_post_g", "norm_ffn_g_2", "norm_final_g_2"]
    s_gb = [k.semaphore("s_gb0"), k.semaphore("s_gb1")]
    row_gain = {}

    def load_row_gain(i, waits):
        if i >= len(row_names):
            return
        name = row_names[i]
        src = A[name] if name == "norm_final_g_2" else A[name][0]
        v = GB[:, i % 2, :]
        row_gain[name] = (v, k.dma("sp", s_gb[i % 2], waits, v, src.unsqueeze(0).broadcast_to([P, D])))

    t = pool([], lambda e: e.memset(ident, 0.0))
    t = pool([], lambda e: e.memset(cst[:, 1:3, :], 1.0))
    t = pool([], lambda e: e.memset(cst[:, 3, :], -1.0))
    t = pool([], lambda e: e.memset(cst[:, 4:8, :], 1.0))
    t = pool([t], lambda e: e.memset(negtri, -1.0))

    def sel(v, base, pattern, cm, op, fill=0.0):
        return lambda e: e.affine_select(out=v, in_=v, compare_op=op, fill=fill, base=base, pattern=pattern,
                                         channel_multiplier=cm)

    t_id = pool([t], sel(ident, 0, [[-1, P]], 1, ALU.not_equal, 1.0))
    pool([], sel(negtri, 0, [[-1, P]], 1, ALU.is_ge))
    pool([], sel(tri_le, 0, [[1, P]], -1, ALU.is_ge))
    pool([], sel(tri_gt, 0, [[-1, P]], 1, ALU.is_gt))
    t1 = pool([], sel(bt_le, 0, [[1, P]], -1, ALU.is_ge))
    t2 = pool([], sel(bt_gt, 0, [[-1, P]], 1, ALU.is_gt))
    t1 = pool([t1, t2], sel(bt_le, 0, [[-32, 4], [0, 32]], 1, ALU.is_ge))
    t_cst = pool([t1], sel(bt_gt, 31, [[32, 4], [0, 32]], -1, ALU.is_ge))

    b = bank[0]
    k.wait("pe", [t_id, t_g])
    nc.tensor.transpose(b.ap[:, 0:n_rows1], AR[0:n_rows1, 0:128], ident[0:n_rows1, 0:n_rows1])
    t = pe([], lambda e: e.transpose(b.ap[:, 112:160], AR[0:48, 128:256], ident[0:48, 0:48]))
    dve([t], lambda e: e.tensor_copy(PG[:, 0:n_rows1], b.ap[:, 0:n_rows1]))
    t_pg = dve([], lambda e: e.tensor_copy(PG[:, 112:160], b.ap[:, 112:160]))
    b.free = [t_pg]

    def pg(name, c):
        a = col[name] + c
        return PG[:, a:a + 1]

    ssq = sm(2)
    rs = sm(2)
    msq = sm(2)
    half_c = sm(16)
    t_hc = pool([], lambda e: e.memset(half_c, -0.5))
    norm_state = {"ja": None, "rs": None}

    def rstd(half, src, n, waits, coef=1.0):
        i = half
        t = act([waits, norm_state["ja"]], lambda e: e.activation(JA[:, 0:src_len(src)], src, ACT.Square,
                                                                  accum_out=ssq[:, i:i + 1]))
        norm_state["ja"] = t
        t1 = dve([t], lambda e: e.tensor_scalar(msq[:, i:i + 1], ssq[:, i:i + 1], 1.0 / (n * coef * coef),
                                                EPS / (coef * coef), ALU.mult, ALU.add))
        t2 = pool([t1, t_hc], lambda e: e.tensor_tensor(rs[:, i:i + 1], msq[:, i:i + 1], half_c[:, 0:1], ALU.pow))
        return t, t2

    def src_len(src):
        return src.shape[-1]

    def turn(src, gain, waits, banks, dst=NT):
        last = []
        for pair in range(4):
            b = banks.take()
            k.wait("pe", [b.free, waits, t_id])
            for cc in range(2):
                for half in range(2):
                    c = 2 * pair + cc
                    ins = nc.tensor.transpose(b.ap[:, cc * 256 + half * 128:cc * 256 + half * 128 + 128],
                                              src[:, half, c * 128:(c + 1) * 128], ident)
            t = k.mark(k.sem["pe"], ins, 1)
            t1 = t
            for cc in range(2):
                c = 2 * pair + cc
                o, i_ = dst[0][:, c, :], b.ap[:, cc * 256:cc * 256 + 256]
                if gain is None:
                    t1 = act([t], lambda e: e.activation(o, i_, ACT.Copy))
                else:
                    t1 = act([t, t_pg], lambda e: e.activation(o, i_, ACT.Copy, scale=pg(gain, c)))
            for cc in range(2):
                c = 2 * pair + cc
                h_, o, i_ = dst[0][:, c, :].bitcast(F32), dst[1][:, c, :], b.ap[:, cc * 256:cc * 256 + 256]
                if gain is None:
                    t2 = dve([t1], lambda e: e.tensor_tensor(o, i_, h_, ALU.subtract))
                else:
                    t2 = dve([t1], lambda e: e.scalar_tensor_tensor(out=o, in0=i_, scalar=pg(gain, c), in1=h_,
                                                                    op0=ALU.mult, op1=ALU.subtract))
            b.free = [t2]
            last.append(t2)
        return last

    def prenorm(src, gain, waits, banks):
        ts = []
        for half in range(2):
            _, t = rstd(half, src[:, half, :], D, [waits, norm_state["rs"]])
            ts.append(dve([t], lambda e: e.tensor_scalar(XN[:, half, :], src[:, half, :],
                                                                           rs[:, half:half + 1], None, ALU.mult)))
        norm_state["rs"] = ts[-1]
        r = turn(XN, gain, ts, banks)
        return r

    def postnorm(gain, coef, waits):
        out_t = []
        for half in range(2):
            acc = ps[:, 2 * half:2 * half + 2, :].rearrange("p a b -> p (a b)")
            ta, t = rstd(half, acc, D, [waits[half], norm_state["rs"]], coef)
            g, t_row = row_gain[gain]
            t_g1 = t = dve([ta, t, t_row], lambda e: e.scalar_tensor_tensor(out=acc, in0=acc,
                                                                            scalar=rs[:, half:half + 1], in1=g,
                                                                            op0=ALU.mult, op1=ALU.mult))
            t = dve([t], lambda e: e.tensor_tensor(H[:, half, :], acc, H[:, half, :], ALU.add))
            bank[2 * half].free = [t]
            bank[2 * half + 1].free = [t]
            out_t.append(t)
        norm_state["rs"] = out_t[-1]
        load_row_gain(row_names.index(gain) + 2, [t_g1])
        return out_t

    b47 = Banks(bank[4:8])
    ball = Banks(bank)

    def product_T(ntiles, x, waits, banks, evac, kt=8):
        per = 2048 // (kt * 128)
        for n0 in range(0, ntiles, per):
            p = take(kt, per * 128)
            k.wait("pe", [p[3], waits])
            for q in range(0, per, 2):
                b = banks.take()
                k.wait("pe", [b.free])
                for r in range(2):
                    a = (q + r) * 128
                    for c in range(kt):
                        ins = mm3(b.ap[:, r * 256:r * 256 + 256], p[1][:, c, a:a + 128], p[2][:, c, a:a + 128], x,
                                  lambda v: v[:, c, :], c == 0, c == kt - 1)
                t = k.mark(k.sem["pe"], ins, 1)
                if q == per - 2:
                    release(p, t)
                b.free = [evac(n0 + q, b.ap, t)]

    def product_N(ncols, x, waits, banks, evac):
        for n0 in range(0, ncols, 256):
            p = take(8, 256)
            b = banks.take()
            k.wait("pe", [p[3], waits, b.free])
            for half in range(2):
                for c in range(8):
                    ins = mm3(b.ap[:, half * 256:half * 256 + 256], p[1][:, c, :], p[2][:, c, :], x,
                              lambda v: v[:, c, half * 128:half * 128 + 128], c == 0, c == 7, True)
            t = k.mark(k.sem["pe"], ins, 1)
            release(p, t)
            b.free = [evac(n0, b.ap, t)]

    def product_acc(j0, total, x, waits, at=None):
        p = take(2, D)
        at = j0 if at is None else at
        k.wait("pe", [p[3], waits] + ([bank[i].free for i in range(4)] if j0 == 0 else []))
        toks = []
        for half in range(2):
            for jj in range(2):
                for nb in range(2):
                    ins = mm3(bank[2 * half + nb].ap, p[1][:, jj, nb * 512:nb * 512 + 512],
                              p[2][:, jj, nb * 512:nb * 512 + 512], x,
                              lambda v: v[:, at + jj, half * 128:half * 128 + 128], j0 + jj == 0,
                              j0 + jj == total - 1, True)
            toks.append(k.mark(k.sem["pe"], ins, 1))
        release(p, toks[-1])
        return toks

    def split(dst_h, dst_l, src, waits):
        t = act([waits], lambda e: e.activation(dst_h, src, ACT.Copy))
        return dve([t, waits], lambda e: e.tensor_tensor(dst_l, src, dst_h.bitcast(F32), ALU.subtract))

    def ffn(nt, post):
        sg = [ar(256 * i, 256) for i in range(4)]
        tm_ = [ar(1024 + 256 * i, 256) for i in range(4)]
        sgfree, tfree, afree = [None] * 4, [None] * 4, [None] * 3
        pend = None
        for i in range(FFN_TILES // 2):
            bb, tb = [b47.take(), b47.take()], [None, None]
            for q in range(2):
                p = take(8, 256)
                for r in range(2):
                    k.wait("pe", [p[3], nt, bb[r].free])
                    for c in range(8):
                        ins = mm3(bb[r].ap[:, q * 256:q * 256 + 256], p[1][:, c, r * 128:(r + 1) * 128],
                                  p[2][:, c, r * 128:(r + 1) * 128], NT, lambda v: v[:, c, :], c == 0, c == 7)
                    tb[r] = k.mark(k.sem["pe"], ins, 1)
                release(p, tb[1])
            for r in range(2):
                j = 2 * i + r
                b, t = bb[r], tb[r]
                x, y = sg[j % 4], tm_[j % 4]
                t1 = act([t, sgfree[j % 4]], lambda e: e.activation(x, b.ap[:, 0:256], ACT.Silu))
                t2 = dve([t1, tfree[j % 4]], lambda e: e.tensor_tensor(y, b.ap[:, 256:512], x, ALU.mult))
                sgfree[j % 4] = t2
                b.free = [t2]
                a = 4 * (i % 3) + r
                tfree[j % 4] = t2 = split(YY[:, a, :], YY[:, a + 2, :], y, [t2, afree[i % 3]])
            if pend is not None:
                v = YY[:, 4 * (pend[0] % 3):4 * (pend[0] % 3) + 4, :]
                afree[pend[0] % 3] = product_acc(2 * pend[0], FFN_TILES, (v[:, 0:2, :], v[:, 2:4, :]), [pend[1]], 0)[1]
            pend = (i, t2)
        v = YY[:, 4 * (pend[0] % 3):4 * (pend[0] % 3) + 4, :]
        toks = product_acc(2 * pend[0], FFN_TILES, (v[:, 0:2, :], v[:, 2:4, :]), [pend[1]], 0)
        return postnorm(post, 0.5, toks)

    nt = prenorm(H, "ffn1_pre_g", [t_x], ball)
    for v, name, n in ((dtb, "dt_bias", 16), (alog, "a_log", 16), (dsk, "d_skip", 16), (sink, "attn_sinks_2", 8)):
        t_b = k.dma("act", s_b, [], v, A[name][0].unsqueeze(0).broadcast_to([P, n]))
    t_b = k.dma("act", s_b, [], LB[:, :, :], A["hgrn_lb_logits_2"].unsqueeze(0).broadcast_to([P, 2, 512]))
    load_row_gain(0, [])
    load_row_gain(1, [])
    lt = ar(4096, 3, 512)
    t = dve([t_b], lambda e: e.tensor_tensor(lt[:, 2, :], LB[:, 0, :], LB[:, 1, :], ALU.max))
    t = dve([t], lambda e: e.tensor_tensor(lt[:, 0:2, :], LB[:, :, :], lt[:, 2, :].unsqueeze(1).broadcast_to([P, 2, 512]),
                                           ALU.subtract))
    t = act([t], lambda e: e.activation(lt[:, 0:2, :], lt[:, 0:2, :], ACT.Exp))
    t = dve([t], lambda e: e.tensor_tensor(lt[:, 1, :], lt[:, 0, :], lt[:, 1, :], ALU.add))
    t = dve([t], lambda e: e.reciprocal(lt[:, 1, :], lt[:, 1, :]))
    t = dve([t], lambda e: e.tensor_tensor(LB[:, 0, :], lt[:, 0, :], lt[:, 1, :], ALU.mult))
    t_lb = dve([t], lambda e: e.tensor_scalar(LB[:, 1, :], LB[:, 0, :], -1.0, 1.0, ALU.mult, ALU.add))

    t_h = ffn(nt, "ffn1_post_g")

    def softplus(dst, e, z, waits, efree):
        t = act([waits, efree], lambda g: g.activation(e, z, ACT.Abs))
        t = act([t], lambda g: g.activation(e, e, ACT.Exp, scale=-1.0))
        t = act([t], lambda g: g.activation(e, e, ACT.Ln, bias=1.0))
        return t, dve([t, waits], lambda g: g.scalar_tensor_tensor(out=dst, in0=z, scalar=0.0, in1=e, op0=ALU.max,
                                                                  op1=ALU.add))

    nt = prenorm(H, "mix_pre_g", t_h, ball)
    qT, kT, Z = ar(0, 8, 256), ar(2048, 8, 256), ar(4096, 2, D)
    wdt = ar(11264, 8, 16)
    s_wdt = k.semaphore("s_wdt")
    t_wdt = k.dma("act", s_wdt, [], wdt, cols(A["w_in"][0], 5632, 16))
    catA = (YY[:, 0:8, :], YY[:, 8:16, :])
    catB = (YY[:, 16:24, :], YY[:, 24:32, :])
    xc = ar(6144, 12, 256)
    xn = ar(9216, 2, D)
    bn = ar(11264, 256)
    raw = [ar(11520 + 259 * i, 259) for i in range(3)]
    V = XN
    two = Banks([bank[4], bank[5]])
    tt = {}

    def ev_q(n, b, t):
        tt["q"] = act([t], lambda e: e.activation(qT[:, n:n + 2, :], b.rearrange("p (a b) -> p a b", a=2), ACT.Copy,
                                                  scale=0.125))
        return tt["q"]

    def ev_k(n, b, t):
        tt["k"] = dve([t], lambda e: e.tensor_copy(kT[:, n:n + 2, :], b.rearrange("p (a b) -> p a b", a=2)))
        return tt["k"]

    def ev_v(n, b, t):
        tt["v"] = dve([t], lambda e: e.tensor_copy(V[:, :, n:n + 256], b.rearrange("p (a b) -> p a b", a=2)))
        return tt["v"]

    product_T(8, NT, nt, ball, ev_q)
    product_T(8, NT, nt, ball, ev_k)
    product_N(1024, NT, nt, ball, ev_v)

    zb = Banks(bank[0:4])
    ee = [ar(12298 + 384 * i, 384) for i in range(2)]
    sp = [ar(13066 + 384 * i, 384) for i in range(2)]
    at_ = [ar(13834 + 384 * i, 384) for i in range(2)]
    sqb = [small[:, 256:512]]
    zbank, t_sp, t_a, pv_t = {}, {}, {}, {}
    sp_free, e_free, a_free = [None, None], [None, None], [None, None]
    sq_state = {"free": None, "pend": None}

    def diag(v, fill):
        return lambda g: g.affine_select(out=v, in_=v, compare_op=ALU.is_gt, fill=fill, base=0,
                                         pattern=[[0, 2], [1, P]], channel_multiplier=-1)

    def dview(x):
        return x.rearrange("p (a b) -> p a b", a=3)[:, 0:3:2, :]

    def at_scores(h):
        b = zb.take()
        zbank[h] = b
        o = 64 * (h % 2)
        k.wait("pe", [b.free, tt["q"], tt["k"]])
        mm(b.ap[:, 0:256], kT[o:o + 64, h // 2, 0:128], qT[o:o + 64, h // 2, :], True)
        t = pe([], lambda e: mm(b.ap[:, 256:384], kT[o:o + 64, h // 2, 128:256], qT[o:o + 64, h // 2, 128:256],
                                False))
        i = h % 2
        te, ts = softplus(sp[i], ee[i], b.ap[:, 0:384], [t, sp_free[i]], e_free[i])
        e_free[i] = ts
        t_sp[h] = pool([ts], diag(dview(sp[i]), 0.0))

    def at_logs(h):
        b, i = zbank[h], h % 2
        k.wait("pe", [t_sp[h], t_cst])
        mm(b.ap[:, 0:256], negtri, sp[i][:, 0:256], False)
        mm(b.ap[:, 128:256], negones, sp[i][:, 256:384], False)
        t = pe([], lambda e: mm(b.ap[:, 256:384], negtri, sp[i][:, 256:384], False))
        sp_free[i] = t
        t = act([t, a_free[i]], lambda e: e.activation(at_[i], b.ap[:, 0:384], ACT.Exp))
        b.free = [t]
        t_a[h] = pool([t], diag(dview(at_[i]), 0.0))


    def at_values(h):
        i, o = h % 2, 64 * (h % 2)
        b = bank[6]
        k.wait("pe", [t_a[h], tt["v"]] + ([b.free] if i == 0 else []))
        mm(b.ap[o:o + 64, 0:256], V[:, 0, 64 * h:64 * h + 64], at_[i][:, 0:256], True)
        t = pe([], lambda e: mm(b.ap[o:o + 64, 128:256], V[:, 1, 64 * h:64 * h + 64], at_[i][:, 256:384], False))
        a_free[i] = t
        if i:
            j = h // 2
            t1 = act([t], lambda e: e.activation(qT[:, j, :], b.ap[:, 0:256], ACT.Copy))
            t2 = act([sq_state["free"]], lambda e: e.activation(sqb[0], b.ap[:, 0:256], ACT.Square))
            b.free = [t2]
            sq_state["pend"] = (j, t2)

    def at_sum():
        if sq_state["pend"] is None:
            return
        j, t = sq_state["pend"]
        sq_state["pend"] = None
        k.wait("pe", [t, t_cst] + ([bank[7].free] if j == 0 else []))
        sq_state["free"] = pe([], lambda e: mm(bank[7].ap[:, 0:256], ones, sqb[0], j == 0, j == 7))

    step = [0]

    def attend():
        i = step[0]
        step[0] += 1
        at_sum()
        for h in (2 * i - 4, 2 * i - 3):
            if 0 <= h < 16:
                at_values(h)
        for h in (2 * i - 2, 2 * i - 1):
            if 0 <= h < 16:
                at_logs(h)
        for h in (2 * i, 2 * i + 1):
            if h < 16:
                at_scores(h)

    def ev_z(n, b, t):
        r = act([t], lambda e: e.activation(Z[:, :, n:n + 256], b.rearrange("p (a b) -> p a b", a=2), ACT.Copy))
        attend()
        tt["z"] = r
        return r

    t_pad = pool([t_pg], lambda e: e.memset(ar(11520, 3, 259)[:, :, 0:3], 0.0))
    raw_free = [None] * 3
    t_xc = {}

    def ev_x(n, b, t):
        for r in range(2):
            c = n + r
            x = raw[c % 3]
            t1 = act([t, raw_free[c % 3], t_pad], lambda e: e.activation(x[:, 3:259], b[:, r * 256:r * 256 + 256],
                                                                         ACT.Copy))
            u = dve([t1], lambda e: e.tensor_scalar(xc[:, c, :], x[:, 0:256], pg("conv_w0", c), pg("conv_b", c),
                                                    ALU.mult, ALU.add))
            for q in (1, 2, 3):
                u = dve([u], lambda e: e.scalar_tensor_tensor(out=xc[:, c, :], in0=x[:, q:q + 256],
                                                              scalar=pg("conv_w%d" % q, c), in1=xc[:, c, :],
                                                              op0=ALU.mult, op1=ALU.add))
            raw_free[c % 3] = t_xc[c] = u
        attend()
        return t1

    state["hi"] = "dve"
    product_N(1024, NT, nt, two, ev_z)
    product_T(12, NT, nt, two, ev_x)

    dt, adt, na = sm(32).rearrange("p (c h) -> p c h", c=2), sm(32).rearrange("p (c h) -> p c h", c=2), sm(16)
    dtmp = sm(32).rearrange("p (c h) -> p c h", c=2)
    wdec, eacs = sm(16), sm(16)

    def ev_dt(n, b, t):
        v = b[:, 0:32].rearrange("p (c h) -> p c h", c=2)
        t1 = dve([t, t_b], lambda e: e.tensor_tensor(dt, v, dtb.unsqueeze(1).broadcast_to([P, 2, 16]), ALU.add))
        ta = act([t_b], lambda e: e.activation(na, alog, ACT.Exp))
        _, t2 = softplus(adt, dtmp, dt, [t1], None)
        t3 = dve([t2], lambda e: e.tensor_copy(dt, adt))
        t3 = dve([t3, ta], lambda e: e.scalar_tensor_tensor(out=adt, in0=dt, scalar=-1.0,
                                                            in1=na.unsqueeze(1).broadcast_to([P, 2, 16]),
                                                            op0=ALU.mult, op1=ALU.mult))
        tt["dt"] = t3
        return t1

    b = two.take()
    k.wait("pe", [t_wdt, b.free])
    for half in range(2):
        for c in range(8):
            for q in range(2):
                ins = mm(b.ap[:, half * 16:half * 16 + 16], NT[q][:, c, half * 128:half * 128 + 128].bitcast(F32),
                         wdt[:, c, :], c == 0 and q == 0, c == 7 and q == 1)
    t = k.mark(k.sem["pe"], ins, 1)
    b.free = [ev_dt(0, b.ap, t)]
    while step[0] < 11:
        attend()
    state["hi"] = "act"

    rbc = sqb[0]
    t = dve([sq_state["free"]], lambda e: e.tensor_scalar(rbc, bank[7].ap[:, 0:256], 1.0 / D, EPS, ALU.mult, ALU.add))
    bank[7].free = [t]
    t = act([t], lambda e: e.activation(rbc, rbc, ACT.Sqrt))
    t = dve([t], lambda e: e.reciprocal(rbc, rbc))
    for j in range(8):
        u = dve([t], lambda e: e.scalar_tensor_tensor(out=qT[:, j, :], in0=qT[:, j, :],
                                                      scalar=pg("attn_norm_g", j), in1=rbc, op0=ALU.mult,
                                                      op1=ALU.mult))
        t_catA = split(catA[0][:, j, :], catA[1][:, j, :], qT[:, j, :], [u])

    for a in (8, 0):
        t = act([t_xc[11]], lambda e: e.activation(xc[:, a:a + (4 if a else 8), :], xc[:, a:a + (4 if a else 8), :],
                                                   ACT.Silu))
        for c in range(a, a + (4 if a else 8)):
            t_xc[c] = t
    tt["z"] = act([tt["z"]], lambda e: e.activation(Z, Z, ACT.Silu))
    for c in range(0, 8, 2):
        b = b47.take()
        k.wait("pe", [b.free, t_xc[c + 1]])
        for half in range(2):
            for r in range(2):
                ins = nc.tensor.transpose(b.ap[:, half * 256 + r * 128:half * 256 + r * 128 + 128],
                                          xc[:, c + r, half * 128:half * 128 + 128], ident)
        t = k.mark(k.sem["pe"], ins, 1)
        t_xn = act([t], lambda e: e.activation(xn[:, :, c * 128:c * 128 + 256],
                                               b.ap.rearrange("p (a b) -> p a b", a=2), ACT.Copy))
        b.free = [t_xn]
    b = b47.take()
    k.wait("pe", [b.free, t_xc[11]])
    for g in range(2):
        ins = nc.tensor.transpose(b.ap[:, g * 128:g * 128 + 128], xc[:, 8 + g, 0:128], ident)
    t = k.mark(k.sem["pe"], ins, 1)
    t_bn = act([t], lambda e: e.activation(bn, b.ap[:, 0:256], ACT.Copy))
    b.free = [t_bn]

    b = b47.take()
    k.wait("pe", [b.free, tt["dt"]])
    mm(b.ap[:, 0:16], tri_le, adt[:, 1, :], True)
    t = pe([], lambda e: mm(b.ap[:, 16:32], tri_gt, adt[:, 0, :], False))
    act([t], lambda e: e.activation(eacs, b.ap[:, 0:16], ACT.Exp))
    t = act([], lambda e: e.activation(wdec, b.ap[:, 16:32], ACT.Exp))
    b.free = [t]
    t_w = dve([t], lambda e: e.tensor_tensor(wdec, wdec, dt[:, 0, :], ALU.mult))

    cb = ar(13322, 4, P)
    b = b47.take()
    k.wait("pe", [b.free, t_sp[15]])
    for c in range(2):
        for g in range(2):
            ins = mm(b.ap[:, (2 * c + g) * 128:(2 * c + g) * 128 + 128], xc[:, 8 + g, c * 128:c * 128 + 128],
                     xc[:, 10 + g, c * 128:c * 128 + 128], True)
    t = k.mark(k.sem["pe"], ins, 1)
    t_cb = dve([t], lambda e: e.tensor_tensor(cb, b.ap.rearrange("p (a b) -> p a b", a=4),
                                              tri_le.unsqueeze(1).broadcast_to([P, 4, P]), ALU.mult))
    b.free = [t_cb]

    xw = ar(0, D)
    st = ar(1024, D)
    t_xw = pool([t_w, t_xn, t_catA], lambda e: e.tensor_tensor(xw.rearrange("p (h d) -> p h d", h=16),
                                                       xn[:, 0, :].rearrange("p (h d) -> p h d", h=16),
                                                       wdec.unsqueeze(2).broadcast_to([P, 16, 64]), ALU.mult))
    Y = XN
    t_y = {}
    for c in range(2):
        t_y[c] = pool([], lambda e: e.tensor_tensor(Y[:, c, :].rearrange("p (h d) -> p h d", h=16),
                                                    xn[:, c, :].rearrange("p (h d) -> p h d", h=16),
                                                    dsk.unsqueeze(2).broadcast_to([P, 16, 64]), ALU.mult))
    for g in range(2):
        b = b47.take()
        k.wait("pe", [b.free, t_xw, t_bn])
        t = pe([], lambda e: mm(b.ap, bn[:, g * 128:g * 128 + 128], xw[:, g * 512:g * 512 + 512], True))
        t_st = act([t], lambda e: e.activation(st[:, g * 512:g * 512 + 512], b.ap, ACT.Copy))
        b.free = [t_st]

    Mb = [ar(2048 + 512 * i, 4, P) for i in range(2)]
    Lb = [ar(3072 + 512 * i, 4, P) for i in range(2)]
    Gb = [ar(12298 + 512 * i, 4, P) for i in range(2)]
    tmp = ar(13834, 512)
    m_free, l_free, g_free = [None] * 2, [None] * 2, [None] * 2
    n = 0
    tmp_free = None
    yb = Banks([bank[6], bank[7]])
    ss2, ms2, rs2 = sm(4), sm(4), sm(4)
    t_catB = []
    quad, ybank = {}, {}

    def decays(n):
        c, g, hq, i = n // 4, (n // 2) % 2, n % 2, n % 2
        h0 = 8 * g + 4 * hq
        for r in range(4):
            t = dve([tt["dt"], m_free[i]], lambda e: e.tensor_scalar(Mb[i][:, r, :], tri_gt,
                                                                     adt[:, c, h0 + r:h0 + r + 1], None, ALU.mult))
        b = two.take()
        k.wait("pe", [t, b.free])
        for r in range(4):
            ins = mm(b.ap[:, r * 128:r * 128 + 128], Mb[i][:, r, :], tri_le, True)
        t = m_free[i] = k.mark(k.sem["pe"], ins, 1)
        quad[n] = act([t, l_free[i]], lambda e: e.activation(Lb[i], b.ap.rearrange("p (a b) -> p a b", a=4), ACT.Exp))
        b.free = [quad[n]]

    def within(n):
        c, g, hq, i = n // 4, (n // 2) % 2, n % 2, n % 2
        h0 = 8 * g + 4 * hq
        if hq == 0:
            ybank[n // 2] = yb.take()
        y = ybank[n // 2]
        for r in range(4):
            t1 = dve([quad[n], t_cb, g_free[i]], lambda e: e.scalar_tensor_tensor(
                out=Gb[i][:, r, :], in0=Lb[i][:, r, :], scalar=dt[:, c, h0 + r:h0 + r + 1],
                in1=cb[:, 2 * c + g, :], op0=ALU.mult, op1=ALU.mult))
        l_free[i] = t1
        k.wait("pe", [t1, t_xn] + ([y.free] if hq == 0 else []))
        for r in range(4):
            h = h0 + r
            ins = mm(y.ap[:, (h % 8) * 64:(h % 8) * 64 + 64], Gb[i][:, r, :], xn[:, c, h * 64:h * 64 + 64], True)
        g_free[i] = quad[n] = k.mark(k.sem["pe"], ins, 1)

    yn = {}

    def combine(i, tmp_free):
        c, g = i // 2, i % 2
        y = ybank[i]
        Yv = Y[:, c, g * 512:g * 512 + 512]
        if c == 1:
            b = two.take()
            k.wait("pe", [b.free, t_st])
            to = pe([], lambda e: mm(b.ap, xc[:, 10 + g, 128:256], st[:, g * 512:g * 512 + 512], True))
        u = dve([quad[2 * i + 1], t_y[c]], lambda e: e.tensor_tensor(Yv, y.ap, Yv, ALU.add))
        y.free = [u]
        if c == 1:
            t = dve([to, tmp_free], lambda e: e.tensor_tensor(
                tmp.rearrange("p (h d) -> p h d", h=8), b.ap.rearrange("p (h d) -> p h d", h=8),
                eacs[:, g * 8:g * 8 + 8].unsqueeze(2).broadcast_to([P, 8, 64]), ALU.mult))
            b.free = [t]
            tmp_free = u = dve([t, u], lambda e: e.tensor_tensor(Yv, Yv, tmp, ALU.add))
        u = dve([u, tt["z"]], lambda e: e.tensor_tensor(Yv, Yv, Z[:, c, g * 512:g * 512 + 512], ALU.mult))
        u = act([u, norm_state["ja"]], lambda e: e.activation(JA[:, 0:512], Yv, ACT.Square, accum_out=ss2[:, i:i + 1]))
        norm_state["ja"] = u
        u = dve([u], lambda e: e.tensor_scalar(ms2[:, i:i + 1], ss2[:, i:i + 1], 1.0 / 512, EPS, ALU.mult, ALU.add))
        u = pool([u], lambda e: e.tensor_tensor(rs2[:, i:i + 1], ms2[:, i:i + 1], half_c[:, 0:1], ALU.pow))
        yn[i] = u
        return tmp_free

    def turn_y(i):
        c, g = i // 2, i % 2
        Yv = Y[:, c, g * 512:g * 512 + 512]
        u = dve([yn[i]], lambda e: e.tensor_scalar(Yv, Yv, rs2[:, i:i + 1], None, ALU.mult))
        b = two.take()
        k.wait("pe", [b.free, u])
        for r in range(4):
            ins = nc.tensor.transpose(b.ap[:, r * 128:r * 128 + 128], Yv[:, r * 128:r * 128 + 128], ident)
        t = k.mark(k.sem["pe"], ins, 1)
        for r in range(4):
            j = 4 * g + r
            u = act([t], lambda e: e.activation(catB[0][:, j, c * 128:c * 128 + 128], b.ap[:, r * 128:r * 128 + 128],
                                                ACT.Copy, scale=pg("ssd_norm_g", j)))
        for r in range(4):
            j = 4 * g + r
            w = dve([u], lambda e: e.scalar_tensor_tensor(
                out=catB[1][:, j, c * 128:c * 128 + 128], in0=b.ap[:, r * 128:r * 128 + 128],
                scalar=pg("ssd_norm_g", j), in1=catB[0][:, j, c * 128:c * 128 + 128].bitcast(F32),
                op0=ALU.mult, op1=ALU.subtract))
        b.free = [w]
        t_catB.append(w)

    decays(0)
    for n in range(8):
        if n < 7:
            decays(n + 1)
        if n % 2 == 0:
            product_acc(n, 16, catA, [t_catA])
        within(n)
        if n >= 2 and n % 2 == 0:
            tmp_free = combine(n // 2 - 1, tmp_free)
        if n >= 3 and n % 2 == 1:
            turn_y(n // 2 - 1)
    tmp_free = combine(3, tmp_free)
    turn_y(3)

    def softmax_rows(S, n_heads, width, scratch, waits, sinks=None):
        mx, sm_, rc, es, _ = scratch
        t = dve([waits], lambda e: e.tensor_reduce(mx, S, AX.X, ALU.max))
        if sinks is not None:
            t = dve([t], lambda e: e.tensor_tensor(mx, mx, sinks, ALU.max))
            t = dve([t], lambda e: e.tensor_tensor(es, sinks, mx, ALU.subtract))
            t_es = act([t], lambda e: e.activation(es, es, ACT.Exp))
        t = dve([t], lambda e: e.tensor_scalar(mx, mx, -1.0, None, ALU.mult))
        for h in range(n_heads):
            te = act([t], lambda e: e.activation(S[:, h, :], S[:, h, :], ACT.Exp, bias=mx[:, h:h + 1],
                                                 accum_out=sm_[:, h:h + 1]))
        if sinks is not None:
            te = dve([te, t_es], lambda e: e.tensor_tensor(sm_, sm_, es, ALU.add))
        t = dve([te], lambda e: e.reciprocal(rc, sm_))
        for h in range(n_heads):
            u = dve([t, te], lambda e: e.tensor_scalar(S[:, h, :], S[:, h, :], rc[:, h:h + 1], None, ALU.mult))
        return u

    M0 = ar(6144, 2, D)
    MT = (YY[:, 0:8, :], YY[:, 8:16, :])
    kTm, Vm, qTm = ar(0, 8, 256), ar(2048, 2, D), ar(8192, 8, 256)
    Sx = [ar(10240 + 1024 * i, 4, 256) for i in range(2)]
    pT = ar(12288, 8, 256)
    oT = (YY[:, 16:24, :], YY[:, 24:32, :])

    def ev_copy(dst, eng, scale=None):
        def f(n, b, t):
            v = b.rearrange("p (a b) -> p a b", a=2)
            if eng == "act":
                tt["cp"] = act([t], lambda e: e.activation(dst[:, n:n + 2, :], v, ACT.Copy, scale=scale or 1.0))
            else:
                tt["cp"] = dve([t], lambda e: e.tensor_copy(dst[:, n:n + 2, :], v))
            return tt["cp"]
        return f

    def ev_nat(dst, key, eng):
        def f(n, b, t):
            v = b.rearrange("p (a b) -> p a b", a=2)
            if eng == "act":
                tt[key] = act([t], lambda e: e.activation(dst[:, :, n:n + 256], v, ACT.Copy))
            else:
                tt[key] = dve([t], lambda e: e.tensor_copy(dst[:, :, n:n + 256], v))
            return tt[key]
        return f

    s_m = k.semaphore("s_m")
    t_m = k.dma("sp", s_m, [t_catB[-1]], M0, A["mem"][0].rearrange("(h p) d -> p h d", p=P))
    ssm, msm, rsm = sm(2), sm(2), sm(2)
    for half in range(2):
        u = act([t_m, norm_state["ja"]], lambda e: e.activation(JA[:, :], M0[:, half, :], ACT.Square,
                                                                accum_out=ssm[:, half:half + 1]))
        norm_state["ja"] = u
        u = dve([u], lambda e: e.tensor_scalar(msm[:, half:half + 1], ssm[:, half:half + 1], 1.0 / D, EPS, ALU.mult,
                                               ALU.add))
        u = pool([u], lambda e: e.tensor_tensor(rsm[:, half:half + 1], msm[:, half:half + 1], half_c[:, 0:1],
                                                ALU.pow))
        t_mn = dve([u], lambda e: e.tensor_scalar(M0[:, half, :], M0[:, half, :], rsm[:, half:half + 1], None,
                                                  ALU.mult))
    t_mt = turn(M0, "mem_g", [t_mn], b47, MT)
    for j in range(8, 16, 2):
        toks = product_acc(j, 16, catB, [t_catB[-1]], j - 8)
    t_h = postnorm("mix_post_g", 1.0, toks)
    product_T(8, MT, t_mt, b47, ev_copy(kTm, "act"))
    t_kTm = tt["cp"]
    product_N(1024, MT, t_mt, b47, ev_nat(Vm, "vm", "act"))
    nt = prenorm(H, "xa_pre_g", t_h, b47)
    product_T(8, NT, nt, ball, ev_copy(qTm, "act", 0.0625))
    t_q = tt["cp"]
    scr = [[sm(8) for _ in range(5)] for _ in range(2)]
    tp = []
    for half in range(2):
        for hp in range(2):
            b = ball.take()
            k.wait("pe", [b.free, t_q, t_kTm])
            for r in range(2):
                h = 2 * hp + r
                for dt_ in range(2):
                    ins = mm(b.ap[:, r * 256:r * 256 + 256], qTm[:, 2 * h + dt_, half * 128:half * 128 + 128],
                             kTm[:, 2 * h + dt_, :], dt_ == 0, dt_ == 1)
            t = k.mark(k.sem["pe"], ins, 1)
            t = dve([t], lambda e: e.tensor_copy(Sx[half][:, 2 * hp:2 * hp + 2, :],
                                                 b.ap.rearrange("p (a b) -> p a b", a=2)))
            b.free = [t]
        tp.append(softmax_rows(Sx[half], 4, 256, [x[:, 0:4] for x in scr[half]], [t]))
    for h in range(4):
        b = ball.take()
        k.wait("pe", [b.free, tp])
        for mt in range(2):
            for half in range(2):
                ins = nc.tensor.transpose(b.ap[:, mt * 256 + half * 128:mt * 256 + half * 128 + 128],
                                          Sx[half][:, h, mt * 128:mt * 128 + 128], ident)
        t = k.mark(k.sem["pe"], ins, 1)
        if h % 2:
            t = act([t], lambda e: e.activation(pT[:, 2 * h:2 * h + 2, :], b.ap.rearrange("p (a b) -> p a b", a=2),
                                                ACT.Copy))
        else:
            t = dve([t], lambda e: e.tensor_copy(pT[:, 2 * h:2 * h + 2, :],
                                                 b.ap.rearrange("p (a b) -> p a b", a=2)))
        b.free = [t]
        b = ball.take()
        k.wait("pe", [b.free, t, tt["vm"]])
        for dt_ in range(2):
            for mt in range(2):
                ins = mm(b.ap[:, dt_ * 256:dt_ * 256 + 256],
                         Vm[:, mt, h * 256 + dt_ * 128:h * 256 + dt_ * 128 + 128], pT[:, 2 * h + mt, :],
                         mt == 0, mt == 1)
        t = k.mark(k.sem["pe"], ins, 1)
        t_o = split(oT[0][:, 2 * h:2 * h + 2, :], oT[1][:, 2 * h:2 * h + 2, :],
                    b.ap.rearrange("p (a b) -> p a b", a=2), [t])
        b.free = [t_o]
    for j in range(0, 8, 2):
        toks = product_acc(j, 8, oT, [t_o])
    t_h = postnorm("xa_post_g", 1.0, toks)
    nt = prenorm(H, "ffn2_pre_g", t_h, ball)
    bias = ar(10752, 8, 256)
    di = AR[:, 12800:13056].bitcast(mybir.dt.int32)
    df, ng = ar(13056, 256), ar(13312, 256)
    t = pool([t_h], lambda e: e.iota(di, pattern=[[-1, 256]], base=128, channel_multiplier=1))
    t = pool([t], lambda e: e.tensor_copy(df, di))
    t = pool([t], lambda e: e.memset(ng, 0.0))
    t = pool([t], sel(ng, 128, [[-1, 256]], 1, ALU.is_ge, -1e30))
    t = pool([t], sel(ng, 0, [[1, 256]], -1, ALU.is_gt, -1e30))
    for h in range(8):
        t_bias = dve([t], lambda e: e.scalar_tensor_tensor(out=bias[:, h, :], in0=df, scalar=-(2.0 ** -(h + 1)),
                                                           in1=ng, op0=ALU.mult, op1=ALU.add))
    t_h = ffn(nt, "ffn2_post_g")

    nt = prenorm(H, "norm_mix_g_2", t_h, ball)
    aq, ak, av = ar(0, 4, 256), ar(1024, 256), ar(1280, 2, 128)
    hq, kn, lf, hv, hg = ar(1536, 4, 256), ar(2560, 2, 512), ar(3584, 2, 512), ar(4608, 2, 512), ar(5632, 4, 256)
    eb, kinv, kd, aT = ar(6656, 4, 256), ar(7680, 4, 256), ar(8704, 2, 512), ar(9728, 2, 4, P)
    ga, gh = ar(10752, 8, 256), ar(2560, 8, 256)
    ST = ar(12800, 2, 4, P)
    S0, S1 = ar(6656, 8, 128), ar(7680, 8, 256)
    pT2 = ar(9728, 8, 3, P)
    ya, yh = (YY[:, 0:4, :], YY[:, 4:8, :]), (YY[:, 8:12, :], YY[:, 12:16, :])

    for jp in range(2):
        p = take(8, 256)
        b = ball.take()
        k.wait("pe", [b.free, nt, p[3]])
        for r in range(2):
            a = 128 * r
            for c in range(8):
                ins = mm3(b.ap[:, r * 256:r * 256 + 256], p[1][:, c, a:a + 128], p[2][:, c, a:a + 128], NT,
                          lambda v: v[:, c, :], c == 0, c == 7)
        t = k.mark(k.sem["pe"], ins, 1)
        release(p, t)
        t_aq = act([t], lambda e: e.activation(aq[:, 2 * jp:2 * jp + 2, :],
                                               b.ap.rearrange("p (a b) -> p a b", a=2), ACT.Copy, scale=0.125))
        b.free = [t_aq]
    p = take(8, 256)
    b = ball.take()
    k.wait("pe", [b.free, p[3]])
    for c in range(8):
        mm3(b.ap[:, 0:256], p[1][:, c, 0:128], p[2][:, c, 0:128], NT, lambda v: v[:, c, :], c == 0, c == 7)
    for half in range(2):
        for c in range(8):
            ins = mm3(b.ap[:, 256 + half * 128:384 + half * 128], p[1][:, c, 128:256], p[2][:, c, 128:256], NT,
                      lambda v: v[:, c, half * 128:half * 128 + 128], c == 0, c == 7, True)
    t = k.mark(k.sem["pe"], ins, 1)
    release(p, t)
    act([t], lambda e: e.activation(ak, b.ap[:, 0:256], ACT.Copy))
    t_av = act([], lambda e: e.activation(av, b.ap[:, 256:512].rearrange("p (a b) -> p a b", a=2), ACT.Copy))
    b.free = [t_av]

    t_s = [None, None]
    for h in range(8):
        o, j = 64 * (h // 4), h % 4
        b = ball.take()
        k.wait("pe", [b.free, t_aq, t_av])
        mm(b.ap[:, 0:128], aq[o:o + 64, j, 0:128], ak[o:o + 64, 0:128], True)
        t = pe([], lambda e: mm(b.ap[:, 128:384], aq[o:o + 64, j, 128:256], ak[o:o + 64, 0:256], False))
        t_s[0] = dve([t, t_bias], lambda e: e.tensor_tensor(S0[:, h, :], b.ap[:, 0:128], bias[:, h, 128:256], ALU.add))
        t_s[1] = dve([], lambda e: e.tensor_tensor(S1[:, h, :], b.ap[:, 128:384], bias[:, h, :], ALU.add))
        b.free = [t_s[1]]

    def ev_f(n, b, t):
        v = b.rearrange("p (a b) -> p a b", a=2)
        lb = LB[:, 0, n:n + 256].unsqueeze(1).broadcast_to([P, 2, 256])
        om = LB[:, 1, n:n + 256].unsqueeze(1).broadcast_to([P, 2, 256])
        kk, ll = kn[:, :, n:n + 256], lf[:, :, n:n + 256]
        r = act([t], lambda e: e.activation(kk, v, ACT.Sigmoid))
        t = dve([r, t_lb], lambda e: e.tensor_tensor(kk, kk, om, ALU.mult))
        t = dve([t], lambda e: e.tensor_tensor(ll, kk, lb, ALU.add))
        tt["kn"] = dve([t], lambda e: e.tensor_scalar(kk, ll, -1.0, 1.0, ALU.mult, ALU.add))
        tt["lf"] = act([tt["kn"]], lambda e: e.activation(ll, ll, ACT.Ln))
        return r

    product_N(512, NT, nt, ball, ev_f)
    product_N(512, NT, nt, ball, ev_nat(hv, "hv", "act"))

    def ev_silu(dst, key, func):
        def f(n, b, t):
            tt[key] = act([t, tt.get("over")], lambda e: e.activation(dst[:, n:n + 2, :],
                                                                      b.rearrange("p (a b) -> p a b", a=2), func))
            return tt[key]
        return f

    t_p = [softmax_rows(S0, 8, 128, scr[0], [t_s[0]], sink), softmax_rows(S1, 8, 256, scr[1], [t_s[1]], sink)]
    product_T(4, NT, nt, ball, ev_silu(hq, "hq", ACT.Silu))
    product_T(4, NT, nt, ball, ev_silu(hg, "hg", ACT.Silu))

    for h in range(8):
        b = ball.take()
        k.wait("pe", [b.free, t_p])
        nc.tensor.transpose(b.ap[:, 0:128], S1[:, h, 0:128], ident)
        nc.tensor.transpose(b.ap[:, 128:256], S1[:, h, 128:256], ident)
        t = pe([], lambda e: e.transpose(b.ap[:, 256:384], S0[:, h, :], ident))
        v = b.ap[:, 0:384].rearrange("p (a b) -> p a b", a=3)
        if h % 2:
            t_pt = act([t], lambda e: e.activation(pT2[:, h, :, :], v, ACT.Copy))
            t_pa = t_pt
        else:
            t_pt = dve([t], lambda e: e.tensor_copy(pT2[:, h, :, :], v))
            t_pd = t_pt
        b.free = [t_pt]
    for jp in range(2):
        b = ball.take()
        k.wait("pe", [b.free, t_pa, t_pd])
        for r in range(2):
            for q in range(2):
                h = 2 * (2 * jp + r) + q
                o, g = 64 * q, h // 4
                c0 = r * 256
                mm(b.ap[o:o + 64, c0:c0 + 128], av[:, 0, g * 64:g * 64 + 64], pT2[:, h, 2, :], r == 0)
                mm(b.ap[o:o + 64, c0 + 128:c0 + 256], av[:, 0, g * 64:g * 64 + 64], pT2[:, h, 0, :], False)
                ins = mm(b.ap[o:o + 64, c0 + 128:c0 + 256], av[:, 1, g * 64:g * 64 + 64], pT2[:, h, 1, :], False)
        t = k.mark(k.sem["pe"], ins, 1)
        t_ya = split(ya[0][:, 2 * jp:2 * jp + 2, :], ya[1][:, 2 * jp:2 * jp + 2, :],
                     b.ap.rearrange("p (a b) -> p a b", a=2), [t])
        b.free = [t_ya]
    tt["over"] = t_ya

    t_z = pool([t_ya], lambda e: e.memset(aT, 0.0))
    for jp in range(2):
        b = ball.take()
        k.wait("pe", [b.free, tt["lf"], t_cst])
        for r in range(2):
            h = 2 * jp + r
            for half in range(2):
                ins = mm(b.ap[:, r * 256 + half * 128:r * 256 + half * 128 + 128],
                         lf[:, half, h * 128:h * 128 + 128], bt_le, True)
        t = k.mark(k.sem["pe"], ins, 1)
        v = b.ap.rearrange("p (a b) -> p a b", a=2)
        act([t, t_ya], lambda e: e.activation(eb[:, 2 * jp:2 * jp + 2, :], v, ACT.Exp))
        t_eb = act([], lambda e: e.activation(kinv[:, 2 * jp:2 * jp + 2, :], v, ACT.Exp, scale=-1.0))
        b.free = [t_eb]
        b = ball.take()
        k.wait("pe", [b.free, tt["kn"]])
        for r in range(2):
            h = 2 * jp + r
            for half in range(2):
                ins = nc.tensor.transpose(b.ap[:, r * 256 + half * 128:r * 256 + half * 128 + 128],
                                          kn[:, half, h * 128:h * 128 + 128], ident)
        t = k.mark(k.sem["pe"], ins, 1)
        v2 = b.ap.rearrange("p (a b) -> p a b", a=2)
        t_ki = dve([t, t_eb], lambda e: e.tensor_tensor(kinv[:, 2 * jp:2 * jp + 2, :], v2,
                                                        kinv[:, 2 * jp:2 * jp + 2, :], ALU.mult))
        b.free = [t_ki]
        t_qd = pool([t_eb, tt["hq"]], lambda e: e.tensor_tensor(hq[:, 2 * jp:2 * jp + 2, :],
                                                                hq[:, 2 * jp:2 * jp + 2, :],
                                                                eb[:, 2 * jp:2 * jp + 2, :], ALU.mult))
    for half in range(2):
        b = ball.take()
        k.wait("pe", [b.free])
        t = pe([], lambda e: mm(b.ap, bt_gt, lf[:, half, :], True))
        t = act([t], lambda e: e.activation(kd[:, half, :], b.ap, ACT.Exp))
        b.free = [t]
        t_gt = t
        t_kd = pool([t, tt["kn"]], lambda e: e.tensor_tensor(kd[:, half, :], kd[:, half, :], kn[:, half, :],
                                                             ALU.mult))
    b67 = Banks(bank[6:8])
    ob = [bank[4], bank[5]]
    for half in range(2):
        b = bank[half]
        k.wait("pe", [b.free, t_ki, t_qd])
        for h in range(4):
            ins = mm(b.ap[:, h * 128:h * 128 + 128], kinv[:, h, half * 128:half * 128 + 128],
                     hq[:, h, half * 128:half * 128 + 128], True)
        t = k.mark(k.sem["pe"], ins, 1)
        m = bt_le.bitcast(U32).unsqueeze(1).broadcast_to([P, 4, P])
        t_aT = dve([t, t_z, t_cst], lambda e: e.copy_predicated(aT[:, half, :, :], m,
                                                                b.ap.rearrange("p (a b) -> p a b", a=4)))
        b.free = [t_aT]

    rec = {"c": 0, "s": None, "free": [None, None]}

    def additions(c):
        b = bank[c % 4]
        half, r = c // 4, 32 * (c % 4)
        k.wait("pe", [b.free, t_kd, tt["hv"]])
        for h in range(4):
            ins = mm(b.ap[:, h * 128:h * 128 + 128], kd[r:r + 32, half, h * 128:h * 128 + 128],
                     hv[r:r + 32, half, h * 128:h * 128 + 128], True)
        t = k.mark(k.sem["pe"], ins, 1)
        if c == 0:
            u = dve([t, t_ya], lambda e: e.tensor_copy(ST[:, 0, :, :], b.ap.rearrange("p (a b) -> p a b", a=4)))
        else:
            for h in range(4):
                u = dve([t, rec["s"], rec["free"][c % 2]], lambda e: e.scalar_tensor_tensor(
                    out=ST[:, c % 2, h, :], in0=ST[:, (c - 1) % 2, h, :], scalar=eb[:, h, 32 * c + 31:32 * c + 32],
                    in1=b.ap[:, h * 128:h * 128 + 128], op0=ALU.mult, op1=ALU.add))
        rec["s"] = u
        b.free = [u]

    def inside():
        k.wait("pe", [ob[0].free, ob[1].free, t_aT, tt["hv"]])
        for h in range(4):
            for half in range(2):
                c0 = (h % 2) * 256 + half * 128
                mm(ob[h // 2].ap[:, c0:c0 + 128], hv[:, half, h * 128:h * 128 + 128], aT[:, half, h, :],
                   c0 == 0)

    def across(c):
        k.wait("pe", [rec["s"]])
        for h in range(4):
            c0 = (h % 2) * 256 + 32 * c
            ins = mm(ob[h // 2].ap[:, c0:c0 + 32], ST[:, (c - 1) % 2, h, :], hq[:, h, 32 * c:32 * c + 32], False)
        t = k.mark(k.sem["pe"], ins, 1)
        rec["free"][(c - 1) % 2] = t
        return t

    def ev_ga(n, b, t):
        tt["ga"] = act([t, t_ya], lambda e: e.activation(ga[:, n:n + 2, :], b.rearrange("p (a b) -> p a b", a=2),
                                                         ACT.Sigmoid))
        if n:
            across(n // 2)
        additions(n // 2)
        if n == 0:
            inside()
        return tt["ga"]

    def ev_gh(n, b, t):
        tt["gh"] = act([t, t_kd, t_ki, t_gt], lambda e: e.activation(gh[:, n:n + 2, :],
                                                                     b.rearrange("p (a b) -> p a b", a=2),
                                                                     ACT.Sigmoid))
        tt["o"] = across(4 + n // 2)
        if n < 6:
            additions(4 + n // 2)
        return tt["gh"]

    product_T(8, NT, nt, b67, ev_ga)
    product_T(8, NT, nt, b67, ev_gh)
    for jp in range(2):
        b = ob[jp]
        u = act([tt["o"], norm_state["ja"]], lambda e: e.activation(JA[:, 0:512], b.ap, ACT.Square))
        norm_state["ja"] = u
        b2 = bank[jp]
        k.wait("pe", [b2.free, u])
        t = pe([], lambda e: mm(b2.ap, ones, JA[:, 0:512], True))
        rb = kinv[:, 2 * jp:2 * jp + 2, :]
        t = dve([t, t_aT], lambda e: e.tensor_scalar(rb, b2.ap.rearrange("p (a b) -> p a b", a=2), 1.0 / 128, EPS,
                                                     ALU.mult, ALU.add))
        b2.free = [t]
        t = act([t], lambda e: e.activation(rb, rb, ACT.Sqrt))
        t = dve([t], lambda e: e.reciprocal(rb, rb))
        t = dve([t, u], lambda e: e.scalar_tensor_tensor(out=rb, in0=b.ap.rearrange("p (a b) -> p a b", a=2),
                                                         scalar=pg("hgrn_norm_g_2", 0), in1=rb, op0=ALU.mult,
                                                         op1=ALU.mult))
        b.free = [t]
        norm_state["ja"] = [u, t]
        t = dve([t, tt["hg"]], lambda e: e.tensor_tensor(rb, rb, hg[:, 2 * jp:2 * jp + 2, :], ALU.mult))
        t_yh = split(yh[0][:, 2 * jp:2 * jp + 2, :], yh[1][:, 2 * jp:2 * jp + 2, :], rb, [t])
    mt = [ar(8704 + 256 * i, 256) for i in range(4)]
    mfree = [None] * 4
    for n0 in range(0, 8, 4):
        bb, tb = [b47.take() for _ in range(4)], [None] * 4
        for q, (x, w) in enumerate(((ya, t_ya), (yh, t_yh))):
            p = take(4, 512)
            for r in range(4):
                k.wait("pe", [bb[r].free, p[3], w])
                for c in range(4):
                    ins = mm3(bb[r].ap[:, q * 256:q * 256 + 256], p[1][:, c, r * 128:r * 128 + 128],
                              p[2][:, c, r * 128:r * 128 + 128], x, lambda v: v[:, c, :], c == 0, c == 3)
                tb[r] = k.mark(k.sem["pe"], ins, 1)
            release(p, tb[3])
        for r in range(4):
            n, b, t = n0 + r, bb[r], tb[r]
            m = mt[n % 4]
            u1 = dve([t, tt["ga"], tt["gh"]], lambda e: e.tensor_tensor(b.ap[:, 0:256], b.ap[:, 0:256], ga[:, n, :],
                                                                        ALU.mult))
            u = dve([mfree[n % 4]], lambda e: e.tensor_tensor(m, b.ap[:, 256:512], gh[:, n, :], ALU.mult))
            u = dve([u1, u], lambda e: e.tensor_tensor(m, b.ap[:, 0:256], m, ALU.add))
            b.free = [u]
            t_m = mfree[n % 4] = split(NT[0][:, n, :], NT[1][:, n, :], m, [u])
    keys = ar(4096, 16, P)
    s_keys = k.semaphore("s_keys")
    t_kraw = k.dma("act", s_keys, [t_yh, tt["o"], tt["gh"], t_m], keys,
                   A["peer_keys_2"][0].rearrange("a h n d -> n (a h) d"))
    for j in range(0, 8, 2):
        toks = product_acc(j, 8, NT, [t_m])
    t_h = []
    for half in range(2):
        acc = ps[:, 2 * half:2 * half + 2, :].rearrange("p a b -> p (a b)")
        t = dve([toks[half]], lambda e: e.tensor_tensor(H[:, half, :], acc, H[:, half, :], ALU.add))
        bank[2 * half].free = [t]
        bank[2 * half + 1].free = [t]
        t_h.append(t)

    keysT, qp = ar(0, 16, P), ar(2048, 16, 256)
    SC = [ar(6144 + 2048 * i, 16, P) for i in range(2)]
    v = keys
    for q in range(4):
        b = b47.take()
        k.wait("pe", [b.free, t_kraw, t_h])
        for r in range(4):
            ins = nc.tensor.transpose(b.ap[:, r * 128:r * 128 + 128], v[:, 4 * q + r, :], ident)
        t = k.mark(k.sem["pe"], ins, 1)
        t_keys = act([t], lambda e: e.activation(keysT[:, 4 * q:4 * q + 4, :],
                                                 b.ap.rearrange("p (a b) -> p a b", a=4), ACT.Copy))
        b.free = [t_keys]
    ts = []
    for half in range(2):
        _, t = rstd(half, H[:, half, :], D, [t_h, norm_state["rs"]])
        g, t_row = row_gain["norm_ffn_g_2"]
        ts.append(dve([t, t_row], lambda e: e.scalar_tensor_tensor(out=XN[:, half, :], in0=H[:, half, :],
                                                                   scalar=rs[:, half:half + 1], in1=g,
                                                                   op0=ALU.mult, op1=ALU.mult)))
    nt = turn(XN, None, ts, ball)
    product_T(16, NT, nt, ball, ev_copy(qp, "act"))
    t_q = tt["cp"]
    t_sc = {}
    for half in range(2):
        for q in range(4):
            b = ball.take()
            k.wait("pe", [b.free, t_q, t_keys])
            for r in range(4):
                i = 4 * q + r
                ins = mm(b.ap[:, r * 128:r * 128 + 128], qp[:, i, half * 128:half * 128 + 128],
                         keysT[:, (i % 2) * 8 + i // 2, :], True)
            t_pq = t = k.mark(k.sem["pe"], ins, 1)
            t_sc[half, q] = act([t], lambda e: e.activation(SC[half][:, 4 * q:4 * q + 4, :],
                                                            b.ap.rearrange("p (a b) -> p a b", a=4), ACT.Copy))
            b.free = [t_sc[half, q]]

    at = [10240]

    def a2(*shape):
        n = 1
        for x in shape:
            n *= x
        o = at[0]
        at[0] += n
        return ar(o, *shape)

    def a2u(n):
        o = at[0]
        at[0] += n
        return AU[:, o:o + n]

    iot = a2(16)
    ioti = AR[:, at[0]:at[0] + 16].bitcast(mybir.dt.int32)
    at[0] += 16
    t = pool([t_pq], lambda e: e.iota(ioti, pattern=[[1, 16]], base=0, channel_multiplier=0))
    t_iota = pool([t], lambda e: e.tensor_copy(iot, ioti))
    UB = 3
    un = []
    for i in range(UB):
        un.append(dict(V=a2(2, 16), I=a2u(32), IF=a2(2, 16), best=a2(16), pos=a2u(16), pp=a2u(32), pf=a2(2, 16),
                       sel=a2(2, 16), idx=a2u(16), e=a2(16), s=a2(1), r=a2(1), nb=a2(1), a=a2(16), g=a2(16),
                       w=a2(16)))
    cand = [ar(0, 256), ar(256, 256)]
    oh = ar(512, 2, 16, 16)
    diag = [ar(1024 + 128 * i, P) for i in range(8)]
    wctx.close()
    GS = sb("GS", [P, 26, D])
    gs = [Slot(GS[:, i, :], k.semaphore(f"gather{i}")) for i in range(26)]
    ngs = [0]

    def gather(table, idx, waits):
        s = gs[ngs[0] % len(gs)]
        ngs[0] += 1
        k.wait("pool", [s.free, waits])
        ins = nc.gpsimd.indirect_dma_start(s.ap, None, table, bass.IndirectOffsetOnAxis(idx, 0))
        return s, k.mark(s.sem, ins, 16)

    def choose(n):
        half, head = n // 8, n % 8
        x = un[n % UB]
        free = [unit_done.get(n - UB)]

        def step(waits, f):
            return dve(waits, f)

        def top16(src, v, i, waits):
            t = step([waits, free], lambda e: e.max(v[:, 0:8], src))
            t1 = step([t], lambda e: e.max_index(i[:, 0:8], v[:, 0:8], src))
            t = step([t, t1], lambda e: e.match_replace(src, v[:, 0:8], src, -3.0e38))
            t = step([t], lambda e: e.max(v[:, 8:16], src))
            return step([t], lambda e: e.max_index(i[:, 8:16], v[:, 8:16], src))

        for a in range(2):
            t = top16(SC[half][:, 2 * head + a, :], x["V"][:, a, :], x["I"][:, 16 * a:16 * a + 16],
                      [t_sc[half, (2 * head + a) // 4], t_pq])
            yield
        ti = step([t], lambda e: e.tensor_copy(x["IF"], x["I"].rearrange("p (a b) -> p a b", a=2)))
        c = cand[n % 2]
        t = step([t], lambda e: e.tensor_tensor(c.rearrange("p (a b) -> p a b", a=16),
                                                x["V"][:, 0, :].unsqueeze(2).broadcast_to([P, 16, 16]),
                                                x["V"][:, 1, :].unsqueeze(1).broadcast_to([P, 16, 16]), ALU.add))
        yield
        t = top16(c, x["best"], x["pos"], [t])
        yield
        u = act([t], lambda e: e.activation(x["nb"], x["best"][:, 0:1], ACT.Copy, scale=-1.0))
        u = act([u], lambda e: e.activation(x["e"], x["best"], ACT.Exp, bias=x["nb"], accum_out=x["s"]))
        step([t], lambda e: e.tensor_scalar(x["pp"][:, 0:16], x["pos"], 4, None, ALU.logical_shift_right))
        t = step([t], lambda e: e.tensor_scalar(x["pp"][:, 16:32], x["pos"], 15, None, ALU.bitwise_and))
        t = step([t], lambda e: e.tensor_copy(x["pf"], x["pp"].rearrange("p (a b) -> p a b", a=2)))
        yield
        t = step([t, t_iota], lambda e: e.tensor_tensor(
            oh, x["pf"].unsqueeze(3).broadcast_to([P, 2, 16, 16]),
            iot.unsqueeze(1).unsqueeze(1).broadcast_to([P, 2, 16, 16]), ALU.is_equal))
        yield
        t = step([t, ti], lambda e: e.tensor_tensor(oh, oh, x["IF"].unsqueeze(2).broadcast_to([P, 2, 16, 16]),
                                                    ALU.mult))
        yield
        t = step([t], lambda e: e.tensor_reduce(x["sel"], oh, AX.X, ALU.add))
        t = step([t], lambda e: e.scalar_tensor_tensor(out=x["idx"], in0=x["sel"][:, 0, :], scalar=128.0,
                                                       in1=x["sel"][:, 1, :], op0=ALU.mult, op1=ALU.add))
        x["t_idx"] = t
        x["t_r"] = step([u], lambda e: e.reciprocal(x["r"], x["s"]))

    U_, V_ = A["peer_u_2"][0], A["peer_v_2"][0]
    unit_done = {}
    acc = {}
    dfree = [None] * 8
    nd = 0
    pieces_done = [s.free for s in slots]
    for g in gs:
        g.free = [t_pq, pieces_done]
    for _ in choose(0):
        pass
    fin = []
    for n in range(17):
        nxt = choose(n + 1) if n + 1 < 16 else iter(())
        half = n // 8
        x = un[n % UB]
        y = un[(n - 1) % UB]
        for kk in range(16):
            if n < 16:
                s, t = gather(U_, x["idx"][:, kk:kk + 1], [x["t_idx"]])
                t = dve([t, ts], lambda e: e.tensor_tensor_reduce(s.ap, s.ap, XN[:, half, :], 1.0, 0.0, ALU.mult,
                                                                  ALU.add, x["a"][:, kk:kk + 1]))
                s.free = [t]
            if n > 0:
                s2, t2 = gather(V_, y["idx"][:, kk:kk + 1], [])
                hv_ = (n - 1) // 8
                d = diag[nd % 8]
                td = act([y["t_w"], dfree[nd % 8]], lambda e: e.activation(d, ident, ACT.Copy,
                                                                            scale=y["w"][:, kk:kk + 1]))
                first, last = (n - 1) % 8 == 0 and kk == 0, (n - 1) % 8 == 7 and kk == 15
                k.wait("pe", [td, t2] + ([bank[4 + 2 * hv_].free, bank[5 + 2 * hv_].free] if first else []))
                for nb in range(2):
                    ins = mm(bank[4 + 2 * hv_ + nb].ap, d, s2.ap[:, nb * 512:nb * 512 + 512], first, last)
                tm = k.mark(k.sem["pe"], ins, 1)
                s2.free = [tm]
                dfree[nd % 8] = tm
                nd += 1
            next(nxt, None)
        for _ in nxt:
            pass
        if n > 0:
            unit_done[n - 1] = tm
        if n < 16:
            t = act([t], lambda e: e.activation(x["g"], x["a"], ACT.Gelu))
            x["t_w"] = dve([t, x["t_r"]], lambda e: e.scalar_tensor_tensor(out=x["w"], in0=x["e"], scalar=x["r"],
                                                                          in1=x["g"], op0=ALU.mult, op1=ALU.mult))
        if n in (8, 16):
            h_ = n // 8 - 1
            av_ = ps[:, 4 + 2 * h_:6 + 2 * h_, :].rearrange("p a b -> p (a b)")
            t = dve([tm], lambda e: e.tensor_tensor(H[:, h_, :], av_, H[:, h_, :], ALU.add))
            _, t = rstd(h_, H[:, h_, :], D, [t, norm_state["rs"]])
            g, t_row = row_gain["norm_final_g_2"]
            fin.append(dve([t, t_row], lambda e: e.scalar_tensor_tensor(out=H[:, h_, :], in0=H[:, h_, :],
                                                                        scalar=rs[:, h_:h_ + 1], in1=g,
                                                                        op0=ALU.mult, op1=ALU.mult)))
    s_o = k.semaphore("s_o")
    for h_ in range(2):
        t = k.dma("sp", s_o, [fin[h_]], out[0, h_ * P:(h_ + 1) * P, :], H[:, h_, :])
    k.wait("sp", [t])


_INS = ['x', 'mem', 'ffn1_pre_g', 'ffn1_w_gu', 'ffn1_w_down', 'ffn1_post_g', 'mix_pre_g', 'w_in', 'conv_w',
        'conv_b', 'dt_bias', 'a_log', 'd_skip', 'ssd_norm_g', 'attn_norm_g', 'w_out', 'mix_post_g', 'xa_pre_g',
        'mem_g', 'xa_wq', 'xa_wkv', 'xa_wo', 'xa_post_g', 'ffn2_pre_g', 'ffn2_w_gu', 'ffn2_w_down', 'ffn2_post_g',
        'norm_mix_g_2', 'w_in_2', 'attn_sinks_2', 'hgrn_lb_logits_2', 'hgrn_norm_g_2', 'w_attn_proj_2',
        'w_hgrn_proj_2', 'w_out_2', 'norm_ffn_g_2', 'w_peer_q_2', 'peer_keys_2', 'peer_u_2', 'peer_v_2',
        'norm_final_g_2']


def kernel(**inputs):
    import numpy as _np
    import concourse.bacc as _bacc
    from concourse import mybir as _mybir
    from concourse.bass_utils import run_bass_kernel_spmd as _run

    nc = _bacc.Bacc("TRN2", target_bir_lowering=False, num_devices=1)
    arrays, args = {}, {}
    for name in _INS:
        a = _np.ascontiguousarray(inputs[name])
        arrays[f"in_{name}_dram"] = a
        args[name] = nc.dram_tensor(f"in_{name}_dram", a.shape, _mybir.dt.from_np(a.dtype),
                                    kind="ExternalInput").ap()
    o = nc.dram_tensor("out_0_dram", (1, T, D), _mybir.dt.float32, kind="ExternalOutput").ap()
    build(nc, args, o)
    r = _run(nc, [arrays], core_ids=[0])
    return r.results[0]["out_0_dram"]
```

```python
from contextlib import ExitStack

import concourse.bass as bass
from concourse import mybir

F32 = mybir.dt.float32
U32 = mybir.dt.uint32
F32R = mybir.dt.float32r
ALU = mybir.AluOpType
ACT = mybir.ActivationFunctionType
AX = mybir.AxisListType

P = 128
D = 1024
T = 256
EPS = 1e-6
NRAW = 4
NCONV = 2
FFN_TILES = 22


class Chip:

    def __init__(self, nc, ctx):
        self.nc = nc
        self.ctx = ctx
        self.count = {}
        self.seen = {}
        self.engine = {"pe": nc.tensor, "dve": nc.vector, "act": nc.scalar, "pool": nc.gpsimd, "sp": nc.sync}
        self.sem = {k: self.semaphore("done_" + k) for k in ("pe", "dve", "act", "pool")}

    def semaphore(self, name):
        s = self.ctx.enter_context(self.nc.semaphore(name))
        self.count[name] = 0
        return (name, s)

    def wait(self, eng, toks):
        for t in toks:
            if t is None:
                continue
            if type(t) is list:
                self.wait(eng, t)
                continue
            (name, s), v = t
            if self.seen.get((eng, name), 0) < v:
                self.seen[(eng, name)] = v
                self.engine[eng].wait_ge(s, v)

    def mark(self, sem, ins, n):
        ins.then_inc(sem[1], n)
        self.count[sem[0]] += n
        return (sem, self.count[sem[0]])

    def dve(self, waits, f):
        self.wait("dve", waits)
        return self.mark(self.sem["dve"], f(self.nc.vector), 1)

    def act(self, waits, f):
        self.wait("act", waits)
        return self.mark(self.sem["act"], f(self.nc.scalar), 1)

    def pool(self, waits, f):
        self.wait("pool", waits)
        return self.mark(self.sem["pool"], f(self.nc.gpsimd), 1)

    def pe(self, waits, f):
        self.wait("pe", waits)
        return self.mark(self.sem["pe"], f(self.nc.tensor), 1)

    def mm(self, out, lhsT, rhs, start, stop=True):
        return self.nc.tensor.matmul(out, lhsT, rhs, start=start, stop=stop, skip_group_check=True)

    def dma(self, eng, sem, waits, out, in_):
        self.wait(eng, waits)
        return self.mark(sem, self.engine[eng].dma_start(out, in_), 16)


class Bank:

    def __init__(self, ap):
        self.ap = ap
        self.free = []


class Banks:
    def __init__(self, banks):
        self.banks = banks
        self.n = 0

    def take(self):
        b = self.banks[self.n % len(self.banks)]
        self.n += 1
        return b


class Slot:
    def __init__(self, ap, sem):
        self.ap = ap
        self.sem = sem
        self.free = []


def build(nc, A, out):
    with ExitStack() as ctx:
        body(nc, ctx, A, out)


def body(nc, ctx, A, out):
    k = Chip(nc, ctx)
    dve, act, pool, pe, mm = k.dve, k.act, k.pool, k.pe, k.mm

    def sb(name, shape, dt=F32):
        return ctx.enter_context(nc.sbuf_tensor(name, shape, dt))

    H = sb("H", [P, 2, D])
    XN = sb("XN", [P, 2, D])
    JA = sb("JA", [P, D])
    GB = sb("GB", [P, 2, D])
    PG = sb("PG", [P, 160])
    cst = sb("cst", [P, 8, P])
    small = sb("small", [P, 512])
    LB = sb("LB", [P, 2, 512])
    AR = sb("AR", [P, 14604])
    AU = AR[:, :].bitcast(U32)
    RAW = sb("RAW", [P, NRAW, 2048])
    wctx = ExitStack()
    YY = wctx.enter_context(nc.sbuf_tensor("YY", [P, 32, T], F32R))

    def operands(n):
        xh, xl = [wctx.enter_context(nc.sbuf_tensor(f"{x}{n}", [P, 8, T], F32R)) for x in ("XH", "XL")]
        wh, wl = [wctx.enter_context(nc.sbuf_tensor(f"{x}{n}", [P, NCONV, 2048], F32R)) for x in ("WH", "WL")]
        return wh, wl, (xh[:, :, :], xl[:, :, :])

    WH, WL, NT = operands(0)
    ps = ctx.enter_context(nc.psum_tensor("ps", [P, 8, 512], F32))
    bank = [Bank(ps[:, i, :]) for i in range(8)]
    slots = [Slot(RAW[:, i, :], k.semaphore(f"raw{i}")) for i in range(NRAW)]
    conv_free = [None] * NCONV

    ident, ones, negtri, negones, tri_le, tri_gt, bt_le, bt_gt = [cst[:, i, :] for i in range(8)]

    smallat = [0]

    def sm(n):
        a = smallat[0]
        smallat[0] += n
        return small[:, a:a + n]

    def ar(off, *shape):
        n = 1
        for s in shape:
            n *= s
        v = AR[:, off:off + n]
        if len(shape) == 2:
            v = v.rearrange("p (a b) -> p a b", a=shape[0])
        if len(shape) == 3:
            v = v.rearrange("p (a b c) -> p a b c", a=shape[0], b=shape[1])
        return v

    def cols(w, a, n):
        return w.rearrange("(c p) n -> p c n", p=P)[:, :, a:a + n]

    def rows(w, j, n):
        return w.rearrange("(j p) n -> p j n", p=P)[:, j:j + n, :]

    plan = []

    def plan_cols(w, a, n, kt=8):
        per = 2048 // kt
        for c in range(a, a + n, per):
            plan.append(cols(w, c, per))

    def plan_rows(w, j0, n):
        for j in range(j0, j0 + n, 2):
            plan.append(rows(w, j, 2))

    def plan_ffn(wgu, wd):
        for i in range(FFN_TILES // 2):
            plan_cols(wgu, i * 256, 256)
            plan_cols(wgu, 2816 + i * 256, 256)
            if i:
                plan_rows(wd, 2 * i - 2, 2)
        plan_rows(wd, FFN_TILES - 2, 2)

    plan_ffn(A["ffn1_w_gu"][0], A["ffn1_w_down"][0])
    plan_cols(A["w_in"][0], 0, 5632)
    unsplit = {len(plan)}
    plan.append(A["mem"][0].rearrange("(h p) d -> p h d", p=P))
    plan_cols(A["xa_wkv"][0], 0, 512)
    for i in range(4):
        plan_rows(A["w_out"][0], 2 * i, 2)
        plan_cols(A["xa_wkv"][0], 512 + 256 * i, 256)
    plan_rows(A["w_out"][0], 8, 8)
    plan_cols(A["xa_wkv"][0], 1536, 512)
    plan_cols(A["xa_wq"][0], 0, 1024)
    plan_rows(A["xa_wo"][0], 0, 8)
    plan_ffn(A["ffn2_w_gu"][0], A["ffn2_w_down"][0])
    w2p = A["w_in_2"][0].rearrange("(c p) n -> p c n", p=P)
    for jp in range(2):
        plan.append((w2p[:, :, jp * 128:jp * 128 + 128], w2p[:, :, 256 + jp * 128:384 + jp * 128]))
    plan_cols(A["w_in_2"][0], 512, 256)
    plan_cols(A["w_in_2"][0], 1280, 1024)
    plan_cols(A["w_in_2"][0], 768, 512)
    plan_cols(A["w_in_2"][0], 2304, 512)
    plan_cols(A["w_in_2"][0], 2816, 2048)
    for n0 in (0, 512):
        plan_cols(A["w_attn_proj_2"][0], n0, 512, 4)
        plan_cols(A["w_hgrn_proj_2"][0], n0, 512, 4)
    plan_rows(A["w_out_2"][0], 0, 8)
    unsplit.add(len(plan))
    plan_cols(A["w_peer_q_2"][0], 0, 2048)

    state = {"hi": "act", "load": 0, "conv": 0, "ready": 0, "take": 0}
    loaded, pieces = {}, {}

    def load_next():
        n = state["load"]
        if n >= len(plan):
            return
        state["load"] += 1
        src = plan[n]
        s = slots[n % NRAW]
        if type(src) is tuple:
            v = s.ap.rearrange("p (k r q n) -> p k r q n", k=8, r=2, q=2)
            for i in range(4):
                tok = k.dma("sp", s.sem, s.free, v[:, :, i // 2, i % 2, :],
                            src[i % 2][:, :, 64 * (i // 2):64 * (i // 2) + 64])
            loaded[n] = (s, s.ap.rearrange("p (k n) -> p k n", k=8), tok)
            return
        kt, w = src.shape[1], src.shape[2]
        v = s.ap[:, 0:kt * w].rearrange("p (k n) -> p k n", k=kt)
        loaded[n] = (s, v, k.dma("sp", s.sem, s.free, v, src))

    def split_next():
        n = state["ready"]
        if n >= len(plan):
            return
        state["ready"] += 1
        load_next()
        s, v, tok = loaded.pop(n)
        i = state["conv"] % NCONV
        state["conv"] += 1
        kt, w = v.shape[1], v.shape[2]
        hi = WH[:, i, 0:kt * w].rearrange("p (k n) -> p k n", k=kt)
        lo = WL[:, i, 0:kt * w].rearrange("p (k n) -> p k n", k=kt)
        if state["hi"] == "act":
            th = act([tok, conv_free[i]], lambda e: e.activation(hi, v, ACT.Copy))
        else:
            th = dve([tok, conv_free[i]], lambda e: e.tensor_copy(hi, v))
        tl = dve([tok, th, conv_free[i]], lambda e: e.tensor_tensor(lo, v, hi.bitcast(F32), ALU.subtract))
        s.free = [th, tl]
        pieces[n] = (i, hi, lo, [th, tl])

    def take(kt, w):
        n = state["take"]
        state["take"] += 1
        if n not in pieces:
            split_next()
        p = pieces.pop(n)
        assert p[1].shape[1] == kt and p[1].shape[2] == w, (n, p[1].shape, kt, w)
        if n + 1 not in pieces and n + 1 not in unsplit:
            split_next()
        return p

    def take_raw():
        state["take"] += 1
        state["ready"] += 1
        load_next()
        return loaded.pop(state["take"] - 1)

    def release(p, t):
        conv_free[p[0]] = t

    def mm3(out, wh, wl, x, cx, first, last, w_moves=False):
        xh, xl = cx(x[0]), cx(x[1])
        for q, (a, b_) in enumerate(((wh, xh), (wh, xl), (wl, xh))):
            if w_moves:
                a, b_ = b_, a
            ins = mm(out, a, b_, first and q == 0, last and q == 2)
        return ins

    s_x, s_x1 = k.semaphore("s_x"), k.semaphore("s_x1")
    t_x = [k.dma(q, s_x if i == 0 else s_x1, [], H[:, i, :], A["x"][0, i * P:(i + 1) * P, :])
           for i, q in ((0, "sp"), (1, "act"))]
    load_next()
    rows1 = AR[:, 0:128]
    rows2 = AR[0:61, 128:256]
    s_g = k.semaphore("s_g")
    col = {}
    at = 0
    t_g = None
    for name, n in (("ffn1_pre_g", 8), ("mix_pre_g", 8), ("xa_pre_g", 8), ("mem_g", 8), ("ffn2_pre_g", 8),
                    ("norm_mix_g_2", 8), ("norm_ffn_g_2", 8), ("attn_norm_g", 8), ("ssd_norm_g", 8),
                    ("conv_b", 12), ("hgrn_norm_g_2", 1)):
        col[name] = at
        t_g = k.dma("sp", s_g, [], AR[at:at + n, 0:128], A[name][0].rearrange("(c p) -> c p", p=P))
        at += n
    n_rows1 = at
    for i in range(4):
        col["conv_w%d" % i] = 112 + 12 * i
    t_g = k.dma("sp", s_g, [], AR[0:48, 128:256], A["conv_w"][0].rearrange("k (c p) -> (k c) p", p=P))

    s_b = k.semaphore("s_b")
    dtb, alog, dsk, sink = sm(16), sm(16), sm(16), sm(8)
    for _ in range(NRAW - 2):
        load_next()

    row_names = ["ffn1_post_g", "mix_post_g", "xa_post_g", "ffn2_post_g", "norm_ffn_g_2", "norm_final_g_2"]
    s_gb = [k.semaphore("s_gb0"), k.semaphore("s_gb1")]
    row_gain = {}

    def load_row_gain(i, waits):
        if i >= len(row_names):
            return
        name = row_names[i]
        src = A[name] if name == "norm_final_g_2" else A[name][0]
        v = GB[:, i % 2, :]
        row_gain[name] = (v, k.dma("sp", s_gb[i % 2], waits, v, src.unsqueeze(0).broadcast_to([P, D])))

    t = pool([], lambda e: e.memset(ident, 0.0))
    t = pool([], lambda e: e.memset(cst[:, 1:3, :], 1.0))
    t = pool([], lambda e: e.memset(cst[:, 3, :], -1.0))
    t = pool([], lambda e: e.memset(cst[:, 4:8, :], 1.0))
    t = pool([t], lambda e: e.memset(negtri, -1.0))

    def sel(v, base, pattern, cm, op, fill=0.0):
        return lambda e: e.affine_select(out=v, in_=v, compare_op=op, fill=fill, base=base, pattern=pattern,
                                         channel_multiplier=cm)

    t_id = pool([t], sel(ident, 0, [[-1, P]], 1, ALU.not_equal, 1.0))
    pool([], sel(negtri, 0, [[-1, P]], 1, ALU.is_ge))
    pool([], sel(tri_le, 0, [[1, P]], -1, ALU.is_ge))
    pool([], sel(tri_gt, 0, [[-1, P]], 1, ALU.is_gt))
    t1 = pool([], sel(bt_le, 0, [[1, P]], -1, ALU.is_ge))
    t2 = pool([], sel(bt_gt, 0, [[-1, P]], 1, ALU.is_gt))
    t1 = pool([t1, t2], sel(bt_le, 0, [[-32, 4], [0, 32]], 1, ALU.is_ge))
    t_cst = pool([t1], sel(bt_gt, 31, [[32, 4], [0, 32]], -1, ALU.is_ge))

    b = bank[0]
    k.wait("pe", [t_id, t_g])
    nc.tensor.transpose(b.ap[:, 0:n_rows1], AR[0:n_rows1, 0:128], ident[0:n_rows1, 0:n_rows1])
    t = pe([], lambda e: e.transpose(b.ap[:, 112:160], AR[0:48, 128:256], ident[0:48, 0:48]))
    dve([t], lambda e: e.tensor_copy(PG[:, 0:n_rows1], b.ap[:, 0:n_rows1]))
    t_pg = dve([], lambda e: e.tensor_copy(PG[:, 112:160], b.ap[:, 112:160]))
    b.free = [t_pg]

    def pg(name, c):
        a = col[name] + c
        return PG[:, a:a + 1]

    ssq = sm(2)
    rs = sm(2)
    msq = sm(2)
    half_c = sm(16)
    eps_c = sm(1)
    pool([], lambda e: e.memset(eps_c, EPS))
    t_hc = pool([], lambda e: e.memset(half_c, -0.5))
    norm_state = {"ja": None, "rs": [None, None]}

    def rstd(half, src, n, waits, coef=1.0):
        i = half
        t = act([waits, norm_state["ja"]], lambda e: e.activation(JA[:, 0:src_len(src)], src, ACT.Square,
                                                                  accum_out=ssq[:, i:i + 1]))
        norm_state["ja"] = t
        t1 = dve([t], lambda e: e.tensor_scalar(msq[:, i:i + 1], ssq[:, i:i + 1], 1.0 / (n * coef * coef),
                                                EPS / (coef * coef), ALU.mult, ALU.add))
        t2 = pool([t1, t_hc], lambda e: e.tensor_tensor(rs[:, i:i + 1], msq[:, i:i + 1], half_c[:, 0:1], ALU.pow))
        return t, t2

    def src_len(src):
        return src.shape[-1]

    def turn(src, gain, waits, banks, dst=None):
        dst = dst or NT
        last = []
        for pair in range(4):
            b = banks.take()
            k.wait("pe", [b.free, waits, t_id])
            for cc in range(2):
                for half in range(2):
                    c = 2 * pair + cc
                    ins = nc.tensor.transpose(b.ap[:, cc * 256 + half * 128:cc * 256 + half * 128 + 128],
                                              src[:, half, c * 128:(c + 1) * 128], ident)
            t = k.mark(k.sem["pe"], ins, 1)
            t1 = t
            for cc in range(2):
                c = 2 * pair + cc
                o, i_ = dst[0][:, c, :], b.ap[:, cc * 256:cc * 256 + 256]
                if gain is None:
                    t1 = act([t], lambda e: e.activation(o, i_, ACT.Copy))
                else:
                    t1 = act([t, t_pg], lambda e: e.activation(o, i_, ACT.Copy, scale=pg(gain, c)))
            for cc in range(2):
                c = 2 * pair + cc
                h_, o, i_ = dst[0][:, c, :].bitcast(F32), dst[1][:, c, :], b.ap[:, cc * 256:cc * 256 + 256]
                if gain is None:
                    t2 = dve([t1], lambda e: e.tensor_tensor(o, i_, h_, ALU.subtract))
                else:
                    t2 = dve([t1], lambda e: e.scalar_tensor_tensor(out=o, in0=i_, scalar=pg(gain, c), in1=h_,
                                                                    op0=ALU.mult, op1=ALU.subtract))
            b.free = [t2]
            last.append(t2)
        return last

    def prenorm(src, gain, waits, banks, between=None):
        ts = []
        for half in range(2):
            _, t = rstd(half, src[:, half, :], D, [waits[half], norm_state["rs"][half]])
            ts.append(dve([t], lambda e: e.tensor_scalar(XN[:, half, :], src[:, half, :],
                                                                           rs[:, half:half + 1], None, ALU.mult)))
        norm_state["rs"] = list(ts)
        if state["ready"] == 0:
            split_next()
        if between:
            between()
        r = turn(XN, gain, ts, banks)
        return r

    gain_read = {}

    def postnorm(gain, coef, waits):
        out_t = []
        for half in range(2):
            acc = ps[:, 2 * half:2 * half + 2, :].rearrange("p a b -> p (a b)")
            ta, t = rstd(half, acc, D, [waits[half], norm_state["rs"][half]], coef)
            g, t_row = row_gain[gain]
            tx = t_g1 = dve([waits[half], t_row], lambda e: e.tensor_tensor(XN[:, half, :], acc, g, ALU.mult))
            bank[2 * half].free = bank[2 * half + 1].free = [ta, tx]
            t = dve([tx, t], lambda e: e.scalar_tensor_tensor(out=H[:, half, :], in0=XN[:, half, :],
                                                              scalar=rs[:, half:half + 1], in1=H[:, half, :],
                                                              op0=ALU.mult, op1=ALU.add))
            out_t.append(t)
        norm_state["rs"] = list(out_t)
        gain_read[gain] = t_g1
        if gain != "ffn1_post_g":
            load_row_gain(row_names.index(gain) + 2, [t_g1])
        return out_t

    b47 = Banks(bank[4:8])
    ball = Banks(bank)

    def tile(waits, c):
        return waits[c // 2:c // 2 + 1] if type(waits) is list and len(waits) == 4 else [waits]

    def product_T(ntiles, x, waits, banks, evac, kt=8):
        per = 2048 // (kt * 128)
        for n0 in range(0, ntiles, per):
            p = take(kt, per * 128)
            k.wait("pe", [p[3]])
            for q in range(0, per, 2):
                b = banks.take()
                k.wait("pe", [b.free])
                for r in range(2):
                    a = (q + r) * 128
                    for c in range(kt):
                        k.wait("pe", tile(waits, c))
                        ins = mm3(b.ap[:, r * 256:r * 256 + 256], p[1][:, c, a:a + 128], p[2][:, c, a:a + 128], x,
                                  lambda v: v[:, c, :], c == 0, c == kt - 1)
                t = k.mark(k.sem["pe"], ins, 1)
                if q == per - 2:
                    release(p, t)
                b.free = [evac(n0 + q, b.ap, t)]

    def product_N(ncols, x, waits, banks, evac):
        for n0 in range(0, ncols, 256):
            p = take(8, 256)
            b = banks.take()
            k.wait("pe", [p[3], b.free])
            for half in range(2):
                for c in range(8):
                    k.wait("pe", tile(waits, c))
                    ins = mm3(b.ap[:, half * 256:half * 256 + 256], p[1][:, c, :], p[2][:, c, :], x,
                              lambda v: v[:, c, half * 128:half * 128 + 128], c == 0, c == 7, True)
            t = k.mark(k.sem["pe"], ins, 1)
            release(p, t)
            b.free = [evac(n0, b.ap, t)]

    def product_acc(j0, total, x, waits, at=None):
        p = take(2, D)
        at = j0 if at is None else at
        k.wait("pe", [p[3], waits] + ([bank[i].free for i in range(4)] if j0 == 0 else []))
        toks = []
        for half in range(2):
            for jj in range(2):
                for nb in range(2):
                    ins = mm3(bank[2 * half + nb].ap, p[1][:, jj, nb * 512:nb * 512 + 512],
                              p[2][:, jj, nb * 512:nb * 512 + 512], x,
                              lambda v: v[:, at + jj, half * 128:half * 128 + 128], j0 + jj == 0,
                              j0 + jj == total - 1, True)
            toks.append(k.mark(k.sem["pe"], ins, 1))
        release(p, toks[-1])
        return toks

    def split(dst_h, dst_l, src, waits):
        t = act([waits], lambda e: e.activation(dst_h, src, ACT.Copy))
        return dve([t, waits], lambda e: e.tensor_tensor(dst_l, src, dst_h.bitcast(F32), ALU.subtract))

    def ffn(nt, post, later=None):
        sg = [ar(256 * i, 256) for i in range(4)]
        tm_ = [ar(1024 + 256 * i, 256) for i in range(4)]
        sgfree, tfree, afree = [None] * 4, [None] * 4, [None] * 3
        pend = None
        for i in range(FFN_TILES // 2):
            if later and i in later:
                later[i]()
            bb, tb = [b47.take(), b47.take()], [None, None]
            for q in range(2):
                p = take(8, 256)
                for r in range(2):
                    k.wait("pe", [p[3], bb[r].free])
                    for c in range(8):
                        k.wait("pe", tile(nt, c))
                        ins = mm3(bb[r].ap[:, q * 256:q * 256 + 256], p[1][:, c, r * 128:(r + 1) * 128],
                                  p[2][:, c, r * 128:(r + 1) * 128], NT, lambda v: v[:, c, :], c == 0, c == 7)
                    tb[r] = k.mark(k.sem["pe"], ins, 1)
                release(p, tb[1])
            for r in range(2):
                j = 2 * i + r
                b, t = bb[r], tb[r]
                x, y = sg[j % 4], tm_[j % 4]
                t1 = act([t, sgfree[j % 4]], lambda e: e.activation(x, b.ap[:, 0:256], ACT.Silu))
                t2 = dve([t1, tfree[j % 4]], lambda e: e.tensor_tensor(y, b.ap[:, 256:512], x, ALU.mult))
                sgfree[j % 4] = t2
                b.free = [t2]
                a = 4 * (i % 3) + r
                tfree[j % 4] = t2 = split(YY[:, a, :], YY[:, a + 2, :], y, [t2, afree[i % 3]])
            if pend is not None:
                v = YY[:, 4 * (pend[0] % 3):4 * (pend[0] % 3) + 4, :]
                afree[pend[0] % 3] = product_acc(2 * pend[0], FFN_TILES, (v[:, 0:2, :], v[:, 2:4, :]), [pend[1]], 0)[1]
            pend = (i, t2)
        v = YY[:, 4 * (pend[0] % 3):4 * (pend[0] % 3) + 4, :]
        toks = product_acc(2 * pend[0], FFN_TILES, (v[:, 0:2, :], v[:, 2:4, :]), [pend[1]], 0)
        return postnorm(post, 0.5, toks)

    nt = prenorm(H, "ffn1_pre_g", t_x, ball)
    for v, name, n in ((dtb, "dt_bias", 16), (alog, "a_log", 16), (dsk, "d_skip", 16), (sink, "attn_sinks_2", 8)):
        t_b = k.dma("act", s_b, [], v, A[name][0].unsqueeze(0).broadcast_to([P, n]))
    t_b = k.dma("act", s_b, [], LB[:, :, :], A["hgrn_lb_logits_2"].unsqueeze(0).broadcast_to([P, 2, 512]))
    load_row_gain(0, [])
    load_row_gain(1, [])
    def forget_bound():
        lt = ar(4096, 3, 512)
        t = dve([t_b], lambda e: e.tensor_tensor(lt[:, 2, :], LB[:, 0, :], LB[:, 1, :], ALU.max))
        t = dve([t], lambda e: e.tensor_tensor(lt[:, 0:2, :], LB[:, :, :], lt[:, 2, :].unsqueeze(1).broadcast_to([P, 2, 512]),
                                               ALU.subtract))
        t = act([t], lambda e: e.activation(lt[:, 0:2, :], lt[:, 0:2, :], ACT.Exp))
        t = dve([t], lambda e: e.tensor_tensor(lt[:, 1, :], lt[:, 0, :], lt[:, 1, :], ALU.add))
        t = dve([t], lambda e: e.reciprocal(lt[:, 1, :], lt[:, 1, :]))
        t = dve([t], lambda e: e.tensor_tensor(LB[:, 0, :], lt[:, 0, :], lt[:, 1, :], ALU.mult))
        t_lb = dve([t], lambda e: e.tensor_scalar(LB[:, 1, :], LB[:, 0, :], -1.0, 1.0, ALU.mult, ALU.add))
        return t_lb

    later = {2: lambda: bound.append(forget_bound())}
    bound = []
    t_h = ffn(nt, "ffn1_post_g", later)
    t_lb = bound[0]

    def softplus(dst, e, z, waits, efree):
        t = act([waits, efree], lambda g: g.activation(e, z, ACT.Abs))
        t = act([t], lambda g: g.activation(e, e, ACT.Exp, scale=-1.0))
        t = act([t], lambda g: g.activation(e, e, ACT.Ln, bias=1.0))
        return t, dve([t, waits], lambda g: g.scalar_tensor_tensor(out=dst, in0=z, scalar=0.0, in1=e, op0=ALU.max,
                                                                  op1=ALU.add))

    nt = prenorm(H, "mix_pre_g", t_h, ball)
    qT, kT, Z = ar(0, 8, 256), ar(2048, 8, 256), ar(4096, 2, D)
    wdt = ar(11264, 8, 16)
    s_wdt = k.semaphore("s_wdt")
    t_wdt = k.dma("act", s_wdt, [], wdt, cols(A["w_in"][0], 5632, 16))
    catA = (YY[:, 0:8, :], YY[:, 8:16, :])
    catB = (YY[:, 16:24, :], YY[:, 24:32, :])
    xc = ar(6144, 12, 256)
    xn = ar(9216, 2, D)
    bn = ar(11264, 256)
    raw = [ar(11520 + 259 * i, 259) for i in range(3)]
    V = XN
    two = Banks([bank[4], bank[5]])
    tt = {}

    def ev_q(n, b, t):
        tt["q"] = act([t], lambda e: e.activation(qT[:, n:n + 2, :], b.rearrange("p (a b) -> p a b", a=2), ACT.Copy,
                                                  scale=0.125))
        return tt["q"]

    def ev_k(n, b, t):
        tt["k"] = dve([t], lambda e: e.tensor_copy(kT[:, n:n + 2, :], b.rearrange("p (a b) -> p a b", a=2)))
        return tt["k"]

    def ev_v(n, b, t):
        tt["v"] = dve([t], lambda e: e.tensor_copy(V[:, :, n:n + 256], b.rearrange("p (a b) -> p a b", a=2)))
        return tt["v"]

    product_T(8, NT, nt, ball, ev_q)
    product_T(8, NT, nt, ball, ev_k)
    product_N(1024, NT, nt, ball, ev_v)

    zb = Banks(bank[0:4])
    ee = [ar(12298 + 384 * i, 384) for i in range(2)]
    sp = [ar(13066 + 384 * i, 384) for i in range(2)]
    at_ = [ar(13834 + 384 * i, 384) for i in range(2)]
    sqb = [small[:, 256:512]]
    zbank, t_sp, t_a, pv_t = {}, {}, {}, {}
    sp_free, e_free, a_free = [None, None], [None, None], [None, None]
    sq_state = {"free": None, "pend": None}

    def diag(v, fill):
        return lambda g: g.affine_select(out=v, in_=v, compare_op=ALU.is_gt, fill=fill, base=0,
                                         pattern=[[0, 2], [1, P]], channel_multiplier=-1)

    def dview(x):
        return x.rearrange("p (a b) -> p a b", a=3)[:, 0:3:2, :]

    def at_scores(h):
        b = zb.take()
        zbank[h] = b
        o = 64 * (h % 2)
        k.wait("pe", [b.free, tt["q"], tt["k"]])
        mm(b.ap[:, 0:256], kT[o:o + 64, h // 2, 0:128], qT[o:o + 64, h // 2, :], True)
        t = pe([], lambda e: mm(b.ap[:, 256:384], kT[o:o + 64, h // 2, 128:256], qT[o:o + 64, h // 2, 128:256],
                                False))
        i = h % 2
        z, e = b.ap[:, 0:384], ee[i]
        t1 = act([t, e_free[i]], lambda g: g.activation(e, z, ACT.Abs))
        t1 = act([t1], lambda g: g.activation(e, e, ACT.Exp, scale=-1.0))
        return z, e, t, t1

    def at_softplus(h, z, e, t, t1):
        i = h % 2
        t1 = act([t1], lambda g: g.activation(e, e, ACT.Ln, bias=1.0))
        e_free[i] = ts = dve([t1, t, sp_free[i]], lambda g: g.scalar_tensor_tensor(out=sp[i], in0=z, scalar=0.0,
                                                                                  in1=e, op0=ALU.max, op1=ALU.add))
        t_sp[h] = pool([ts], diag(dview(sp[i]), 0.0))

    def at_logs(h):
        b, i = zbank[h], h % 2
        k.wait("pe", [t_sp[h], t_cst])
        mm(b.ap[:, 0:256], negtri, sp[i][:, 0:256], False)
        mm(b.ap[:, 128:256], negones, sp[i][:, 256:384], False)
        t = pe([], lambda e: mm(b.ap[:, 256:384], negtri, sp[i][:, 256:384], False))
        sp_free[i] = t
        t = act([t, a_free[i]], lambda e: e.activation(at_[i], b.ap[:, 0:384], ACT.Exp))
        b.free = [t]
        t_a[h] = pool([t], diag(dview(at_[i]), 0.0))


    def at_values(h):
        i, o = h % 2, 64 * (h % 2)
        b = bank[6]
        k.wait("pe", [t_a[h], tt["v"]] + ([b.free] if i == 0 else []))
        mm(b.ap[o:o + 64, 0:256], V[:, 0, 64 * h:64 * h + 64], at_[i][:, 0:256], True)
        t = pe([], lambda e: mm(b.ap[o:o + 64, 128:256], V[:, 1, 64 * h:64 * h + 64], at_[i][:, 256:384], False))
        a_free[i] = t
        if i:
            j = h // 2
            t1 = act([t], lambda e: e.activation(qT[:, j, :], b.ap[:, 0:256], ACT.Copy))
            t2 = act([sq_state["free"]], lambda e: e.activation(sqb[0], b.ap[:, 0:256], ACT.Square))
            b.free = [t2]
            sq_state["pend"] = (j, t2)

    def at_sum():
        if sq_state["pend"] is None:
            return
        j, t = sq_state["pend"]
        sq_state["pend"] = None
        k.wait("pe", [t, t_cst] + ([bank[7].free] if j == 0 else []))
        sq_state["free"] = pe([], lambda e: mm(bank[7].ap[:, 0:256], ones, sqb[0], j == 0, j == 7))

    step = [0]

    def attend():
        i = step[0]
        step[0] += 1
        at_sum()
        for h in (2 * i - 4, 2 * i - 3):
            if 0 <= h < 16:
                at_values(h)
        for h in (2 * i - 2, 2 * i - 1):
            if 0 <= h < 16:
                at_logs(h)
        if i < 8:
            ab = [at_scores(h) for h in (2 * i, 2 * i + 1)]
            for h in (0, 1):
                at_softplus(2 * i + h, *ab[h])

    def ev_z(n, b, t):
        r = act([t], lambda e: e.activation(Z[:, :, n:n + 256], b.rearrange("p (a b) -> p a b", a=2), ACT.Copy))
        attend()
        tt["z"] = r
        return r

    t_pad = pool([t_pg], lambda e: e.memset(ar(11520, 3, 259)[:, :, 0:3], 0.0))
    raw_free = [None] * 3
    t_xc = {}

    def ev_x(n, b, t):
        for r in range(2):
            c = n + r
            x = raw[c % 3]
            t1 = act([t, raw_free[c % 3], t_pad], lambda e: e.activation(x[:, 3:259], b[:, r * 256:r * 256 + 256],
                                                                         ACT.Copy))
            u = dve([t1], lambda e: e.tensor_scalar(xc[:, c, :], x[:, 0:256], pg("conv_w0", c), pg("conv_b", c),
                                                    ALU.mult, ALU.add))
            for q in (1, 2, 3):
                u = dve([u], lambda e: e.scalar_tensor_tensor(out=xc[:, c, :], in0=x[:, q:q + 256],
                                                              scalar=pg("conv_w%d" % q, c), in1=xc[:, c, :],
                                                              op0=ALU.mult, op1=ALU.add))
            raw_free[c % 3] = t_xc[c] = u
        attend()
        return t1

    state["hi"] = "dve"
    product_N(1024, NT, nt, two, ev_z)
    product_T(12, NT, nt, two, ev_x)

    MR, M0, t_m = take_raw()
    ssm, msm, rsm = sm(2), sm(2), sm(2)
    for half in range(2):
        u = act([t_m, norm_state["ja"]], lambda e: e.activation(JA[:, :], M0[:, half, :], ACT.Square,
                                                                accum_out=ssm[:, half:half + 1]))
        norm_state["ja"] = u
        u = dve([u], lambda e: e.tensor_scalar(msm[:, half:half + 1], ssm[:, half:half + 1], 1.0 / D, EPS, ALU.mult,
                                               ALU.add))
        u = pool([u], lambda e: e.tensor_tensor(rsm[:, half:half + 1], msm[:, half:half + 1], half_c[:, 0:1],
                                                ALU.pow))
        t_mn = dve([u], lambda e: e.tensor_scalar(M0[:, half, :], M0[:, half, :], rsm[:, half:half + 1], None,
                                                  ALU.mult))

    dt, adt, na = sm(32).rearrange("p (c h) -> p c h", c=2), sm(32).rearrange("p (c h) -> p c h", c=2), sm(16)
    dtmp = sm(32).rearrange("p (c h) -> p c h", c=2)
    wdec, eacs = sm(16), sm(16)

    def ev_dt(n, b, t):
        v = b[:, 0:32].rearrange("p (c h) -> p c h", c=2)
        t1 = dve([t, t_b], lambda e: e.tensor_tensor(dt, v, dtb.unsqueeze(1).broadcast_to([P, 2, 16]), ALU.add))
        ta = act([t_b], lambda e: e.activation(na, alog, ACT.Exp))
        _, t2 = softplus(adt, dtmp, dt, [t1], None)
        t3 = dve([t2], lambda e: e.tensor_copy(dt, adt))
        t3 = dve([t3, ta], lambda e: e.scalar_tensor_tensor(out=adt, in0=dt, scalar=-1.0,
                                                            in1=na.unsqueeze(1).broadcast_to([P, 2, 16]),
                                                            op0=ALU.mult, op1=ALU.mult))
        tt["dt"] = t3
        return t1

    b = two.take()
    k.wait("pe", [t_wdt, b.free])
    for half in range(2):
        for c in range(8):
            for q in range(2):
                ins = mm(b.ap[:, half * 16:half * 16 + 16], NT[q][:, c, half * 128:half * 128 + 128].bitcast(F32),
                         wdt[:, c, :], c == 0 and q == 0, c == 7 and q == 1)
    t = k.mark(k.sem["pe"], ins, 1)
    b.free = [ev_dt(0, b.ap, t)]
    state["hi"] = "act"
    t_mt = turn(M0, "mem_g", [t_mn], two)
    MR.free = t_mt
    kTm = [GB[:, 0, :].rearrange("p (a b) -> p a b", a=4), ar(6144, 4, 256)]
    Vm = [ar(7168, 2, 512), ar(2048, 2, 512)]

    def kv(n, banks):
        dst, a = (kTm if n < 4 else Vm)[(n // 2) % 2], n % 2

        def ev(_, b, t):
            o = dst[:, 2 * a:2 * a + 2, :] if n < 4 else dst[:, :, 256 * a:256 * a + 256]
            tt["km" if n < 4 else "vm"] = t = act([t, gain_read["ffn1_post_g"]], lambda e: e.activation(
                o, b.rearrange("p (a b) -> p a b", a=2), ACT.Copy))
            return t

        (product_T if n < 4 else product_N)(2 if n < 4 else 256, NT, t_mt, banks, ev)

    while step[0] < 11:
        attend()
    kv(0, two)

    for a in (8, 0):
        t = act([t_xc[11]], lambda e: e.activation(xc[:, a:a + (4 if a else 8), :], xc[:, a:a + (4 if a else 8), :],
                                                   ACT.Silu))
        for c in range(a, a + (4 if a else 8)):
            t_xc[c] = t
    rbc = sqb[0]
    t = act([sq_state["free"], t_hc], lambda e: e.activation(rbc, bank[7].ap[:, 0:256], ACT.Sqrt, scale=1.0 / D,
                                                             bias=eps_c))
    bank[7].free = [t]
    t = dve([t], lambda e: e.reciprocal(rbc, rbc))
    t_rbc = t
    kv(1, two)
    for c in range(0, 8, 2):
        b = b47.take()
        k.wait("pe", [b.free, t_xc[c + 1]])
        for half in range(2):
            for r in range(2):
                ins = nc.tensor.transpose(b.ap[:, half * 256 + r * 128:half * 256 + r * 128 + 128],
                                          xc[:, c + r, half * 128:half * 128 + 128], ident)
        t = k.mark(k.sem["pe"], ins, 1)
        t_xn = act([t], lambda e: e.activation(xn[:, :, c * 128:c * 128 + 256],
                                               b.ap.rearrange("p (a b) -> p a b", a=2), ACT.Copy))
        b.free = [t_xn]
    b = b47.take()
    k.wait("pe", [b.free, t_xc[11]])
    for g in range(2):
        ins = nc.tensor.transpose(b.ap[:, g * 128:g * 128 + 128], xc[:, 8 + g, 0:128], ident)
    t = k.mark(k.sem["pe"], ins, 1)
    t_bn = act([t], lambda e: e.activation(bn, b.ap[:, 0:256], ACT.Copy))
    b.free = [t_bn]

    b = b47.take()
    k.wait("pe", [b.free, tt["dt"]])
    mm(b.ap[:, 0:16], tri_le, adt[:, 1, :], True)
    t = pe([], lambda e: mm(b.ap[:, 16:32], tri_gt, adt[:, 0, :], False))
    act([t], lambda e: e.activation(eacs, b.ap[:, 0:16], ACT.Exp))
    t = act([], lambda e: e.activation(wdec, b.ap[:, 16:32], ACT.Exp))
    b.free = [t]
    t_w = dve([t], lambda e: e.tensor_tensor(wdec, wdec, dt[:, 0, :], ALU.mult))

    cb = ar(13322, 4, P)
    b = b47.take()
    k.wait("pe", [b.free, t_sp[15]])
    for c in range(2):
        for g in range(2):
            ins = mm(b.ap[:, (2 * c + g) * 128:(2 * c + g) * 128 + 128], xc[:, 8 + g, c * 128:c * 128 + 128],
                     xc[:, 10 + g, c * 128:c * 128 + 128], True)
    t = k.mark(k.sem["pe"], ins, 1)
    t_cb = dve([t], lambda e: e.tensor_tensor(cb, b.ap.rearrange("p (a b) -> p a b", a=4),
                                              tri_le.unsqueeze(1).broadcast_to([P, 4, P]), ALU.mult))
    b.free = [t_cb]

    Mb = [ar(2048 + 512 * i, 4, P) for i in range(2)]
    m_free, t_m = [None] * 2, {}

    def build(n):
        c, h0, i = n // 4, 8 * ((n // 2) % 2) + 4 * (n % 2), n % 2
        for r in range(4):
            t_m[n] = dve([tt["dt"], m_free[i]], lambda e: e.tensor_scalar(Mb[i][:, r, :], tri_gt,
                                                                          adt[:, c, h0 + r:h0 + r + 1], None,
                                                                          ALU.mult))

    t_catA = {}
    for js in (range(0, 2), range(2, 8)):
        us = {j: dve([t_rbc], lambda e: e.scalar_tensor_tensor(out=qT[:, j, :], in0=qT[:, j, :],
                                                               scalar=pg("attn_norm_g", j), in1=rbc, op0=ALU.mult,
                                                               op1=ALU.mult)) for j in js}
        us = {j: act([us[j]], lambda e: e.activation(catA[0][:, j, :], qT[:, j, :], ACT.Copy)) for j in js}
        for j in js:
            t_catA[j] = dve([us[j]], lambda e: e.tensor_tensor(catA[1][:, j, :], qT[:, j, :],
                                                               catA[0][:, j, :].bitcast(F32), ALU.subtract))
    build(0)
    product_acc(0, 16, catA, [t_catA[0], t_catA[1]])
    xw = ar(0, D)
    st = ar(1024, D)
    t_xw = pool([t_w, t_xn, t_catA[7]], lambda e: e.tensor_tensor(xw.rearrange("p (h d) -> p h d", h=16),
                                                       xn[:, 0, :].rearrange("p (h d) -> p h d", h=16),
                                                       wdec.unsqueeze(2).broadcast_to([P, 16, 64]), ALU.mult))
    Y = XN
    t_y = {}
    for c in range(2):
        t_y[c] = pool([], lambda e: e.tensor_tensor(Y[:, c, :].rearrange("p (h d) -> p h d", h=16),
                                                    xn[:, c, :].rearrange("p (h d) -> p h d", h=16),
                                                    dsk.unsqueeze(2).broadcast_to([P, 16, 64]), ALU.mult))
    for g in range(2):
        b = b47.take()
        k.wait("pe", [b.free, t_xw, t_bn])
        t = pe([], lambda e: mm(b.ap, bn[:, g * 128:g * 128 + 128], xw[:, g * 512:g * 512 + 512], True))
        t_st = act([t], lambda e: e.activation(st[:, g * 512:g * 512 + 512], b.ap, ACT.Copy))
        b.free = [t_st]

    Lb = [ar(3072 + 512 * i, 4, P) for i in range(2)]
    Gb = [ar(12298 + 512 * i, 4, P) for i in range(2)]
    tmp = ar(13834, 512)
    l_free, g_free = [None] * 2, [None] * 2
    n = 0
    tmp_free = None
    yb = Banks([bank[6], bank[7]])
    ss2, ms2, rs2 = sm(4), sm(4), sm(4)
    t_catB = []
    quad, ybank = {}, {}

    def decays(n):
        i = n % 2
        if n not in t_m:
            build(n)
        b = two.take()
        k.wait("pe", [t_m[n], b.free])
        for r in range(4):
            ins = mm(b.ap[:, r * 128:r * 128 + 128], Mb[i][:, r, :], tri_le, True)
        t = m_free[i] = k.mark(k.sem["pe"], ins, 1)
        quad[n] = act([t, l_free[i]], lambda e: e.activation(Lb[i], b.ap.rearrange("p (a b) -> p a b", a=4), ACT.Exp))
        b.free = [quad[n]]

    def within(n):
        c, g, hq, i = n // 4, (n // 2) % 2, n % 2, n % 2
        h0 = 8 * g + 4 * hq
        if hq == 0:
            ybank[n // 2] = yb.take()
        y = ybank[n // 2]
        for r in range(4):
            t1 = dve([quad[n], t_cb, g_free[i]], lambda e: e.scalar_tensor_tensor(
                out=Gb[i][:, r, :], in0=Lb[i][:, r, :], scalar=dt[:, c, h0 + r:h0 + r + 1],
                in1=cb[:, 2 * c + g, :], op0=ALU.mult, op1=ALU.mult))
        l_free[i] = t1
        k.wait("pe", [t1, t_xn] + ([y.free] if hq == 0 else []))
        for r in range(4):
            h = h0 + r
            ins = mm(y.ap[:, (h % 8) * 64:(h % 8) * 64 + 64], Gb[i][:, r, :], xn[:, c, h * 64:h * 64 + 64], True)
        g_free[i] = quad[n] = k.mark(k.sem["pe"], ins, 1)

    yn = {}

    def combine(i, tmp_free):
        c, g = i // 2, i % 2
        y = ybank[i]
        Yv = Y[:, c, g * 512:g * 512 + 512]
        if c == 1:
            b = two.take()
            k.wait("pe", [b.free, t_st])
            to = pe([], lambda e: mm(b.ap, xc[:, 10 + g, 128:256], st[:, g * 512:g * 512 + 512], True))
        u = dve([quad[2 * i + 1], t_y[c]], lambda e: e.tensor_tensor(Yv, y.ap, Yv, ALU.add))
        y.free = [u]
        if c == 1:
            t = dve([to, tmp_free], lambda e: e.tensor_tensor(
                tmp.rearrange("p (h d) -> p h d", h=8), b.ap.rearrange("p (h d) -> p h d", h=8),
                eacs[:, g * 8:g * 8 + 8].unsqueeze(2).broadcast_to([P, 8, 64]), ALU.mult))
            b.free = [t]
            tmp_free = u = dve([t, u], lambda e: e.tensor_tensor(Yv, Yv, tmp, ALU.add))
        u = dve([u, tt["z"]], lambda e: e.tensor_tensor(Yv, Yv, Z[:, c, g * 512:g * 512 + 512], ALU.mult))
        u = act([u, norm_state["ja"]], lambda e: e.activation(JA[:, 0:512], Yv, ACT.Square, accum_out=ss2[:, i:i + 1]))
        norm_state["ja"] = u
        u = dve([u], lambda e: e.tensor_scalar(ms2[:, i:i + 1], ss2[:, i:i + 1], 1.0 / 512, EPS, ALU.mult, ALU.add))
        u = pool([u], lambda e: e.tensor_tensor(rs2[:, i:i + 1], ms2[:, i:i + 1], half_c[:, 0:1], ALU.pow))
        yn[i] = u
        return tmp_free

    def turn_y(i):
        c, g = i // 2, i % 2
        Yv = Y[:, c, g * 512:g * 512 + 512]
        u = dve([yn[i]], lambda e: e.tensor_scalar(Yv, Yv, rs2[:, i:i + 1], None, ALU.mult))
        b = two.take()
        k.wait("pe", [b.free, u])
        for r in range(4):
            ins = nc.tensor.transpose(b.ap[:, r * 128:r * 128 + 128], Yv[:, r * 128:r * 128 + 128], ident)
        t = k.mark(k.sem["pe"], ins, 1)
        for r in range(4):
            j = 4 * g + r
            u = act([t], lambda e: e.activation(catB[0][:, j, c * 128:c * 128 + 128], b.ap[:, r * 128:r * 128 + 128],
                                                ACT.Copy, scale=pg("ssd_norm_g", j)))
        for r in range(4):
            j = 4 * g + r
            w = dve([u], lambda e: e.scalar_tensor_tensor(
                out=catB[1][:, j, c * 128:c * 128 + 128], in0=b.ap[:, r * 128:r * 128 + 128],
                scalar=pg("ssd_norm_g", j), in1=catB[0][:, j, c * 128:c * 128 + 128].bitcast(F32),
                op0=ALU.mult, op1=ALU.subtract))
        b.free = [w]
        t_catB.append(w)

    decays(0)
    tt["z"] = act([tt["z"]], lambda e: e.activation(Z, Z, ACT.Silu))
    for n in range(8):
        if n < 7:
            decays(n + 1)
        if n % 2:
            kv(2 + n // 2, two)
        elif n:
            product_acc(n, 16, catA, [t_catA[n], t_catA[n + 1]])
        within(n)
        if n >= 2 and n % 2 == 0:
            tmp_free = combine(n // 2 - 1, tmp_free)
        if n >= 3 and n % 2 == 1:
            turn_y(n // 2 - 1)
    tmp_free = combine(3, tmp_free)
    product_acc(8, 16, catB, [t_catB[0], t_catB[2]], 0)
    turn_y(3)

    def softmax_stages(S, n_heads, scratch, waits, sinks=None, src=None):
        mx, sm_, rc, es, _ = scratch
        if src is None:
            t = dve([waits], lambda e: e.tensor_reduce(mx, S, AX.X, ALU.max))
        else:
            for i, v in enumerate(src):
                n = n_heads // len(src)
                t = dve([waits], lambda e: e.tensor_reduce(mx[:, n * i:n * i + n], v, AX.X, ALU.max))
        if sinks is not None:
            t = dve([t], lambda e: e.tensor_tensor(mx, mx, sinks, ALU.max))
            ts_ = dve([t], lambda e: e.tensor_tensor(es, sinks, mx, ALU.subtract))
        t = dve([t], lambda e: e.tensor_scalar(mx, mx, -1.0, None, ALU.mult))
        yield t
        if sinks is not None:
            t_es = act([ts_], lambda e: e.activation(es, es, ACT.Exp))
        for h in range(n_heads):
            v = S[:, h, :]
            if src is not None:
                n = n_heads // len(src)
                v = src[h // n][:, h % n, :]
            te = act([t], lambda e: e.activation(S[:, h, :], v, ACT.Exp, bias=mx[:, h:h + 1],
                                                 accum_out=sm_[:, h:h + 1]))
        yield te
        if sinks is not None:
            te = dve([te, t_es], lambda e: e.tensor_tensor(sm_, sm_, es, ALU.add))
        t = dve([te], lambda e: e.reciprocal(rc, sm_))
        u = []
        for h in range(n_heads):
            u.append(dve([t, te], lambda e: e.tensor_scalar(S[:, h, :], S[:, h, :], rc[:, h:h + 1], None, ALU.mult)))
        yield u

    qTm = ar(8192, 8, 256)
    Sx = [ar(10240 + 1024 * i, 4, 256) for i in range(2)]
    pT = ar(12288, 8, 256)
    oT = (YY[:, 16:24, :], YY[:, 24:32, :])

    def ev_copy(dst, eng, scale=None):
        def f(n, b, t):
            v = b.rearrange("p (a b) -> p a b", a=2)
            if eng == "act":
                tt["cp"] = act([t], lambda e: e.activation(dst[:, n:n + 2, :], v, ACT.Copy, scale=scale or 1.0))
            else:
                tt["cp"] = dve([t], lambda e: e.tensor_copy(dst[:, n:n + 2, :], v))
            return tt["cp"]
        return f

    def ev_nat(dst, key, eng):
        def f(n, b, t):
            v = b.rearrange("p (a b) -> p a b", a=2)
            if eng == "act":
                tt[key] = act([t], lambda e: e.activation(dst[:, :, n:n + 256], v, ACT.Copy))
            else:
                tt[key] = dve([t], lambda e: e.tensor_copy(dst[:, :, n:n + 256], v))
            return tt[key]
        return f

    for j in range(10, 16, 2):
        toks = product_acc(j, 16, catB, [t_catB[2]] if j < 12 else [t_catB[1], t_catB[3]], j - 8)
    t_h = postnorm("mix_post_g", 1.0, toks)
    split_next()
    nt = prenorm(H, "xa_pre_g", t_h, b47, lambda: [kv(6, b47), kv(7, b47)])
    product_T(8, NT, nt, ball, ev_copy(qTm, "act", 0.0625))
    t_q = tt["cp"]
    scr = [[sm(8) for _ in range(5)] for _ in range(2)]
    tp, sg_ = [], []
    for half in range(2):
        bs = []
        for hp in range(2):
            b = ball.take()
            bs.append(b)
            k.wait("pe", [b.free, t_q, tt["km"]])
            for r in range(2):
                h = 2 * hp + r
                for dt_ in range(2):
                    ins = mm(b.ap[:, r * 256:r * 256 + 256], qTm[:, 2 * h + dt_, half * 128:half * 128 + 128],
                             kTm[h // 2][:, 2 * (h % 2) + dt_, :], dt_ == 0, dt_ == 1)
            t_sx = t = k.mark(k.sem["pe"], ins, 1)
        g = softmax_stages(Sx[half], 4, [x[:, 0:4] for x in scr[half]], [t], None,
                           [b.ap.rearrange("p (a b) -> p a b", a=2) for b in bs])
        next(g)
        t = next(g)
        for b in bs:
            b.free = [t]
        sg_.append(g)
    for g in sg_:
        tp.append(next(g))
    load_row_gain(row_names.index("xa_post_g"), [t_sx])
    for h in range(4):
        b = ball.take()
        k.wait("pe", [b.free, tp])
        for mt in range(2):
            for half in range(2):
                ins = nc.tensor.transpose(b.ap[:, mt * 256 + half * 128:mt * 256 + half * 128 + 128],
                                          Sx[half][:, h, mt * 128:mt * 128 + 128], ident)
        t = k.mark(k.sem["pe"], ins, 1)
        if h % 2:
            t = act([t], lambda e: e.activation(pT[:, 2 * h:2 * h + 2, :], b.ap.rearrange("p (a b) -> p a b", a=2),
                                                ACT.Copy))
        else:
            t = dve([t], lambda e: e.tensor_copy(pT[:, 2 * h:2 * h + 2, :],
                                                 b.ap.rearrange("p (a b) -> p a b", a=2)))
        b.free = [t]
        b = ball.take()
        k.wait("pe", [b.free, t, tt["vm"]])
        for dt_ in range(2):
            for mt in range(2):
                ins = mm(b.ap[:, dt_ * 256:dt_ * 256 + 256],
                         Vm[h // 2][:, mt, (h % 2) * 256 + dt_ * 128:(h % 2) * 256 + dt_ * 128 + 128], pT[:, 2 * h + mt, :],
                         mt == 0, mt == 1)
        t = k.mark(k.sem["pe"], ins, 1)
        t_o = split(oT[0][:, 2 * h:2 * h + 2, :], oT[1][:, 2 * h:2 * h + 2, :],
                    b.ap.rearrange("p (a b) -> p a b", a=2), [t])
        b.free = [t_o]
    for j in range(0, 8, 2):
        toks = product_acc(j, 8, oT, [t_o])
    t_h = postnorm("xa_post_g", 1.0, toks)
    nt = prenorm(H, "ffn2_pre_g", t_h, ball)
    bias = ar(10752, 8, 256)
    di = AR[:, 12800:13056].bitcast(mybir.dt.int32)
    df, ng = ar(13056, 256), ar(13312, 256)
    t = pool([t_h], lambda e: e.iota(di, pattern=[[-1, 256]], base=128, channel_multiplier=1))
    t = pool([t], lambda e: e.tensor_copy(df, di))
    t = pool([t], lambda e: e.memset(ng, 0.0))
    t = pool([t], sel(ng, 128, [[-1, 256]], 1, ALU.is_ge, -1e30))
    t = pool([t], sel(ng, 0, [[1, 256]], -1, ALU.is_gt, -1e30))
    for h in range(8):
        t_bias = dve([t], lambda e: e.scalar_tensor_tensor(out=bias[:, h, :], in0=df, scalar=-(2.0 ** -(h + 1)),
                                                           in1=ng, op0=ALU.mult, op1=ALU.add))
    t_h = ffn(nt, "ffn2_post_g")

    nt = prenorm(H, "norm_mix_g_2", t_h, ball)
    aq, ak, av = ar(0, 4, 256), ar(1024, 256), ar(1280, 2, 128)
    hq, kn, lf, hv, hg = ar(1536, 4, 256), ar(2560, 2, 512), ar(3584, 2, 512), ar(4608, 2, 512), ar(5632, 4, 256)
    eb, kinv, kd, aT = ar(6656, 4, 256), ar(7680, 4, 256), ar(8704, 2, 512), ar(9728, 2, 4, P)
    ga, gh = ar(10752, 8, 256), ar(2560, 8, 256)
    ST = ar(12800, 2, 4, P)
    S0, S1 = ar(6656, 8, 128), ar(7680, 8, 256)
    pT2 = ar(9728, 8, 3, P)
    ya, yh = (YY[:, 0:4, :], YY[:, 4:8, :]), (YY[:, 8:12, :], YY[:, 12:16, :])

    for jp in range(2):
        p = take(8, 256)
        b = ball.take()
        k.wait("pe", [b.free, p[3]])
        for r in range(2):
            a = 128 * r
            for c in range(8):
                k.wait("pe", tile(nt, c))
                ins = mm3(b.ap[:, r * 256:r * 256 + 256], p[1][:, c, a:a + 128], p[2][:, c, a:a + 128], NT,
                          lambda v: v[:, c, :], c == 0, c == 7)
        t = k.mark(k.sem["pe"], ins, 1)
        release(p, t)
        t_aq = act([t], lambda e: e.activation(aq[:, 2 * jp:2 * jp + 2, :],
                                               b.ap.rearrange("p (a b) -> p a b", a=2), ACT.Copy, scale=0.125))
        b.free = [t_aq]
    p = take(8, 256)
    b = ball.take()
    k.wait("pe", [b.free, p[3]])
    for c in range(8):
        mm3(b.ap[:, 0:256], p[1][:, c, 0:128], p[2][:, c, 0:128], NT, lambda v: v[:, c, :], c == 0, c == 7)
    for half in range(2):
        for c in range(8):
            ins = mm3(b.ap[:, 256 + half * 128:384 + half * 128], p[1][:, c, 128:256], p[2][:, c, 128:256], NT,
                      lambda v: v[:, c, half * 128:half * 128 + 128], c == 0, c == 7, True)
    t = k.mark(k.sem["pe"], ins, 1)
    release(p, t)
    act([t], lambda e: e.activation(ak, b.ap[:, 0:256], ACT.Copy))
    t_av = act([], lambda e: e.activation(av, b.ap[:, 256:512].rearrange("p (a b) -> p a b", a=2), ACT.Copy))
    b.free = [t_av]

    t_s = [None, None]
    for h in range(8):
        o, j = 64 * (h // 4), h % 4
        b = ball.take()
        k.wait("pe", [b.free, t_aq, t_av])
        mm(b.ap[:, 0:128], aq[o:o + 64, j, 0:128], ak[o:o + 64, 0:128], True)
        t = pe([], lambda e: mm(b.ap[:, 128:384], aq[o:o + 64, j, 128:256], ak[o:o + 64, 0:256], False))
        t_s[0] = dve([t, t_bias], lambda e: e.tensor_tensor(S0[:, h, :], b.ap[:, 0:128], bias[:, h, 128:256], ALU.add))
        t_s[1] = dve([], lambda e: e.tensor_tensor(S1[:, h, :], b.ap[:, 128:384], bias[:, h, :], ALU.add))
        b.free = [t_s[1]]

    def ev_f(n, b, t):
        v = b.rearrange("p (a b) -> p a b", a=2)
        lb = LB[:, 0, n:n + 256].unsqueeze(1).broadcast_to([P, 2, 256])
        om = LB[:, 1, n:n + 256].unsqueeze(1).broadcast_to([P, 2, 256])
        kk, ll = kn[:, :, n:n + 256], lf[:, :, n:n + 256]
        r = act([t], lambda e: e.activation(kk, v, ACT.Sigmoid))
        t = dve([r, t_lb], lambda e: e.tensor_tensor(kk, kk, om, ALU.mult))
        t = dve([t], lambda e: e.tensor_tensor(ll, kk, lb, ALU.add))
        tt["kn"] = dve([t], lambda e: e.tensor_scalar(kk, ll, -1.0, 1.0, ALU.mult, ALU.add))
        tt["lf"] = act([tt["kn"]], lambda e: e.activation(ll, ll, ACT.Ln))
        return r

    s0 = softmax_stages(S0, 8, scr[0], [t_s[0]], sink)
    s1 = softmax_stages(S1, 8, scr[1], [t_s[1]], sink)
    product_N(512, NT, nt, ball, ev_f)
    next(s0)
    next(s1)
    ev_hv = ev_nat(hv, "hv", "act")
    product_N(256, NT, nt, ball, ev_hv)
    next(s0)
    product_N(256, NT, nt, ball, lambda n, b, t: ev_hv(n + 256, b, t))
    next(s1)

    def ev_silu(dst, key, func):
        def f(n, b, t):
            tt[key] = act([t, tt.get("over")], lambda e: e.activation(dst[:, n:n + 2, :],
                                                                      b.rearrange("p (a b) -> p a b", a=2), func))
            return tt[key]
        return f

    product_T(4, NT, nt, ball, ev_silu(hq, "hq", ACT.Silu))
    t_p = [next(s0), next(s1)]
    product_T(4, NT, nt, ball, ev_silu(hg, "hg", ACT.Silu))

    for h in range(8):
        b = ball.take()
        k.wait("pe", [b.free, t_p])
        nc.tensor.transpose(b.ap[:, 0:128], S1[:, h, 0:128], ident)
        nc.tensor.transpose(b.ap[:, 128:256], S1[:, h, 128:256], ident)
        t = pe([], lambda e: e.transpose(b.ap[:, 256:384], S0[:, h, :], ident))
        v = b.ap[:, 0:384].rearrange("p (a b) -> p a b", a=3)
        if h % 2:
            t_pt = act([t], lambda e: e.activation(pT2[:, h, :, :], v, ACT.Copy))
            t_pa = t_pt
        else:
            t_pt = dve([t], lambda e: e.tensor_copy(pT2[:, h, :, :], v))
            t_pd = t_pt
        b.free = [t_pt]
    for jp in range(2):
        b = ball.take()
        k.wait("pe", [b.free, t_pa, t_pd])
        for r in range(2):
            for q in range(2):
                h = 2 * (2 * jp + r) + q
                o, g = 64 * q, h // 4
                c0 = r * 256
                mm(b.ap[o:o + 64, c0:c0 + 128], av[:, 0, g * 64:g * 64 + 64], pT2[:, h, 2, :], r == 0)
                mm(b.ap[o:o + 64, c0 + 128:c0 + 256], av[:, 0, g * 64:g * 64 + 64], pT2[:, h, 0, :], False)
                ins = mm(b.ap[o:o + 64, c0 + 128:c0 + 256], av[:, 1, g * 64:g * 64 + 64], pT2[:, h, 1, :], False)
        t = k.mark(k.sem["pe"], ins, 1)
        t_ya = split(ya[0][:, 2 * jp:2 * jp + 2, :], ya[1][:, 2 * jp:2 * jp + 2, :],
                     b.ap.rearrange("p (a b) -> p a b", a=2), [t])
        b.free = [t_ya]
    tt["over"] = t_ya

    t_z = pool([t_ya], lambda e: e.memset(aT, 0.0))
    for jp in range(2):
        b = ball.take()
        k.wait("pe", [b.free, tt["lf"], t_cst])
        for r in range(2):
            h = 2 * jp + r
            for half in range(2):
                ins = mm(b.ap[:, r * 256 + half * 128:r * 256 + half * 128 + 128],
                         lf[:, half, h * 128:h * 128 + 128], bt_le, True)
        t = k.mark(k.sem["pe"], ins, 1)
        v = b.ap.rearrange("p (a b) -> p a b", a=2)
        act([t, t_ya], lambda e: e.activation(eb[:, 2 * jp:2 * jp + 2, :], v, ACT.Exp))
        t_eb = act([], lambda e: e.activation(kinv[:, 2 * jp:2 * jp + 2, :], v, ACT.Exp, scale=-1.0))
        b.free = [t_eb]
        b = ball.take()
        k.wait("pe", [b.free, tt["kn"]])
        for r in range(2):
            h = 2 * jp + r
            for half in range(2):
                ins = nc.tensor.transpose(b.ap[:, r * 256 + half * 128:r * 256 + half * 128 + 128],
                                          kn[:, half, h * 128:h * 128 + 128], ident)
        t = k.mark(k.sem["pe"], ins, 1)
        v2 = b.ap.rearrange("p (a b) -> p a b", a=2)
        t_ki = dve([t, t_eb], lambda e: e.tensor_tensor(kinv[:, 2 * jp:2 * jp + 2, :], v2,
                                                        kinv[:, 2 * jp:2 * jp + 2, :], ALU.mult))
        b.free = [t_ki]
        t_qd = pool([t_eb, tt["hq"]], lambda e: e.tensor_tensor(hq[:, 2 * jp:2 * jp + 2, :],
                                                                hq[:, 2 * jp:2 * jp + 2, :],
                                                                eb[:, 2 * jp:2 * jp + 2, :], ALU.mult))
    for half in range(2):
        b = ball.take()
        k.wait("pe", [b.free])
        t = pe([], lambda e: mm(b.ap, bt_gt, lf[:, half, :], True))
        t = act([t], lambda e: e.activation(kd[:, half, :], b.ap, ACT.Exp))
        b.free = [t]
        t_gt = t
        t_kd = pool([t, tt["kn"]], lambda e: e.tensor_tensor(kd[:, half, :], kd[:, half, :], kn[:, half, :],
                                                             ALU.mult))
    b67 = Banks(bank[6:8])
    ob = [bank[4], bank[5]]
    rec = {"c": 0, "s": None, "free": [None, None]}

    def additions(c):
        b = bank[c % 4]
        half, r = c // 4, 32 * (c % 4)
        k.wait("pe", [b.free, t_kd, tt["hv"]])
        for h in range(4):
            ins = mm(b.ap[:, h * 128:h * 128 + 128], kd[r:r + 32, half, h * 128:h * 128 + 128],
                     hv[r:r + 32, half, h * 128:h * 128 + 128], True)
        t = k.mark(k.sem["pe"], ins, 1)
        if c == 0:
            u = dve([t, t_ya], lambda e: e.tensor_copy(ST[:, 0, :, :], b.ap.rearrange("p (a b) -> p a b", a=4)))
        else:
            for h in range(4):
                u = dve([t, rec["s"], rec["free"][c % 2]], lambda e: e.scalar_tensor_tensor(
                    out=ST[:, c % 2, h, :], in0=ST[:, (c - 1) % 2, h, :], scalar=eb[:, h, 32 * c + 31:32 * c + 32],
                    in1=b.ap[:, h * 128:h * 128 + 128], op0=ALU.mult, op1=ALU.add))
        rec["s"] = u
        b.free = [u]

    def inside():
        k.wait("pe", [ob[0].free, ob[1].free, t_aT, tt["hv"]])
        for h in range(4):
            for half in range(2):
                c0 = (h % 2) * 256 + half * 128
                mm(ob[h // 2].ap[:, c0:c0 + 128], hv[:, half, h * 128:h * 128 + 128], aT[:, half, h, :],
                   c0 == 0)

    def across(c):
        k.wait("pe", [rec["s"]])
        for h in range(4):
            c0 = (h % 2) * 256 + 32 * c
            ins = mm(ob[h // 2].ap[:, c0:c0 + 32], ST[:, (c - 1) % 2, h, :], hq[:, h, 32 * c:32 * c + 32], False)
        t = k.mark(k.sem["pe"], ins, 1)
        rec["free"][(c - 1) % 2] = t
        return t

    def ev_ga(n, b, t):
        tt["ga"] = act([t, t_ya], lambda e: e.activation(ga[:, n:n + 2, :], b.rearrange("p (a b) -> p a b", a=2),
                                                         ACT.Sigmoid))
        if n:
            across(n // 2)
            additions(n // 2)
        return tt["ga"]

    def ev_gh(n, b, t):
        tt["gh"] = act([t, t_kd, t_ki, t_gt], lambda e: e.activation(gh[:, n:n + 2, :],
                                                                     b.rearrange("p (a b) -> p a b", a=2),
                                                                     ACT.Sigmoid))
        tt["o"] = across(4 + n // 2)
        if n < 6:
            additions(4 + n // 2)
        return tt["gh"]

    product_T(2, NT, nt, b67, ev_ga)
    for half in range(2):
        b = bank[half]
        k.wait("pe", [b.free, t_ki, t_qd])
        for h in range(4):
            ins = mm(b.ap[:, h * 128:h * 128 + 128], kinv[:, h, half * 128:half * 128 + 128],
                     hq[:, h, half * 128:half * 128 + 128], True)
        t = k.mark(k.sem["pe"], ins, 1)
        m = bt_le.bitcast(U32).unsqueeze(1).broadcast_to([P, 4, P])
        t_aT = dve([t, t_z, t_cst], lambda e: e.copy_predicated(aT[:, half, :, :], m,
                                                                b.ap.rearrange("p (a b) -> p a b", a=4)))
        b.free = [t_aT]

    additions(0)
    inside()
    product_T(6, NT, nt, b67, lambda n, b, t: ev_ga(n + 2, b, t))
    product_T(8, NT, nt, b67, ev_gh)
    mbank = [[bank[i] for i in (2, 3, 6, 7)], bank[4:8]]
    mtok = [[None] * 4, [None] * 4]

    def project(i, q, x, w):
        p = take(4, 512)
        for r in range(4):
            b = mbank[i][r]
            k.wait("pe", [b.free, p[3], w])
            for c in range(4):
                ins = mm3(b.ap[:, q * 256:q * 256 + 256], p[1][:, c, r * 128:r * 128 + 128],
                          p[2][:, c, r * 128:r * 128 + 128], x, lambda v: v[:, c, :], c == 0, c == 3)
            mtok[i][r] = k.mark(k.sem["pe"], ins, 1)
        release(p, mtok[i][3])

    us, tn = [], []
    for jp in range(2):
        us.append(act([tt["o"], norm_state["ja"]], lambda e: e.activation(JA[:, 512 * jp:512 * jp + 512], ob[jp].ap,
                                                                          ACT.Square)))
    for jp in range(2):
        k.wait("pe", [bank[jp].free, us[jp], t_cst])
        tn.append(pe([], lambda e: mm(bank[jp].ap, ones, JA[:, 512 * jp:512 * jp + 512], True)))
    norm_state["ja"] = [us[1], tn[1]]
    project(0, 0, ya, t_ya)
    rb = [kinv[:, 2 * jp:2 * jp + 2, :] for jp in range(2)]
    for jp in range(2):
        tn[jp] = act([tn[jp], t_aT, t_hc], lambda e: e.activation(rb[jp], bank[jp].ap.rearrange("p (a b) -> p a b", a=2),
                                                                  ACT.Ln, scale=1.0 / 128, bias=eps_c))
        bank[jp].free = [tn[jp]]
    for jp in range(2):
        tn[jp] = act([tn[jp]], lambda e: e.activation(rb[jp], rb[jp], ACT.Exp, scale=-0.5))
    for jp in range(2):
        b = ob[jp]
        t = dve([tn[jp], us[jp]], lambda e: e.scalar_tensor_tensor(
            out=rb[jp], in0=b.ap.rearrange("p (a b) -> p a b", a=2), scalar=pg("hgrn_norm_g_2", 0), in1=rb[jp],
            op0=ALU.mult, op1=ALU.mult))
        b.free = [t]
        t = dve([t, tt["hg"]], lambda e: e.tensor_tensor(rb[jp], rb[jp], hg[:, 2 * jp:2 * jp + 2, :], ALU.mult))
        t_yh = split(yh[0][:, 2 * jp:2 * jp + 2, :], yh[1][:, 2 * jp:2 * jp + 2, :], rb[jp], [t])
    mt = [ar(8704 + 256 * i, 256) for i in range(4)]
    mfree = [None] * 4
    t_mg = {}
    for n0 in range(0, 8, 4):
        if n0:
            project(1, 0, ya, t_ya)
        project(n0 // 4, 1, yh, t_yh)
        bb, tb = mbank[n0 // 4], mtok[n0 // 4]
        for r in range(4):
            n, b, t = n0 + r, bb[r], tb[r]
            m = mt[n % 4]
            u1 = dve([t, tt["ga"], tt["gh"]], lambda e: e.tensor_tensor(b.ap[:, 0:256], b.ap[:, 0:256], ga[:, n, :],
                                                                        ALU.mult))
            u = dve([mfree[n % 4]], lambda e: e.tensor_tensor(m, b.ap[:, 256:512], gh[:, n, :], ALU.mult))
            u = dve([u1, u], lambda e: e.tensor_tensor(m, b.ap[:, 0:256], m, ALU.add))
            b.free = [u]
            t_m = t_mg[n] = mfree[n % 4] = split(NT[0][:, n, :], NT[1][:, n, :], m, [u])
    keys = ar(4096, 16, P)
    s_keys = k.semaphore("s_keys")
    t_kraw = k.dma("act", s_keys, [t_yh, tt["o"], tt["gh"], t_m], keys,
                   A["peer_keys_2"][0].rearrange("a h n d -> n (a h) d"))
    for j in range(0, 8, 2):
        toks = product_acc(j, 8, NT, [t_mg[j], t_mg[j + 1]])
    t_h = []
    for half in range(2):
        acc = ps[:, 2 * half:2 * half + 2, :].rearrange("p a b -> p (a b)")
        t = dve([toks[half]], lambda e: e.tensor_tensor(H[:, half, :], acc, H[:, half, :], ALU.add))
        bank[2 * half].free = [t]
        bank[2 * half + 1].free = [t]
        t_h.append(t)

    wctx.close()
    wctx = ExitStack()
    gs1 = sb("GS1", [P, 8, D])
    WH, WL, NT = operands(1)
    conv_free = [t_h] * NCONV
    keysT, qp = ar(0, 16, P), ar(2048, 4, 256)
    SC = [ar(6144 + 2048 * i, 16, P) for i in range(2)]
    ts = []
    for half in range(2):
        _, t = rstd(half, H[:, half, :], D, [t_h[half], norm_state["rs"][half]])
        g, t_row = row_gain["norm_ffn_g_2"]
        ts.append(dve([t, t_row], lambda e: e.scalar_tensor_tensor(out=XN[:, half, :], in0=H[:, half, :],
                                                                   scalar=rs[:, half:half + 1], in1=g,
                                                                   op0=ALU.mult, op1=ALU.mult)))
    split_next()
    nt = turn(XN, None, ts, ball)
    v = keys
    for q in range(4):
        b = b47.take()
        k.wait("pe", [b.free, t_kraw, t_h])
        for r in range(4):
            ins = nc.tensor.transpose(b.ap[:, r * 128:r * 128 + 128], v[:, 4 * q + r, :], ident)
        t = k.mark(k.sem["pe"], ins, 1)
        t_keys = act([t], lambda e: e.activation(keysT[:, 4 * q:4 * q + 4, :],
                                                 b.ap.rearrange("p (a b) -> p a b", a=4), ACT.Copy))
        b.free = [t_keys]
    t_sc = {}

    b03 = Banks(bank[0:4])
    qfree = [None, None]

    def query(i):
        p = take(8, 256)
        b = b03.take()
        k.wait("pe", [p[3], b.free])
        for r in range(2):
            for c in range(8):
                k.wait("pe", tile(nt, c))
                ins = mm3(b.ap[:, r * 256:r * 256 + 256], p[1][:, c, r * 128:r * 128 + 128],
                          p[2][:, c, r * 128:r * 128 + 128], NT, lambda v: v[:, c, :], c == 0, c == 7)
        t = k.mark(k.sem["pe"], ins, 1)
        release(p, t)
        a = 2 * (i % 2)
        t = act([t, qfree[i % 2]], lambda e: e.activation(qp[:, a:a + 2, :], b.ap.rearrange("p (a b) -> p a b", a=2),
                                            ACT.Copy))
        b.free = [t]
        b = b03.take()
        k.wait("pe", [b.free, t, t_keys])
        for half in range(2):
            for r in range(2):
                c0 = half * 256 + r * 128
                ins = mm(b.ap[:, c0:c0 + 128], qp[:, a + r, half * 128:half * 128 + 128],
                         keysT[:, r * 8 + i, :], True)
        t = qfree[i % 2] = k.mark(k.sem["pe"], ins, 1)
        for half in range(2):
            t_sc[half, i] = act([t], lambda e: e.activation(
                SC[half][:, 2 * i:2 * i + 2, :],
                b.ap[:, half * 256:half * 256 + 256].rearrange("p (a b) -> p a b", a=2), ACT.Copy))
        b.free = [t_sc[1, i]]
        return t

    at = [10240]

    def a2(*shape):
        n = 1
        for x in shape:
            n *= x
        o = at[0]
        at[0] += n
        return ar(o, *shape)

    def a2u(n):
        o = at[0]
        at[0] += n
        return AU[:, o:o + n]

    iot = a2(16)
    ioti = AR[:, at[0]:at[0] + 16].bitcast(mybir.dt.int32)
    at[0] += 16
    t = pool([t_h], lambda e: e.iota(ioti, pattern=[[1, 16]], base=0, channel_multiplier=0))
    t_iota = pool([t], lambda e: e.tensor_copy(iot, ioti))
    UB = 3
    un = []
    for i in range(UB):
        un.append(dict(V=a2(2, 16), I=a2u(32), IF=a2(2, 16), best=a2(16), pos=a2u(16), pp=a2u(32), pf=a2(2, 16),
                       sel=a2(2, 16), idx=a2u(16), e=a2(16), s=a2(1), r=a2(1), nb=a2(1), a=a2(16), g=a2(16),
                       w=a2(16)))
    cand = [a2(256), a2(256)]
    oh = a2(2, 16, 16)
    diag = [a2(P) for _ in range(8)]
    spots = [gs1[:, i, :] for i in range(8)] + [a2(D), ar(3072, D), ar(4096, D), ar(5120, D),
                                                LB[:, :, :].rearrange("p a b -> p (a b)")]
    assert at[0] <= 14604
    gs = [Slot(v, k.semaphore(f"gather{i}")) for i, v in enumerate(spots)]
    for g in gs:
        g.free = [t_h, t_keys]
    ngs = [0]

    def gather(table, idx, waits):
        s = gs[ngs[0] % len(gs)]
        ngs[0] += 1
        k.wait("pool", [s.free, waits])
        ins = nc.gpsimd.indirect_dma_start(s.ap, None, table, bass.IndirectOffsetOnAxis(idx, 0))
        return s, k.mark(s.sem, ins, 16)

    def choose(n):
        half, head = n // 8, n % 8
        x = un[n % UB]
        free = [unit_done.get(n - UB)]

        def step(waits, f):
            return dve(waits, f)

        def top16(src, v, i, waits):
            t = step([waits, free], lambda e: e.max(v[:, 0:8], src))
            t1 = step([t], lambda e: e.max_index(i[:, 0:8], v[:, 0:8], src))
            t = step([t, t1], lambda e: e.match_replace(src, v[:, 0:8], src, -3.0e38))
            t = step([t], lambda e: e.max(v[:, 8:16], src))
            return step([t], lambda e: e.max_index(i[:, 8:16], v[:, 8:16], src))

        for a in range(2):
            t = top16(SC[half][:, 2 * head + a, :], x["V"][:, a, :], x["I"][:, 16 * a:16 * a + 16],
                      [t_sc[half, head]])
            yield
        ti = step([t], lambda e: e.tensor_copy(x["IF"], x["I"].rearrange("p (a b) -> p a b", a=2)))
        c = cand[n % 2]
        t = step([t], lambda e: e.tensor_tensor(c.rearrange("p (a b) -> p a b", a=16),
                                                x["V"][:, 0, :].unsqueeze(2).broadcast_to([P, 16, 16]),
                                                x["V"][:, 1, :].unsqueeze(1).broadcast_to([P, 16, 16]), ALU.add))
        yield
        t = top16(c, x["best"], x["pos"], [t])
        yield
        u = act([t], lambda e: e.activation(x["nb"], x["best"][:, 0:1], ACT.Copy, scale=-1.0))
        u = act([u], lambda e: e.activation(x["e"], x["best"], ACT.Exp, bias=x["nb"], accum_out=x["s"]))
        step([t], lambda e: e.tensor_scalar(x["pp"][:, 0:16], x["pos"], 4, None, ALU.logical_shift_right))
        t = step([t], lambda e: e.tensor_scalar(x["pp"][:, 16:32], x["pos"], 15, None, ALU.bitwise_and))
        t = step([t], lambda e: e.tensor_copy(x["pf"], x["pp"].rearrange("p (a b) -> p a b", a=2)))
        yield
        t = step([t, t_iota], lambda e: e.tensor_tensor(
            oh, x["pf"].unsqueeze(3).broadcast_to([P, 2, 16, 16]),
            iot.unsqueeze(1).unsqueeze(1).broadcast_to([P, 2, 16, 16]), ALU.is_equal))
        yield
        t = step([t, ti], lambda e: e.tensor_tensor(oh, oh, x["IF"].unsqueeze(2).broadcast_to([P, 2, 16, 16]),
                                                    ALU.mult))
        yield
        t = step([t], lambda e: e.tensor_reduce(x["sel"], oh, AX.X, ALU.add))
        t = step([t], lambda e: e.scalar_tensor_tensor(out=x["idx"], in0=x["sel"][:, 0, :], scalar=128.0,
                                                       in1=x["sel"][:, 1, :], op0=ALU.mult, op1=ALU.add))
        x["t_idx"] = t
        x["t_r"] = step([u], lambda e: e.reciprocal(x["r"], x["s"]))

    U_, V_ = A["peer_u_2"][0], A["peer_v_2"][0]
    unit_done = {}
    acc = {}
    dfree = [None] * 8
    fin_t = {}

    def finish(h_, stage):
        g, t_row = row_gain["norm_final_g_2"]
        if stage == 0:
            av_ = ps[:, 4 + 2 * h_:6 + 2 * h_, :].rearrange("p a b -> p (a b)")
            t = dve([unit_done[8 * h_ + 7], fin_t.get("h")], lambda e: e.tensor_tensor(H[:, h_, :], av_, H[:, h_, :], ALU.add))
            t = act([t, norm_state["ja"]], lambda e: e.activation(JA[:, :], H[:, h_, :], ACT.Square,
                                                                  accum_out=ssq[:, h_:h_ + 1]))
            norm_state["ja"] = fin_t[h_] = t
        elif stage == 1:
            fin_t[h_] = dve([fin_t[h_]], lambda e: e.tensor_scalar(msq[:, h_:h_ + 1], ssq[:, h_:h_ + 1], 1.0 / D,
                                                                   EPS, ALU.mult, ALU.add))
        elif stage == 2:
            fin_t[h_] = pool([fin_t[h_]], lambda e: e.tensor_tensor(rs[:, h_:h_ + 1], msq[:, h_:h_ + 1],
                                                                    half_c[:, 0:1], ALU.pow))
        else:
            t = dve([fin_t[h_], t_row], lambda e: e.scalar_tensor_tensor(out=H[:, h_, :], in0=H[:, h_, :],
                                                                         scalar=rs[:, h_:h_ + 1], in1=g,
                                                                         op0=ALU.mult, op1=ALU.mult))
            fin_t[h_] = k.dma("sp", s_o, [t], out[0, h_ * P:(h_ + 1) * P, :], H[:, h_, :])

    s_o = k.semaphore("s_o")
    later = {(9, 6): 0, (9, 10): 1, (9, 13): 2, (10, 2): 3}
    LAG = 8

    def stream():
        nd = 0
        nxt = iter(())
        for j in range(256 + LAG):
            n, kk = j // 16, j % 16
            if kk == 0:
                nxt = choose(n + 1) if n + 1 < 16 else iter(())
            if j < 256:
                half, x = n // 8, un[n % UB]
                s, t = gather(U_, x["idx"][:, kk:kk + 1], [x["t_idx"]])
                t = dve([t, ts], lambda e: e.tensor_tensor_reduce(s.ap, s.ap, XN[:, half, :], 1.0, 0.0, ALU.mult,
                                                                  ALU.add, x["a"][:, kk:kk + 1]))
                s.free = [t]
            if j >= LAG:
                m, mk = (j - LAG) // 16, (j - LAG) % 16
                y, hv_ = un[m % UB], m // 8
                s2, t2 = gather(V_, y["idx"][:, mk:mk + 1], [])
                t_w = y["t_w", mk // LAG]
                if j >= 256 and mk % 4 == 2:
                    s2.free = [dve([t2, t_w, fin_t.get("h")], lambda e: e.scalar_tensor_tensor(
                        out=H[:, 1, :], in0=s2.ap, scalar=y["w"][:, mk:mk + 1], in1=H[:, 1, :], op0=ALU.mult,
                        op1=ALU.add))]
                    fin_t["h"] = s2.free[0]
                else:
                    d = diag[nd % 8]
                    td = act([t_w, dfree[nd % 8]], lambda e: e.activation(d, ident, ACT.Copy,
                                                                          scale=y["w"][:, mk:mk + 1]))
                    first, last = m % 8 == 0 and mk == 0, m % 8 == 7 and mk == 15
                    k.wait("pe", [td, t2] + ([bank[4 + 2 * hv_].free, bank[5 + 2 * hv_].free] if first else []))
                    for nb in range(2):
                        ins = mm(bank[4 + 2 * hv_ + nb].ap, d, s2.ap[:, nb * 512:nb * 512 + 512], first, last)
                    tm = k.mark(k.sem["pe"], ins, 1)
                    s2.free = [tm]
                    dfree[nd % 8] = tm
                    nd += 1
                    if mk == 15:
                        unit_done[m] = tm
            if kk > 5:
                next(nxt, None)
            if kk == 15:
                for _ in nxt:
                    pass
            if (n, kk) in later:
                finish(0, later[n, kk])
            if j < 256 and kk % LAG == LAG - 1:
                g = kk // LAG
                v = slice(LAG * g, LAG * g + LAG)
                t = act([t], lambda e: e.activation(x["g"][:, v], x["a"][:, v], ACT.Gelu))
                x["t_w", g] = dve([t, x["t_r"]], lambda e: e.scalar_tensor_tensor(
                    out=x["w"][:, v], in0=x["e"][:, v], scalar=x["r"], in1=x["g"][:, v], op0=ALU.mult,
                    op1=ALU.mult))
            yield

    r = stream()

    def items(n):
        for _ in range(n):
            next(r)

    query(0)
    c = choose(0)
    for _ in range(3):
        next(c)
    query(1)
    for _ in c:
        pass
    split_next()
    for i in range(2, 8):
        t_pq = query(i)
        items((2, 2, 2, 2, 3, 3)[i - 2])
    items(8)
    wctx.close()
    NG = 12
    GS = sb("GS", [P, NG, D])
    gs += [Slot(GS[:, i, :], k.semaphore(f"gather{len(spots) + i}")) for i in range(NG)]
    gs += [Slot(RAW[:, i // 2, D * (i % 2):D * (i % 2) + D], k.semaphore(f"gather{len(spots) + NG + i}")) for i in range(8)]
    for g in gs[len(spots):]:
        g.free = [t_pq]
    for _ in r:
        pass
    for stage in range(4):
        finish(1, stage)
    k.wait("sp", [fin_t[0], fin_t[1]])


_INS = ['x', 'mem', 'ffn1_pre_g', 'ffn1_w_gu', 'ffn1_w_down', 'ffn1_post_g', 'mix_pre_g', 'w_in', 'conv_w',
        'conv_b', 'dt_bias', 'a_log', 'd_skip', 'ssd_norm_g', 'attn_norm_g', 'w_out', 'mix_post_g', 'xa_pre_g',
        'mem_g', 'xa_wq', 'xa_wkv', 'xa_wo', 'xa_post_g', 'ffn2_pre_g', 'ffn2_w_gu', 'ffn2_w_down', 'ffn2_post_g',
        'norm_mix_g_2', 'w_in_2', 'attn_sinks_2', 'hgrn_lb_logits_2', 'hgrn_norm_g_2', 'w_attn_proj_2',
        'w_hgrn_proj_2', 'w_out_2', 'norm_ffn_g_2', 'w_peer_q_2', 'peer_keys_2', 'peer_u_2', 'peer_v_2',
        'norm_final_g_2']


def kernel(**inputs):
    import numpy as _np
    import concourse.bacc as _bacc
    from concourse import mybir as _mybir
    from concourse.bass_utils import run_bass_kernel_spmd as _run

    nc = _bacc.Bacc("TRN2", target_bir_lowering=False, num_devices=1)
    arrays, args = {}, {}
    for name in _INS:
        a = _np.ascontiguousarray(inputs[name])
        arrays[f"in_{name}_dram"] = a
        args[name] = nc.dram_tensor(f"in_{name}_dram", a.shape, _mybir.dt.from_np(a.dtype),
                                    kind="ExternalInput").ap()
    o = nc.dram_tensor("out_0_dram", (1, T, D), _mybir.dt.float32, kind="ExternalOutput").ap()
    build(nc, args, o)
    r = _run(nc, [arrays], core_ids=[0])
    return r.results[0]["out_0_dram"]
```
